# Optimizing a Trainium2 kernel written in Bass

```python
import jax, jax.numpy as jnp
from jax import lax
import numpy as np

D_MODEL = 1024
BATCH = 1
SEQ = 1024
DEPTH = 1

N_META = 16
EPS = 1e-6
ATT_HEADS = 8
Q_LORA = 384
KV_LORA = 256
QK_NOPE = 128
QK_ROPE = 64
V_HEAD = 128
ROPE_THETA = 10000.0
ATT_WIDTH = ATT_HEADS * V_HEAD
Q_BLOCK = 128
SSM_HEADS = 16
SSM_HEAD_DIM = 64
SSM_WIDTH = SSM_HEADS * SSM_HEAD_DIM
SSM_GROUPS = 2
SSM_HEADS_PER_GROUP = SSM_HEADS // SSM_GROUPS
SSM_STATE = 128
CONV_K = 4
CHUNK = 128
CONV_DIM = SSM_WIDTH + 2 * SSM_GROUPS * SSM_STATE
MIX_WIDTH = ATT_WIDTH + SSM_WIDTH
D_FF = 4 * D_MODEL
IN_SPLITS = (Q_LORA, KV_LORA, QK_ROPE, SSM_WIDTH, CONV_DIM, SSM_HEADS)
IN_WIDTH = sum(IN_SPLITS)
IN_OFFSETS = tuple(int(v) for v in np.cumsum(IN_SPLITS)[:-1])

kernel_name = "hymba_mla_ssd_sandwich_layer"

def rmsnorm(x, w):
    x32 = x.astype(jnp.float32)
    y = x32 * lax.rsqrt(jnp.mean(jnp.square(x32), axis=-1, keepdims=True) + EPS)
    return y.astype(x.dtype) * w

def gated_group_rmsnorm(y, z, w):
    g = (y * jax.nn.silu(z)).astype(jnp.float32)
    shp = g.shape
    g = g.reshape(*shp[:-1], SSM_GROUPS, shp[-1] // SSM_GROUPS)
    g = g * lax.rsqrt(jnp.mean(jnp.square(g), axis=-1, keepdims=True) + EPS)
    return g.reshape(shp).astype(z.dtype) * w

def rope_tables(length, dtype):
    inv_freq = ROPE_THETA ** (-jnp.arange(0, QK_ROPE, 2, dtype=jnp.float32) / QK_ROPE)
    ang = jnp.arange(length, dtype=jnp.float32)[:, None] * inv_freq[None, :]
    return jnp.cos(ang).astype(dtype), jnp.sin(ang).astype(dtype)

def apply_rope(x, cos, sin):
    x1, x2 = jnp.split(x, 2, axis=-1)
    return jnp.concatenate([x1 * cos - x2 * sin, x2 * cos + x1 * sin], axis=-1)

def mla_attention(q_nope, q_rope, k_nope, k_rope, v):
    bsz, length = q_nope.shape[:2]
    scale = (QK_NOPE + QK_ROPE) ** -0.5
    pos = jnp.arange(length)

    def attend(qn, qr, qpos, kn, kr, vv, kpos):
        s = jnp.einsum('bqhd,bkhd->bhqk', qn, kn) + jnp.einsum('bqhd,bkd->bhqk', qr, kr)
        s = s.astype(jnp.float32) * scale
        s = jnp.where(kpos[None, None, None, :] <= qpos[None, None, :, None], s, -jnp.inf)
        p = jax.nn.softmax(s, axis=-1).astype(vv.dtype)
        return jnp.einsum('bhqk,bkhd->bqhd', p, vv)

    out_meta = attend(q_nope[:, :N_META], q_rope[:, :N_META], pos[:N_META],
                      k_nope[:, :N_META], k_rope[:, :N_META], v[:, :N_META], pos[:N_META])
    n_blocks = (length - N_META) // Q_BLOCK

    def to_blocks(t):
        t = t[:, N_META:]
        return jnp.moveaxis(t.reshape(bsz, n_blocks, Q_BLOCK, *t.shape[2:]), 1, 0)

    def block_fn(args):
        qn, qr, qp = args
        return attend(qn, qr, qp, k_nope, k_rope, v, pos)

    out_real = lax.map(block_fn, (to_blocks(q_nope), to_blocks(q_rope), pos[N_META:].reshape(n_blocks, Q_BLOCK)))
    out_real = jnp.moveaxis(out_real, 0, 1).reshape(bsz, length - N_META, ATT_HEADS, V_HEAD)
    return jnp.concatenate([out_meta, out_real], axis=1)

def causal_depthwise_conv(u, w, bias):
    out = lax.conv_general_dilated(u, w[:, None, :], window_strides=(1,), padding=((CONV_K - 1, 0),),
                                   dimension_numbers=('NWC', 'WIO', 'NWC'), feature_group_count=u.shape[-1])
    return out + bias

def ssd_chunked(x, dt, a, b_mat, c_mat, state0, chunk):
    bsz, total = x.shape[:2]
    nc = total // chunk

    def chunks(t):
        return t.reshape(bsz, nc, chunk, *t.shape[2:])

    x, dt, b_mat, c_mat = chunks(x), chunks(dt), chunks(b_mat), chunks(c_mat)
    a_cum = jnp.cumsum(dt * a, axis=2)
    seg = a_cum[:, :, :, None] - a_cum[:, :, None, :]
    causal = jnp.tril(jnp.ones((chunk, chunk), dtype=bool))[:, :, None, None]
    decay = jnp.where(causal, jnp.exp(jnp.where(causal, seg, 0.0)), 0.0)
    cb = jnp.einsum('bclgn,bcsgn->bclsg', c_mat, b_mat)
    w_ls = cb[..., None] * decay * dt[:, :, None]
    y_diag = jnp.einsum('bclsgr,bcsgrp->bclgrp', w_ls, x)
    decay_to_end = jnp.exp(a_cum[:, :, -1:] - a_cum)
    states = jnp.einsum('bcsgn,bcsgr,bcsgrp->bcgrpn', b_mat, decay_to_end * dt, x)
    chunk_decay = jnp.exp(a_cum[:, :, -1])

    def step(h, inp):
        dec, st = inp
        return dec[..., None, None] * h + st, h

    final, prev = lax.scan(step, state0, (jnp.moveaxis(chunk_decay, 1, 0), jnp.moveaxis(states, 1, 0)))
    prev = jnp.moveaxis(prev, 0, 1)
    y_off = jnp.einsum('bclgn,bcgrpn,bclgr->bclgrp', c_mat, prev, jnp.exp(a_cum))
    y = (y_diag + y_off).reshape(bsz, total, *x.shape[3:])
    return y, final

def hybrid_mixer(h, w_in, q_a_norm, w_q_up, kv_a_norm, w_kv_up, conv_w, conv_b,
                 dt_bias, a_log, d_skip, ssm_norm, w_out, cos, sin):
    bsz, length, _ = h.shape
    proj = h @ w_in
    c_q, c_kv, k_rope, z, xbc, dt_raw = jnp.split(proj, IN_OFFSETS, axis=-1)

    q = (rmsnorm(c_q, q_a_norm) @ w_q_up).reshape(bsz, length, ATT_HEADS, QK_NOPE + QK_ROPE)
    q_nope, q_rope = q[..., :QK_NOPE], q[..., QK_NOPE:]
    kv = (rmsnorm(c_kv, kv_a_norm) @ w_kv_up).reshape(bsz, length, ATT_HEADS, QK_NOPE + V_HEAD)
    k_nope, v = kv[..., :QK_NOPE], kv[..., QK_NOPE:]
    q_rope = apply_rope(q_rope, cos[None, :, None, :], sin[None, :, None, :])
    k_rope = apply_rope(k_rope, cos[None], sin[None])
    att = mla_attention(q_nope, q_rope, k_nope, k_rope, v).reshape(bsz, length, ATT_WIDTH)

    xbc = jax.nn.silu(causal_depthwise_conv(xbc, conv_w, conv_b))
    xs, bm, cm = jnp.split(xbc, (SSM_WIDTH, SSM_WIDTH + SSM_GROUPS * SSM_STATE), axis=-1)
    xs32 = xs.astype(jnp.float32).reshape(bsz, length, SSM_GROUPS, SSM_HEADS_PER_GROUP, SSM_HEAD_DIM)
    bm = bm.astype(jnp.float32).reshape(bsz, length, SSM_GROUPS, SSM_STATE)
    cm = cm.astype(jnp.float32).reshape(bsz, length, SSM_GROUPS, SSM_STATE)
    dt = jax.nn.softplus(dt_raw.astype(jnp.float32) + dt_bias.astype(jnp.float32))
    dt = dt.reshape(bsz, length, SSM_GROUPS, SSM_HEADS_PER_GROUP)
    a = -jnp.exp(a_log.astype(jnp.float32)).reshape(SSM_GROUPS, SSM_HEADS_PER_GROUP)
    state0 = jnp.zeros((bsz, SSM_GROUPS, SSM_HEADS_PER_GROUP, SSM_HEAD_DIM, SSM_STATE), jnp.float32)
    y_meta, st = ssd_chunked(xs32[:, :N_META], dt[:, :N_META], a, bm[:, :N_META], cm[:, :N_META], state0, N_META)
    y_real, _ = ssd_chunked(xs32[:, N_META:], dt[:, N_META:], a, bm[:, N_META:], cm[:, N_META:], st, CHUNK)
    y = jnp.concatenate([y_meta, y_real], axis=1)
    y = y + d_skip.astype(jnp.float32).reshape(SSM_GROUPS, SSM_HEADS_PER_GROUP)[:, :, None] * xs32
    y = y.reshape(bsz, length, SSM_WIDTH).astype(h.dtype)
    ssm = gated_group_rmsnorm(y, z, ssm_norm)

    return jnp.concatenate([att, ssm], axis=-1) @ w_out

def setup_inputs(seed: int = 0) -> dict:
    key = jax.random.key(seed)
    ks = jax.random.split(key, 24)
    f32 = jnp.float32

    def nrm(k, shape, fan_in):
        return jax.random.normal(k, shape, f32) * (fan_in ** -0.5)

    def gain(k, shape):
        return 1.0 + 0.05 * jax.random.normal(k, shape, f32)

    dt0 = jnp.exp(jax.random.uniform(ks[10], (DEPTH, SSM_HEADS), f32) * (jnp.log(0.1) - jnp.log(0.001)) + jnp.log(0.001))
    return {
        "x": jax.random.normal(ks[0], (BATCH, SEQ, D_MODEL), f32),
        "meta_tokens": jax.random.normal(ks[1], (N_META, D_MODEL), f32),
        "norm_mix_pre": gain(ks[2], (DEPTH, D_MODEL)),
        "w_in": nrm(ks[3], (DEPTH, D_MODEL, IN_WIDTH), D_MODEL),
        "q_a_norm": gain(ks[4], (DEPTH, Q_LORA)),
        "w_q_up": nrm(ks[5], (DEPTH, Q_LORA, ATT_HEADS * (QK_NOPE + QK_ROPE)), Q_LORA),
        "kv_a_norm": gain(ks[6], (DEPTH, KV_LORA)),
        "w_kv_up": nrm(ks[7], (DEPTH, KV_LORA, ATT_HEADS * (QK_NOPE + V_HEAD)), KV_LORA),
        "conv_w": nrm(ks[8], (DEPTH, CONV_K, CONV_DIM), CONV_K),
        "conv_b": 0.01 * jax.random.normal(ks[9], (DEPTH, CONV_DIM), f32),
        "dt_bias": dt0 + jnp.log(-jnp.expm1(-dt0)),
        "a_log": jnp.log(jax.random.uniform(ks[11], (DEPTH, SSM_HEADS), f32, 1.0, 16.0)),
        "d_skip": gain(ks[12], (DEPTH, SSM_HEADS)),
        "ssm_norm": gain(ks[13], (DEPTH, SSM_WIDTH)),
        "w_out": nrm(ks[14], (DEPTH, MIX_WIDTH, D_MODEL), MIX_WIDTH),
        "norm_mix_post": gain(ks[15], (DEPTH, D_MODEL)),
        "norm_mlp_pre": gain(ks[16], (DEPTH, D_MODEL)),
        "w_mlp_up": nrm(ks[17], (DEPTH, D_MODEL, D_FF), D_MODEL),
        "w_mlp_down": nrm(ks[18], (DEPTH, D_FF, D_MODEL), D_FF),
        "norm_mlp_post": gain(ks[19], (DEPTH, D_MODEL)),
    }

def reference(x, meta_tokens, norm_mix_pre, w_in, q_a_norm, w_q_up, kv_a_norm, w_kv_up, conv_w, conv_b,
              dt_bias, a_log, d_skip, ssm_norm, w_out, norm_mix_post, norm_mlp_pre, w_mlp_up, w_mlp_down,
              norm_mlp_post):
    bsz = x.shape[0]
    h = jnp.concatenate([jnp.broadcast_to(meta_tokens[None].astype(x.dtype), (bsz, N_META, D_MODEL)), x], axis=1)
    cos, sin = rope_tables(h.shape[1], h.dtype)
    for layer in range(DEPTH):
        mix = hybrid_mixer(rmsnorm(h, norm_mix_pre[layer]), w_in[layer], q_a_norm[layer], w_q_up[layer],
                           kv_a_norm[layer], w_kv_up[layer], conv_w[layer], conv_b[layer], dt_bias[layer],
                           a_log[layer], d_skip[layer], ssm_norm[layer], w_out[layer], cos, sin)
        h = h + rmsnorm(mix, norm_mix_post[layer])
        f = jnp.square(jax.nn.relu(rmsnorm(h, norm_mlp_pre[layer]) @ w_mlp_up[layer])) @ w_mlp_down[layer]
        h = h + rmsnorm(f, norm_mlp_post[layer])
    return h[:, N_META:]


_drawn_inputs = setup_inputs


def setup_inputs(seed=0):
    import zlib

    import numpy as np

    out = dict(_drawn_inputs(seed))
    spreads = {}
    factors = {'q_a_norm': 8.0, 'kv_a_norm': 8.0, 'conv_b': 39.329, 'd_skip': 8.0, 'ssm_norm': 8.0}
    for name, (base, spread) in spreads.items():
        noise = np.random.default_rng([zlib.crc32(name.encode()), seed]).standard_normal(out[name].shape)
        drawn = base * np.exp(spread * noise) if base else spread * noise
        out[name] = __import__('jax').numpy.asarray(drawn.astype(out[name].dtype))
    for name, factor in factors.items():
        out[name] = (out[name] * factor).astype(out[name].dtype)
    return out
```

```python
import numpy as np

import concourse.bass as bass
from concourse import mybir

F32 = mybir.dt.float32
F32R = mybir.dt.float32r
BF16 = mybir.dt.bfloat16
ALU = mybir.AluOpType
ACT = mybir.ActivationFunctionType
AX = mybir.AxisListType

P = 128
D = 1024
SEQ = 1024
META = 16
POS = SEQ + META
KD = D // P
NT = SEQ // P
QL, KVL, ROPE, NOPE, VH = 384, 256, 64, 128, 128
HEADS = 8
SSMW, GROUPS, STATE, SH, SHD = 1024, 2, 128, 16, 64
CONVW = SSMW + 2 * GROUPS * STATE
DFF = 4096
OFF_KV, OFF_KR, OFF_Z, OFF_X, OFF_DT = QL, QL + KVL, QL + KVL + ROPE, QL + KVL + ROPE + SSMW, QL + KVL + ROPE + SSMW + CONVW
SCALE = float((NOPE + ROPE) ** -0.5)
EPS = 1e-6
NEG = -1.0e30
TC = [(0, 348), (348, 346), (694, 346)]
RING = 16
STAGES = 4


class Sems:

    def __init__(self, nc):
        self.nc, self.of = nc, {}

    def __call__(self, name):
        if name not in self.of:
            self.of[name] = self.nc.alloc_semaphore(name)
        return self.of[name]

    def renew(self):
        self.nc.clear_and_free_semaphores(list(self.of.values()))
        self.of = {}
        self.nc.all_engine_barrier()


class Map:

    def __init__(self, nc):
        self.nc, self.base = nc, (nc.sbuf_base + 31) // 32 * 32

    def at(self, name, shape, dt, offset):
        size = (int(np.prod(shape[1:])) * mybir.dt.size(dt) + 31) // 32 * 32
        assert self.base + offset + size <= self.nc.sbuf_usable_end, (name, offset, size)
        return self.nc.alloc_sbuf_tensor_at(name, list(shape), dt, offset=self.base + offset), offset + size


PARAM = {}
_at = 0
for _n, _w in (("pre", KD), ("mlp", KD), ("qa", QL // P), ("kva", KVL // P), ("convw", 4 * CONVW // P), ("convb", CONVW // P)):
    PARAM[_n] = _at
    _at += _w
NPARAM = _at

O_RING = 6144
O_STAGE = O_RING + RING * 512 * 8
O_R = O_STAGE + STAGES * 512 * 4
O_DT = 212256
O_TABLES = O_DT - 7744


class K:
    pass


def setup(nc, io):
    k = K()
    k.nc, k.io, k.sem, m = nc, io, Sems(nc), Map(nc)
    k.map = m
    o = 0
    k.ident, o = m.at("ident", [P, P], F32, o)
    k.ident_b, o = m.at("ident_b", [P, P], BF16, o)
    k.mask_b, o = m.at("mask_b", [P, P], BF16, o)
    k.tri, o = m.at("tri", [P, P], F32R, o)
    k.ones, o = m.at("ones", [P, P], F32R, o)
    k.par, o = m.at("par", [P, NPARAM], F32, o)
    k.st = []
    for n in range(6):
        t, o = m.at(f"stat{n}", [P, 24], F32, o)
        k.st.append(t)
    k.zero, o = m.at("zero", [P, 8], F32, o)
    k.spare, o = m.at("spare", [P, 512], F32, o)
    assert o <= O_RING
    k.whi, o = m.at("whi", [P, RING, 512], F32R, O_RING)
    k.wlo, o = m.at("wlo", [P, RING, 512], F32R, o)
    k.stage, o = m.at("stage", [P, STAGES, 512], F32, O_STAGE)
    k.ps = nc.alloc_psum_tensor("ps", [P, 8, 512], F32)
    dr = lambda n, s, dt: nc.dram_tensor(n, s, dt, kind="Internal").ap()
    k.d_x = dr("d_x", (SEQ, SSMW), F32)
    k.d_xm = dr("d_xm", (META, SSMW), F32)
    k.d_z = dr("d_z", (SEQ, SSMW), F32)
    pair = lambda n, s: [dr(n + "hi", s, F32), dr(n + "lo", s, F32)]
    k.d_bt = pair("d_bt", (GROUPS * STATE, SEQ))
    k.d_ct = pair("d_ct", (GROUPS * STATE, SEQ))
    k.d_b = pair("d_b", (SEQ, GROUPS * STATE))
    k.d_bm = pair("d_bm", (META, GROUPS * STATE))
    k.d_qr = pair("d_qr", (HEADS * ROPE, SEQ))
    k.d_att = pair("d_att", (HEADS * VH, SEQ))
    k.d_ssm = pair("d_ssm", (SSMW, SEQ))
    k.d_mix = dr("d_mix", (SEQ, D), F32)
    k.d_h = dr("d_h", (SEQ, D), F32)
    k.blocks = []
    k.fam = "w"
    return k


def col(k, name, n):
    return k.par[:, PARAM[name] + n:PARAM[name] + n + 1]



def load_block(sp, k, n, src, base=0, turn=0):
    if n >= STAGES:
        sp.wait_ge(k.sem(k.fam + "_cut"), n - STAGES + 1 + turn)
    width = src.shape[-1]
    sp.dma_start(k.stage[:, n % STAGES, 0:width], src).then_inc(k.sem(f"{k.fam}_landed{n % STAGES}"), 16)


def cut_block(pool, k, n, width, turn=0, by_stages=0):
    pool.wait_ge(k.sem(f"{k.fam}_landed{n % STAGES}"), 16 * (n // STAGES + 1) + by_stages)
    src = k.stage[:, n % STAGES, 0:width]
    hi, lo = k.whi[:, n % RING, 0:width], k.wlo[:, n % RING, 0:width]
    pool.tensor_tensor(hi, src, k.zero[:, 0:1].broadcast_to([P, width]), ALU.add).then_inc(k.sem(k.fam + "_hi"), 1)
    pool.wait_ge(k.sem(k.fam + "_hi"), n + 1 + turn)
    pool.tensor_tensor(lo, src, hi.bitcast(F32), ALU.subtract).then_inc(k.sem(k.fam + "_cut"), 1)


def mm3(pe, out, l, r, first, last):
    pe.matmul(out, l[0], r[0], start=first, stop=False)
    pe.matmul(out, l[0], r[1], start=False, stop=False)
    return pe.matmul(out, l[1], r[0], start=False, stop=last)



def phase_norm(k):
    nc, sem, m, ps, io = k.nc, k.sem, k.map, k.ps, k.io
    k.hT = []
    o = O_R
    for s in ("hi", "lo"):
        t, o = m.at("hT" + s, [P, KD, POS], F32R, o)
        k.hT.append(t)
    k.o_work = o
    xt, o = m.at("xt", [P, NT + 1, D], F32, o)
    cst, o = m.at("cst", [P, 2, P], F32, o)
    mtmp, o = m.at("mtmp", [P, KD, META], F32, o)
    ss, v, s_, r, t1 = k.st[0], k.st[1], k.st[2], k.st[3], k.st[4]
    hT = k.hT
    win = io["w_in"][0]
    wqu = io["w_q_up"][0]
    cols = [(OFF_X, 512), (OFF_X + 512, 512), (OFF_X + 1024, 512), (OFF_Z, 512), (OFF_Z + 512, 512), (0, QL), (OFF_KV, KVL + ROPE)]
    k.blocks = [win[P * kk:P * kk + P, c:c + w] for c, w in cols for kk in range(KD)]
    qr_view = wqu.rearrange("k (h c) -> k h c", h=HEADS)[:, :, NOPE:NOPE + ROPE]
    k.qr_blocks = [qr_view[P * kk:P * kk + P] for kk in range(QL // P)]

    with nc.Block() as block:
        @block.sync
        def _(sp):
            sp.dma_start(k.ident[:, :], io["c_ident"]).then_inc(sem("c_in"), 16)
            sp.dma_start(cst[:, 0, :], io["c_tri"]).then_inc(sem("c_in"), 16)
            sp.dma_start(cst[:, 1, :], io["c_mask"]).then_inc(sem("c_in"), 16)
            sp.dma_start(k.par[:, :], io["c_par"]).then_inc(sem("c_in"), 16)
            for t in range(NT):
                sp.dma_start(xt[:, t, :], io["x"][0, P * t:P * t + P, :]).then_inc(sem(f"x_in{t}"), 16)
            sp.dma_start(xt[0:META, NT, :], io["meta_tokens"]).then_inc(sem(f"x_in{NT}"), 16)
            for n in range(RING):
                load_block(sp, k, n, k.blocks[n])

        @block.gpsimd
        def _(pool):
            pool.memset(k.zero[:, :], 0.0).then_inc(sem("zeroed"), 1)
            pool.wait_ge(sem("zeroed"), 1)
            for n in range(RING):
                cut_block(pool, k, n, k.blocks[n].shape[-1])

        @block.scalar
        def _(act):
            for t in range(NT + 1):
                rows = P if t < NT else META
                act.wait_ge(sem(f"x_in{t}"), 16)
                if t == 0:
                    act.wait_ge(sem("ss_set"), 1)
                if t >= 1:
                    act.wait_ge(sem("sq"), t)
                act.activation(ps[0:rows, 6:8, :].rearrange("p a b -> p (a b)"), xt[0:rows, t, :], ACT.Square,
                               accum_out=ss[0:rows, t:t + 1]).then_inc(sem("sq"), 1)
            act.wait_ge(sem("v"), 1)
            act.activation(s_[:, 0:9], v[:, 0:9], ACT.Sqrt).then_inc(sem("sqrt"), 1)
            act.wait_ge(sem("c_in"), 64)
            for n in range(2 * KD):
                kk, half = n // 2, n % 2
                act.wait_ge(sem("turned"), n + 1)
                c0 = META + 512 * half
                act.activation(hT[0][:, kk, c0:c0 + 512], ps[:, n % 4, :], ACT.Copy, scale=col(k, "pre", kk)).then_inc(sem("t_hi"), 1)
            act.wait_ge(sem("mt"), 1)
            act.activation(hT[0][:, :, 0:META], mtmp[:, :, :], ACT.Copy).then_inc(sem("t_hi"), 1)

        @block.vector
        def _(dve):
            dve.memset(ss[:, :], 1.0).then_inc(sem("ss_set"), 1)
            dve.wait_ge(sem("c_in"), 64)
            dve.tensor_copy(k.ident_b[:, :], k.ident[:, :]).then_inc(sem("consts"), 1)
            dve.tensor_copy(k.mask_b[:, :], cst[:, 1, :]).then_inc(sem("consts"), 1)
            dve.tensor_copy(k.tri[:, :], cst[:, 0, :]).then_inc(sem("consts"), 1)
            dve.tensor_scalar(k.ones[:, :], cst[:, 0, :], 0.0, 1.0, ALU.mult, ALU.add).then_inc(sem("consts"), 1)
            dve.wait_ge(sem("sq"), NT + 1)
            rsqrt_before(dve, k, v[:, 0:9], ss[:, 0:9], 1.0 / D, "v", 1)
            rsqrt_after(dve, k, r[:, 0:9], v[:, 0:9], s_[:, 0:9], t1[:, 0:9], "sqrt", 1, "rs1")
            for t in range(NT + 1):
                rows = P if t < NT else META
                dve.tensor_scalar(xt[0:rows, t, :], xt[0:rows, t, :], r[0:rows, t:t + 1], None, ALU.mult).then_inc(sem("xn"), 1)
            for n in range(2 * KD):
                kk, half = n // 2, n % 2
                dve.wait_ge(sem("t_hi"), n + 1)
                c0 = META + 512 * half
                dve.scalar_tensor_tensor(hT[1][:, kk, c0:c0 + 512], ps[:, n % 4, :], col(k, "pre", kk), hT[0][:, kk, c0:c0 + 512].bitcast(F32),
                                         ALU.mult, ALU.subtract).then_inc(sem("t_lo"), 1)
            dve.wait_ge(sem("turned"), 2 * KD + 1)
            w = k.par[:, PARAM["pre"]:PARAM["pre"] + KD].unsqueeze(2).broadcast_to([P, KD, META])
            dve.tensor_tensor(mtmp[:, :, :], ps[:, 0, 0:P].rearrange("p (a b) -> p a b", a=KD), w, ALU.mult).then_inc(sem("mt"), 1)
            dve.wait_ge(sem("t_hi"), 2 * KD + 1)
            dve.wait_ge(sem("mt"), 1)
            dve.tensor_tensor(hT[1][:, :, 0:META], mtmp[:, :, :], hT[0][:, :, 0:META].bitcast(F32), ALU.subtract).then_inc(sem("t_lo"), 1)

        @block.tensor
        def _(pe):
            pe.wait_ge(sem("c_in"), 64)
            for n in range(2 * KD):
                kk, half = n // 2, n % 2
                pe.wait_ge(sem("xn"), 4 * half + 4)
                if n >= 4:
                    pe.wait_ge(sem("t_lo"), n - 3)
                for i in range(4):
                    mm = pe.transpose(ps[:, n % 4, P * i:P * i + P], xt[:, 4 * half + i, P * kk:P * kk + P], k.ident[:, :])
                mm.then_inc(sem("turned"), 1)
            pe.wait_ge(sem("xn"), NT + 1)
            pe.wait_ge(sem("t_lo"), 2 * KD - 3)
            for kk in range(KD):
                mm = pe.transpose(ps[:, 0, META * kk:META * kk + META], xt[0:META, NT, P * kk:P * kk + P], k.ident[0:META, 0:META])
            mm.then_inc(sem("turned"), 1)


def rsqrt_before(dve, k, v, ss, scale, name, count):
    dve.tensor_scalar(v, ss, scale, EPS, ALU.mult, ALU.add).then_inc(k.sem(name), 1)


def rsqrt_after(dve, k, r, v, s, t, name, count, own, base=0):
    c = k.sem(own)
    dve.wait_ge(k.sem(name), count)
    dve.reciprocal(r, s).then_inc(c, 1)
    dve.wait_ge(c, base + 1)
    dve.tensor_tensor(t, r, r, ALU.mult).then_inc(c, 1)
    dve.wait_ge(c, base + 2)
    dve.tensor_tensor(t, t, v, ALU.mult).then_inc(c, 1)
    dve.wait_ge(c, base + 3)
    dve.tensor_scalar(t, t, -0.5, 1.5, ALU.mult, ALU.add).then_inc(c, 1)
    dve.wait_ge(c, base + 4)
    dve.tensor_tensor(r, r, t, ALU.mult).then_inc(c, 1)
    dve.wait_ge(c, base + 5)



NX = CONVW // P
NXT = NX - GROUPS


def phase_project(k):
    nc, sem, m, ps, io, hT = k.nc, k.sem, k.map, k.ps, k.io, k.hT
    o = k.o_work
    pre, o = m.at("pre", [P, 2, POS + 4], F32, o)
    acc, o = m.at("conv_acc", [P, 2, POS], F32, o)
    xc, o = m.at("xc", [P, 2, POS], F32, o)
    o1 = o
    xt, o = m.at("x_tok", [P, 2, NT + 1, P], F32, o)
    fb, o = [], o
    for s in ("hi", "lo"):
        t, o = m.at("bc" + s, [P, SEQ], F32R, o)
        fb.append(t)
    zs, o = m.at("zs", [P, 4, 512], F32, o)
    o_top = o
    bt = []
    for s in ("hi", "lo"):
        t, o = m.at("btok" + s, [P, NT + 1, P], F32R, o)
        bt.append(t)
    oc = k.o_work
    cqs, oc = m.at("cqs", [P, NT, QL], F32, oc)
    cks, oc = m.at("cks", [P, NT + 1, KVL + ROPE], F32, oc)
    assert oc <= o1
    oc = o1
    kro, oc = m.at("kro", [P, NT + 1, P], F32, oc)
    ta, oc = m.at("rot_a", [P, 288], F32, oc)
    tb, oc = m.at("rot_b", [P, 288], F32, oc)
    junk, oc = m.at("junk", [P, QL], F32, oc)
    assert oc <= o_top
    rope, o = m.at("rope", [P, NT + 1, ROPE], F32, o)
    wdt, o = m.at("wdt", [P, KD, SH], F32, o)
    wd = []
    for s in ("hi", "lo"):
        t, o = m.at("wdt" + s, [P, KD, SH], F32R, o)
        wd.append(t)
    k.dt_at = m.base + O_DT
    assert o <= O_DT
    o = O_DT
    k.dt, o = m.at("dt", [P, NT + 1, SH], F32, o)
    oh = O_R
    k.cqT, k.ckT, k.krT, k.qrT = [], [], [], []
    for lst, name, shape in ((k.cqT, "cqT", [P, QL // P, SEQ]), (k.ckT, "ckT", [P, KVL // P, POS]), (k.krT, "krT", [P, POS])):
        for s in ("hi", "lo"):
            t, oh = m.at(name + s, shape, F32R, oh)
            lst.append(t)
    k.o_lat = oh
    mt, oh = m.at("mtmp2", [P, 3, META], F32, oh)
    qro, oh = m.at("qro", [P, HEADS, ROPE], F32, oh)
    for s in ("hi", "lo"):
        t, oh = m.at("qrT" + s, [P, 4, P], F32R, oh)
        k.qrT.append(t)
    assert oh <= k.o_work
    ss, v, s_, r, t1 = k.st[0], k.st[1], k.st[2], k.st[3], k.st[4]
    nb = len(k.blocks)
    W = (k.whi, k.wlo)
    PASSES = ((0, 0), (0, 1), (1, 0))
    NW = NT + NT + 1
    KQ, KK = QL // P, KVL // P

    def chunk_used(eng, c):
        if c < 3:
            eng.wait_ge(sem("x_done"), 4 * c + 4)
        elif c < 5:
            eng.wait_ge(sem("z_done"), NT * (c - 2))
        elif c == 5:
            eng.wait_ge(sem("cq_done"), NT)
        elif c == 6:
            eng.wait_ge(sem("ck_done"), NT + 1)

    with nc.Block() as block:
        @block.sync
        def _(sp):
            sp.dma_start(rope[:, :, :], io["c_rope"]).then_inc(sem("rope_in"), 16)
            sp.dma_start(wdt[:, :, :], io["w_in"][0, :, OFF_DT:OFF_DT + SH].rearrange("(k p) n -> p k n", p=P)).then_inc(sem("wdt_in"), 16)
            loaded = [RING]

            def loads(until):
                for n in range(loaded[0], until):
                    if n < nb:
                        load_block(sp, k, n, k.blocks[n])
                    else:
                        sp.wait_ge(sem("w_cut"), n - STAGES + 1)
                        sp.dma_start(k.stage[:, n % STAGES, :].rearrange("p (h c) -> p h c", h=HEADS),
                                     k.qr_blocks[n - nb]).then_inc(sem(f"w_landed{n % STAGES}"), 16)
                loaded[0] = until

            loads(RING + STAGES)
            for f in range(NX):
                q = f - 2
                if 0 <= q < NXT:
                    sp.wait_ge(sem("xt1_out"), q + 1)
                    sp.wait_ge(sem("xt2_out"), q + 1)
                if 0 <= q < KD:
                    sent = sem(f"xt_sent{q % 2}")
                    sp.dma_start(k.d_x[:, P * q:P * q + P].rearrange("(t p) n -> p t n", p=P), xt[:, q % 2, 0:NT, :]).then_inc(sent, 16)
                    sp.dma_start(k.d_xm[:, P * q:P * q + P], xt[0:META, q % 2, NT, :]).then_inc(sent, 16)
                elif 0 <= q < NXT:
                    g = q - KD
                    for i in range(2):
                        sp.dma_start(k.d_b[i][:, P * g:P * g + P].rearrange("(t p) n -> p t n", p=P),
                                     bt[i][:, 0:NT, :].bitcast(F32)).then_inc(sem("bt_sent"), 16)
                        sp.dma_start(k.d_bm[i][:, P * g:P * g + P], bt[i][0:META, NT, :].bitcast(F32)).then_inc(sem("bt_sent"), 16)
                if f >= KD:
                    sp.wait_ge(sem("bc_lo"), f - KD + 1)
                    d = k.d_bt if f < KD + GROUPS else k.d_ct
                    g = (f - KD) % GROUPS
                    for i in range(2):
                        sp.dma_start(d[i][P * g:P * g + P, :], fb[i][:, :].bitcast(F32)).then_inc(sem("bc_sent"), 16)
                if f in (4, 8, NX - 1):
                    loads(loaded[0] + 8)
            for g in range(2 * NT):
                c, t = g // NT, g % NT
                sp.wait_ge(sem("zs_done"), g + 1)
                sp.dma_start(k.d_z[P * t:P * t + P, 512 * c:512 * c + 512], zs[:, g % 4, :]).then_inc(sem(f"z_sent{g % 4}"), 16)
                if g == NT:
                    loads(loaded[0] + 8)
            loads(nb + KQ)
            for t in range(NT):
                sp.wait_ge(sem("qrT_lo"), t + 1)
                for i in range(2):
                    sp.dma_start(k.d_qr[i][:, P * t:P * t + P].rearrange("(a p) n -> p a n", p=P),
                                 k.qrT[i][:, :, :].bitcast(F32)).then_inc(sem("qr_sent"), 16)
            for q in range(4):
                sp.wait_ge(sem(f"z_sent{q}"), 16 * 4)
            sp.wait_ge(sem("bt_sent"), 64 * GROUPS)
            sp.wait_ge(sem("bc_sent"), 32 * 2 * GROUPS)
            sp.wait_ge(sem("qr_sent"), 32 * NT)

        @block.gpsimd
        def _(pool):
            for n in range(RING, nb + KQ):
                if n % 8 == 0:
                    chunk_used(pool, n // 8 - 2)
                cut_block(pool, k, n, k.blocks[n].shape[-1] if n < nb else 512)

        @block.tensor
        def _(pe):
            def turn_x(f, parts):
                pe.wait_ge(sem("xc_done"), f + 1)
                for part in parts:
                    bank = (6, 7, 6)[part]
                    if part == 0 and f:
                        pe.wait_ge(sem("xt2_out"), f)
                    if part == 1 and f:
                        pe.wait_ge(sem("xt1_out"), f)
                    if part == 2:
                        pe.wait_ge(sem("xt0_out"), f + 1)
                        mm = pe.transpose(ps[:, 6, 0:P], xc[:, f % 2, 0:P], k.ident[:, :])
                    else:
                        for i in range(4):
                            c0 = META + P * (4 * part + i)
                            mm = pe.transpose(ps[:, bank, P * i:P * i + P], xc[:, f % 2, c0:c0 + P], k.ident[:, :])
                    mm.then_inc(sem("x_turned"), 1)

            for f in range(NX):
                c, j = f // 4, f % 4
                base = 3 * (f % 2)
                if f >= 2:
                    pe.wait_ge(sem("pre_out"), 3 * (f - 1))
                for kk in range(KD):
                    if kk == 2 and 2 <= f <= NXT + 1:
                        turn_x(f - 2, (2,))
                    if j == 0:
                        pe.wait_ge(sem("w_cut"), 8 * c + kk + 1)
                    for a, b in PASSES:
                        for q, (c0, w) in enumerate(TC):
                            mm = pe.matmul(ps[:, base + q, 0:w], W[a][:, (8 * c + kk) % RING, P * j:P * j + P], hT[b][:, kk, c0:c0 + w],
                                           start=(kk == 0 and (a, b) == (0, 0)), stop=(kk == KD - 1 and a == 1))
                mm.then_inc(sem("x_done"), 1)
                if 1 <= f <= NXT:
                    turn_x(f - 1, (0, 1))
            for c in (3, 4):
                for t in range(NT):
                    g = NT * (c - 3) + t
                    if g < 4:
                        pe.wait_ge(sem("pre_out"), 3 * NX)
                    else:
                        pe.wait_ge(sem("zs_done"), g - 3)
                    for kk in range(KD):
                        if t == 0:
                            pe.wait_ge(sem("w_cut"), 8 * c + kk + 1)
                        for a, b in PASSES:
                            mm = pe.matmul(ps[:, g % 4, :], hT[a][:, kk, META + P * t:META + P * t + P], W[b][:, (8 * c + kk) % RING, :],
                                           start=(kk == 0 and (a, b) == (0, 0)), stop=(kk == KD - 1 and a == 1))
                    mm.then_inc(sem("z_done"), 1)
            for t in range(NT):
                if t < 4:
                    pe.wait_ge(sem("zs_done"), 2 * NT - 3 + t)
                else:
                    pe.wait_ge(sem("cq_out"), t - 3)
                for kk in range(KD):
                    if t == 0:
                        pe.wait_ge(sem("w_cut"), 40 + kk + 1)
                    for a, b in PASSES:
                        mm = pe.matmul(ps[:, t % 4, 0:QL], hT[a][:, kk, META + P * t:META + P * t + P], W[b][:, (40 + kk) % RING, 0:QL],
                                       start=(kk == 0 and (a, b) == (0, 0)), stop=(kk == KD - 1 and a == 1))
                mm.then_inc(sem("cq_done"), 1)
            pe.wait_ge(sem("wdt_cut"), 2)
            for t in range(NT + 1):
                if t < 4:
                    pe.wait_ge(sem("cq_out"), NT - 3 + t)
                else:
                    pe.wait_ge(sem("ck_out"), t - 3)
                c0 = META + P * t if t < NT else 0
                for part, w in ((0, KVL + ROPE), (1, SH)):
                    for kk in range(KD):
                        if t == 0:
                            pe.wait_ge(sem("w_cut"), 48 + kk + 1)
                        for a, b in PASSES:
                            rhs = W[b][:, (48 + kk) % RING, 0:w] if part == 0 else wd[b][:, kk, :]
                            mm = pe.matmul(ps[:, t % 4, (KVL + ROPE) * part:(KVL + ROPE) * part + w], hT[a][:, kk, c0:c0 + P], rhs,
                                           start=(kk == 0 and (a, b) == (0, 0)), stop=(kk == KD - 1 and a == 1))
                mm.then_inc(sem("ck_done"), 1)
            pe.wait_ge(sem("xt2_out"), NXT)
            for n in range(13):
                bank = 4 + n % 4
                if n >= 4:
                    pe.wait_ge(sem("lat_lo"), n - 3)
                if n < 6:
                    pe.wait_ge(sem("cq_scaled"), NT)
                elif n < 10:
                    pe.wait_ge(sem("ck_scaled"), NT + 1)
                else:
                    pe.wait_ge(sem("kro_done"), 2)
                half = n % 2
                if n < 12:
                    for i in range(4):
                        t = 4 * half + i
                        if n < 6:
                            src = cqs[:, t, P * (n // 2):P * (n // 2) + P]
                        elif n < 10:
                            kk = (n - 6) // 2
                            src = cks[:, t, P * kk:P * kk + P]
                        else:
                            src = kro[:, t, :]
                        mm = pe.transpose(ps[:, bank, P * i:P * i + P], src, k.ident[:, :])
                else:
                    for i in range(3):
                        src = cks[0:META, NT, P * i:P * i + P] if i < 2 else kro[0:META, NT, :]
                        mm = pe.transpose(ps[:, bank, META * i:META * i + META], src, k.ident[0:META, 0:META])
                mm.then_inc(sem("lat_turned"), 1)
            def turn_qr(t):
                pe.wait_ge(sem("qro_done"), 2 * t + 2)
                if t < 2:
                    pe.wait_ge(sem("lat_lo"), 13)
                else:
                    pe.wait_ge(sem("qrT_lo"), t - 1)
                for i in range(4):
                    mm = pe.transpose(ps[:, 4 + t % 2, P * i:P * i + P], qro[:, 2 * i:2 * i + 2, :].rearrange("p a b -> p (a b)"), k.ident[:, :])
                mm.then_inc(sem("qr_turned"), 1)

            pe.wait_ge(sem("lat_lo"), 13)
            for t in range(NT):
                if t < 4:
                    pe.wait_ge(sem("ck_out"), NT + 1)
                else:
                    pe.wait_ge(sem("qro_done"), 2 * (t - 3))
                for kk in range(KQ):
                    if t == 0:
                        pe.wait_ge(sem("w_cut"), nb + kk + 1)
                    for a, b in PASSES:
                        mm = pe.matmul(ps[:, t % 4, :], k.cqT[a][:, kk, P * t:P * t + P], W[b][:, (nb + kk) % RING, :],
                                       start=(kk == 0 and (a, b) == (0, 0)), stop=(kk == KQ - 1 and a == 1))
                mm.then_inc(sem("qr_done"), 1)
                if t:
                    turn_qr(t - 1)
            turn_qr(NT - 1)

        @block.scalar
        def _(act):
            def out_x(f, part):
                act.wait_ge(sem("x_turned"), 3 * f + part + 1)
                src = ps[:, 6, :].rearrange("p (a b) -> p a b", b=P) if part == 0 else ps[0:META, 6, 0:P]
                if f < KD:
                    if part == 0 and f >= 2:
                        act.wait_ge(sem(f"xt_sent{f % 2}"), 32 * (f // 2))
                    dst = xt[:, f % 2, 0:4, :] if part == 0 else xt[0:META, f % 2, NT, :]
                    act.activation(dst, src, ACT.Copy).then_inc(sem(f"xt{part}_out"), 1)
                else:
                    if part == 0 and f > KD:
                        act.wait_ge(sem("bt_sent"), 64 * (f - KD))
                    dst = bt[0][:, 0:4, :] if part == 0 else bt[0][0:META, NT, :]
                    act.activation(dst, src, ACT.Copy).then_inc(sem("bt_hi"), 1)
                    if part == 0:
                        act.wait_ge(sem("x_turned"), 3 * f + 2)
                        act.activation(bt[0][:, 4:8, :], ps[:, 7, :].rearrange("p (a b) -> p a b", b=P), ACT.Copy).then_inc(sem("bt_hi"), 1)

            for f in range(NX):
                act.wait_ge(sem("x_done"), f + 1)
                if f >= 2:
                    act.wait_ge(sem("conv_done"), f - 1)
                for q, (c0, w) in enumerate(TC):
                    act.activation(pre[:, f % 2, 4 + c0:4 + c0 + w], ps[:, 3 * (f % 2) + q, 0:w], ACT.Copy).then_inc(sem("pre_out"), 1)
                if 2 <= f <= NXT + 1:
                    out_x(f - 2, 2)
                if 1 <= f <= NXT:
                    out_x(f - 1, 0)
                act.wait_ge(sem("conv_done"), f + 1)
                if f >= 2:
                    if f - 2 < NXT:
                        act.wait_ge(sem("x_turned"), 3 * (f - 1))
                    if f - 2 >= KD:
                        act.wait_ge(sem("bc_lo"), f - 1 - KD)
                act.activation(xc[:, f % 2, :], acc[:, f % 2, :], ACT.Silu, bias=col(k, "convb", f)).then_inc(sem("xc_done"), 1)
                if f >= KD:
                    act.wait_ge(sem("xc_done"), f + 1)
                    if f > KD:
                        act.wait_ge(sem("bc_sent"), 32 * (f - KD))
                    act.activation(fb[0][:, :], xc[:, f % 2, META:POS], ACT.Copy).then_inc(sem("bc_hi"), 1)
            for g in range(2 * NT):
                act.wait_ge(sem("z_done"), g + 1)
                if g >= 4:
                    act.wait_ge(sem(f"z_sent{g % 4}"), 16 * (g // 4))
                act.activation(zs[:, g % 4, :], ps[:, g % 4, :], ACT.Silu).then_inc(sem("zs_done"), 1)
            act.wait_ge(sem("stat_set"), 1)
            for t in range(NW):
                if t < NT:
                    act.wait_ge(sem("cq_out"), t + 1)
                    rows, src = P, cqs[:, t, :]
                else:
                    act.wait_ge(sem("ck_out"), t - NT + 1)
                    rows = P if t < NW - 1 else META
                    src = cks[0:rows, t - NT, 0:KVL]
                if t:
                    act.wait_ge(sem("lat_sq"), t)
                act.activation(junk[0:rows, 0:src.shape[-1]], src, ACT.Square, accum_out=ss[0:rows, t:t + 1]).then_inc(sem("lat_sq"), 1)
            act.wait_ge(sem("lat_v"), 2)
            act.activation(s_[:, 0:NW], v[:, 0:NW], ACT.Sqrt).then_inc(sem("lat_sqrt"), 1)
            for n in range(13):
                act.wait_ge(sem("lat_turned"), n + 1)
                c0 = 512 * (n % 2)
                src = ps[:, 4 + n % 4, :]
                if n < 6:
                    act.activation(k.cqT[0][:, n // 2, c0:c0 + 512], src, ACT.Copy, scale=col(k, "qa", n // 2)).then_inc(sem("lat_hi"), 1)
                elif n < 10:
                    kk = (n - 6) // 2
                    act.activation(k.ckT[0][:, kk, META + c0:META + c0 + 512], src, ACT.Copy, scale=col(k, "kva", kk)).then_inc(sem("lat_hi"), 1)
                elif n < 12:
                    act.activation(k.krT[0][:, META + c0:META + c0 + 512], src, ACT.Copy).then_inc(sem("lat_hi"), 1)
                else:
                    act.wait_ge(sem("lat_mt"), 2)
                    act.activation(k.ckT[0][:, :, 0:META], mt[:, 0:2, :], ACT.Copy).then_inc(sem("lat_hi"), 1)
                    act.activation(k.krT[0][:, 0:META], mt[:, 2, :], ACT.Copy).then_inc(sem("lat_hi"), 1)
            for t in range(NT):
                act.wait_ge(sem("qr_turned"), t + 1)
                if t:
                    act.wait_ge(sem("qr_sent"), 32 * t)
                act.activation(k.qrT[0][:, :, :], ps[:, 4 + t % 2, :].rearrange("p (a b) -> p a b", b=P), ACT.Copy).then_inc(sem("qrT_hi"), 1)

        @block.vector
        def _(dve):
            dve.memset(pre[:, :, 0:4], 0.0).then_inc(sem("pad_set"), 1)
            dve.wait_ge(sem("wdt_in"), 16)
            dve.tensor_copy(wd[0][:, :, :], wdt[:, :, :]).then_inc(sem("wdt_cut"), 1)
            dve.wait_ge(sem("wdt_cut"), 1)
            dve.tensor_tensor(wd[1][:, :, :], wdt[:, :, :], wd[0][:, :, :].bitcast(F32), ALU.subtract).then_inc(sem("wdt_cut"), 1)
            dve.memset(ss[:, :], 1.0).then_inc(sem("stat_set"), 1)

            def out_x(f, parts):
                if f < KD and 1 in parts:
                    dve.wait_ge(sem("x_turned"), 3 * f + 2)
                    if f >= 2:
                        dve.wait_ge(sem(f"xt_sent{f % 2}"), 32 * (f // 2))
                    dve.tensor_copy(xt[:, f % 2, 4:8, :], ps[:, 7, :].rearrange("p (a b) -> p a b", b=P)).then_inc(sem("xt1_out"), 1)
                for part in parts:
                    if f < KD:
                        continue
                    name = ("xt0_out", "xt1_out", "xt2_out")[part]
                    dve.wait_ge(sem("bt_hi"), 3 * (f - KD) + part + 1)
                    if part == 0 and f > KD:
                        dve.wait_ge(sem("bt_sent"), 64 * (f - KD))
                    if part < 2:
                        src = ps[:, 6 + part, :].rearrange("p (a b) -> p a b", b=P)
                        hi, lo = (x[:, 4 * part:4 * part + 4, :] for x in bt)
                    else:
                        src = ps[0:META, 6, 0:P]
                        hi, lo = (x[0:META, NT, :] for x in bt)
                    dve.tensor_tensor(lo, src, hi.bitcast(F32), ALU.subtract).then_inc(sem(name), 1)

            for f in range(NX):
                if 2 <= f <= NXT + 1:
                    out_x(f - 2, (2,))
                if 1 <= f <= NXT:
                    out_x(f - 1, (0, 1))
                dve.wait_ge(sem("pre_out"), 3 * f + 3)
                if f == 0:
                    dve.wait_ge(sem("pad_set"), 1)
                if f >= 2:
                    dve.wait_ge(sem("xc_done"), f - 1)
                a = acc[:, f % 2, :]
                for i in range(4):
                    w = col(k, "convw", 4 * f + i)
                    src = pre[:, f % 2, 1 + i:1 + i + POS]
                    if i == 0:
                        dve.tensor_scalar(a, src, w, None, ALU.mult).then_inc(sem("conv_step"), 1)
                    else:
                        dve.wait_ge(sem("conv_step"), 3 * f + i)
                        mm = dve.scalar_tensor_tensor(a, src, w, a, ALU.mult, ALU.add)
                        mm.then_inc(sem("conv_done" if i == 3 else "conv_step"), 1)
                if f >= KD:
                    dve.wait_ge(sem("bc_hi"), f - KD + 1)
                    if f > KD:
                        dve.wait_ge(sem("bc_sent"), 32 * (f - KD))
                    dve.tensor_tensor(fb[1][:, :], xc[:, f % 2, META:POS], fb[0][:, :].bitcast(F32), ALU.subtract).then_inc(sem("bc_lo"), 1)
            dve.wait_ge(sem("xc_done"), NX)
            dve.wait_ge(sem("bc_lo"), NX - KD)
            dve.wait_ge(sem("bt_sent"), 64 * GROUPS)
            dve.wait_ge(sem("bc_sent"), 32 * 2 * GROUPS)
            for q in range(2):
                dve.wait_ge(sem(f"xt_sent{q}"), 32 * KD // 2)
            dve.memset(cks[:, NT, :], 0.0).then_inc(sem("rest_set"), 1)
            dve.memset(kro[:, :, ROPE:P], 0.0).then_inc(sem("rest_set"), 1)
            dve.memset(k.dt[:, NT, :], 0.0).then_inc(sem("rest_set"), 1)
            for t in range(NT):
                dve.wait_ge(sem("cq_done"), t + 1)
                dve.tensor_copy(cqs[:, t, :], ps[:, t % 4, 0:QL]).then_inc(sem("cq_out"), 1)
            dve.wait_ge(sem("rest_set"), 3)
            for t in range(NT + 1):
                rows = P if t < NT else META
                dve.wait_ge(sem("ck_done"), t + 1)
                dve.tensor_copy(cks[0:rows, t, :], ps[0:rows, t % 4, 0:KVL + ROPE]).then_inc(sem("ck_raw"), 1)
                dve.tensor_copy(k.dt[0:rows, t, :], ps[0:rows, t % 4, KVL + ROPE:KVL + ROPE + SH]).then_inc(sem("ck_out"), 1)
            dve.wait_ge(sem("lat_sq"), NW)
            rsqrt_before(dve, k, v[:, 0:NT], ss[:, 0:NT], 1.0 / QL, "lat_v", 1)
            rsqrt_before(dve, k, v[:, NT:NW], ss[:, NT:NW], 1.0 / KVL, "lat_v", 2)
            rsqrt_after(dve, k, r[:, 0:NW], v[:, 0:NW], s_[:, 0:NW], t1[:, 0:NW], "lat_sqrt", 1, "rs2")
            for t in range(NT):
                dve.tensor_scalar(cqs[:, t, :], cqs[:, t, :], r[:, t:t + 1], None, ALU.mult).then_inc(sem("cq_scaled"), 1)
            for t in range(NT + 1):
                rows = P if t < NT else META
                dve.tensor_scalar(cks[0:rows, t, 0:KVL], cks[0:rows, t, 0:KVL], r[0:rows, NT + t:NT + t + 1], None,
                                  ALU.mult).then_inc(sem("ck_scaled"), 1)
            dve.wait_ge(sem("rope_in"), 16)
            dve.wait_ge(sem("ck_out"), NT + 1)
            x1, x2 = cks[:, :, KVL:KVL + 32], cks[:, :, KVL + 32:KVL + 64]
            cos, sin = rope[:, :, 0:32], rope[:, :, 32:64]
            a3, b3 = ta[:, 0:288].rearrange("p (t c) -> p t c", c=32), tb[:, 0:288].rearrange("p (t c) -> p t c", c=32)
            rotate(dve, k, x1, x2, cos, sin, a3, b3, kro[:, :, 0:32], kro[:, :, 32:64], "kro", 0)
            for n in range(13):
                c0 = 512 * (n % 2)
                src = ps[:, 4 + n % 4, :]
                if n == 12:
                    dve.wait_ge(sem("lat_turned"), 13)
                    w = k.par[:, PARAM["kva"]:PARAM["kva"] + 2].unsqueeze(2).broadcast_to([P, 2, META])
                    dve.tensor_tensor(mt[:, 0:2, :], ps[:, 4, 0:2 * META].rearrange("p (a b) -> p a b", a=2), w, ALU.mult).then_inc(sem("lat_mt"), 1)
                    dve.tensor_copy(mt[:, 2, :], ps[:, 4, 2 * META:3 * META]).then_inc(sem("lat_mt"), 1)
                    dve.wait_ge(sem("lat_hi"), 14)
                    dve.wait_ge(sem("lat_mt"), 2)
                    dve.tensor_tensor(k.ckT[1][:, :, 0:META], mt[:, 0:2, :], k.ckT[0][:, :, 0:META].bitcast(F32), ALU.subtract).then_inc(sem("lat_m"), 1)
                    dve.tensor_tensor(k.krT[1][:, 0:META], mt[:, 2, :], k.krT[0][:, 0:META].bitcast(F32), ALU.subtract).then_inc(sem("lat_lo"), 1)
                    continue
                dve.wait_ge(sem("lat_hi"), n + 1)
                if n < 6:
                    hi, lo = (x[:, n // 2, c0:c0 + 512] for x in k.cqT)
                    w = col(k, "qa", n // 2)
                elif n < 10:
                    kk = (n - 6) // 2
                    hi, lo = (x[:, kk, META + c0:META + c0 + 512] for x in k.ckT)
                    w = col(k, "kva", kk)
                else:
                    hi, lo = (x[:, META + c0:META + c0 + 512] for x in k.krT)
                    w = 1.0
                dve.scalar_tensor_tensor(lo, src, w, hi.bitcast(F32), ALU.mult, ALU.subtract).then_inc(sem("lat_lo"), 1)

            def low_qr(t):
                dve.wait_ge(sem("qrT_hi"), t + 1)
                if t:
                    dve.wait_ge(sem("qr_sent"), 32 * t)
                dve.tensor_tensor(k.qrT[1][:, :, :], ps[:, 4 + t % 2, :].rearrange("p (a b) -> p a b", b=P), k.qrT[0][:, :, :].bitcast(F32),
                                  ALU.subtract).then_inc(sem("qrT_lo"), 1)

            a3, b3 = ta[:, 0:256].rearrange("p (t c) -> p t c", c=32), tb[:, 0:256].rearrange("p (t c) -> p t c", c=32)
            for t in range(NT):
                dve.wait_ge(sem("qr_done"), t + 1)
                if t:
                    dve.wait_ge(sem("qr_turned"), t)
                q = ps[:, t % 4, :].rearrange("p (h c) -> p h c", c=ROPE)
                cos = rope[:, t, 0:32].unsqueeze(1).broadcast_to([P, HEADS, 32])
                sin = rope[:, t, 32:64].unsqueeze(1).broadcast_to([P, HEADS, 32])
                rotate(dve, k, q[:, :, 0:32], q[:, :, 32:64], cos, sin, a3, b3, qro[:, :, 0:32], qro[:, :, 32:64], "qro", t)
                if t:
                    low_qr(t - 1)
            low_qr(NT - 1)


def rotate(dve, k, x1, x2, cos, sin, a, b, out1, out2, name, turn):
    c = k.sem(name + "_step")
    n = 4 * turn
    if turn:
        dve.wait_ge(k.sem(name + "_done"), 2 * turn)
    dve.tensor_tensor(a, x1, cos, ALU.mult).then_inc(c, 1)
    dve.tensor_tensor(b, x2, sin, ALU.mult).then_inc(c, 1)
    dve.wait_ge(c, n + 2)
    dve.tensor_tensor(out1, a, b, ALU.subtract).then_inc(k.sem(name + "_done"), 1)
    dve.wait_ge(k.sem(name + "_done"), 2 * turn + 1)
    dve.tensor_tensor(a, x2, cos, ALU.mult).then_inc(c, 1)
    dve.tensor_tensor(b, x1, sin, ALU.mult).then_inc(c, 1)
    dve.wait_ge(c, n + 4)
    dve.tensor_tensor(out2, a, b, ALU.add).then_inc(k.sem(name + "_done"), 1)



def phase_attend(k):
    nc, sem, m, ps, io = k.nc, k.sem, k.map, k.ps, k.io
    o = O_RING

    def pair(name, shape, o):
        a, o = m.at(name + "hi", shape, F32R, o)
        b, o = m.at(name + "lo", shape, F32R, o)
        return (a, b), o

    kT, o = pair("kT", [P, POS], o)
    v, o = pair("v", [P, NT + 1, VH], o)
    wq, o = pair("wq", [P, QL // P, NOPE], o)
    wkv, o = pair("wkv", [P, KVL // P, NOPE + VH], o)
    assert o <= O_RING + 32768
    o = k.o_lat
    wq_f, o = m.at("wq_f", [P, QL // P, NOPE], F32, o)
    wkv_f, o = m.at("wkv_f", [P, KVL // P, NOPE + VH], F32, o)
    qT, o = pair("qT", [P, SEQ], o)
    qr, o = pair("qr", [ROPE, SEQ], o)
    pT, o = pair("pT", [P, NT + 1, 512], o)
    oT, o = pair("oT", [P, 2, 512], o)
    prob, o = m.at("prob", [P, 2, POS], F32, o)
    assert m.base + o <= k.dt_at
    mx, nb, sm, rs, bias = k.st[0], k.st[1], k.st[2], k.st[3], k.st[4]
    flat = ps[:, :, :].rearrange("p a b -> p (a b)")
    SB = (0, 1024)
    KQ, KK = QL // P, KVL // P
    PASSES = ((0, 0), (0, 1), (1, 0))
    wqh = io["w_q_up"][0].rearrange("(k p) (h c) -> h p k c", p=P, h=HEADS)
    wkh = io["w_kv_up"][0].rearrange("(k p) (h c) -> h p k c", p=P, h=HEADS)
    width = lambda b: META + P * (b + 1)
    batches = [(b, p0, min(4, b + 2 - p0)) for b in range(NT) for p0 in range(0, b + 2, 4)]
    NB = len(batches)
    assert NB % 2 == 0
    first_batch = [next(i for i, x in enumerate(batches) if x[0] == b) for b in range(NT)]

    def of_block(b):
        return [(i, x) for i, x in enumerate(batches) if x[0] == b]

    def evacs():
        for q in range(2):
            yield ps[:, q, :], [x[:, 512 * q:512 * q + 512] for x in qT]
        for q, (c0, w) in enumerate(TC):
            yield ps[:, 2 + q, 0:w], [x[:, c0:c0 + w] for x in kT]
        yield ps[0:META, 4, TC[2][1]:TC[2][1] + VH], [x[0:META, NT, :] for x in v]
        for q in range(2):
            yield ps[:, 5 + q, :].rearrange("p (a b) -> p a b", b=VH), [x[:, 4 * q:4 * q + 4, :] for x in v]
    EV = list(evacs())
    NE = len(EV)
    stage_of = [1, 1, 2, 2, 2, 2, 3, 3]

    with nc.Block() as block:
        @block.sync
        def _(sp):
            def weights(h):
                sp.dma_start(wq_f[:, :, :], wqh[h][:, :, 0:NOPE]).then_inc(sem("a_q_in"), 16)
                sp.dma_start(wkv_f[:, :, :], wkh[h]).then_inc(sem("a_kv_in"), 16)

            def rotated(h):
                for i in range(2):
                    sp.dma_start(qr[i][:, :].bitcast(F32), k.d_qr[i].rearrange("(h c) t -> h c t", c=ROPE)[h]).then_inc(sem("a_qr_in"), 16)

            def outputs(h, g):
                sp.wait_ge(sem("a_o_lo"), 2 * h + g + 2)
                for i in range(2):
                    sp.dma_start(k.d_att[i].rearrange("(h c) t -> h c t", c=VH)[h][:, 512 * g:512 * g + 512],
                                 oT[i][:, g, :].bitcast(F32)).then_inc(sem(f"a_sent{g}"), 16)

            weights(0)
            rotated(0)
            with sp.Fori(0, HEADS - 1) as h:
                sp.wait_ge(sem("a_cut"), 4 * h + 4)
                weights(h + 1)
                outputs(h, 0)
                sp.wait_ge(sem("a_s"), NT * h + NT)
                rotated(h + 1)
                outputs(h, 1)
            outputs(HEADS - 1, 0)
            outputs(HEADS - 1, 1)
            for g in range(2):
                sp.wait_ge(sem(f"a_sent{g}"), 32 * HEADS + 1)

        @block.gpsimd
        def _(pool):
            def cut(h, peeled):
                for src, dst, name in ((wq_f, wq, "a_q_in"), (wkv_f, wkv, "a_kv_in")):
                    n = 0 if name == "a_q_in" else 2
                    pool.wait_ge(sem(name), 16 * h + 16)
                    if not peeled and n == 0:
                        pool.wait_ge(sem("a_proj"), 3 * h)
                    a, hi, lo = (x[:, :, :].rearrange("p a b -> p (a b)") for x in (src, *dst))
                    pool.tensor_tensor(hi, a, k.zero[:, 0:1].broadcast_to([P, a.shape[-1]]), ALU.add).then_inc(sem("a_cut"), 1)
                    pool.wait_ge(sem("a_cut"), 4 * h + n + 1)
                    pool.tensor_tensor(lo, a, hi.bitcast(F32), ALU.subtract).then_inc(sem("a_cut"), 1)

            cut(0, True)
            with pool.Fori(1, HEADS) as h:
                cut(h, False)

        @block.tensor
        def _(pe):
            def project(h):
                pe.wait_ge(sem("a_cut"), 4 * h + 2)
                for kk in range(KQ):
                    for a, b in PASSES:
                        for q in range(2):
                            mm = pe.matmul(ps[:, q, :], wq[a][:, kk, :], k.cqT[b][:, kk, 512 * q:512 * q + 512],
                                           start=(kk == 0 and (a, b) == (0, 0)), stop=(kk == KQ - 1 and a == 1))
                mm.then_inc(sem("a_proj"), 1)
                pe.wait_ge(sem("a_cut"), 4 * h + 4)
                for kk in range(KK):
                    for a, b in PASSES:
                        for q, (c0, w) in enumerate(TC):
                            pe.matmul(ps[:, 2 + q, 0:w], wkv[a][:, kk, 0:NOPE], k.ckT[b][:, kk, c0:c0 + w],
                                      start=(kk == 0 and (a, b) == (0, 0)), stop=(kk == KK - 1 and a == 1))

                def values(out, c0):
                    for kk in range(KK):
                        for a, b in PASSES:
                            mm = pe.matmul(out, k.ckT[a][:, kk, c0:c0 + P], wkv[b][:, kk, NOPE:NOPE + VH],
                                           start=(kk == 0 and (a, b) == (0, 0)), stop=(kk == KK - 1 and a == 1))
                    return mm

                values(ps[:, 4, TC[2][1]:TC[2][1] + VH], 0).then_inc(sem("a_proj"), 1)
                for t in range(NT):
                    mm = values(ps[:, 5 + t // 4, VH * (t % 4):VH * (t % 4) + VH], META + P * t)
                mm.then_inc(sem("a_proj"), 1)

            def scores(h, b):
                n, s0 = width(b), SB[b % 2]
                if b == 0:
                    pe.wait_ge(sem("a_e_lo"), NE * h + 5)
                    pe.wait_ge(sem("a_qr_in"), 32 * h + 32)
                if b >= 2:
                    pe.wait_ge(sem("a_exp"), NT * h + b - 1)
                tiles = [(c, min(n, c + 512)) for c in range(0, n, 512)]
                d0, d1 = n - P, n
                for i, (c0, c1) in enumerate(tiles):
                    out = flat[:, s0 + c0:s0 + c1]
                    q = slice(P * b, P * b + P)
                    pe.matmul(out, qT[0][:, q], kT[0][:, c0:c1], start=True, stop=False)
                    lo, hi = max(c0, d0), min(c1, d1)
                    if lo < hi:
                        pe.matmul(flat[:, s0 + lo:s0 + hi], k.mask_b[:, :], k.ident_b[:, lo - d0:hi - d0], start=False, stop=False)
                    pe.matmul(out, qT[0][:, q], kT[1][:, c0:c1], start=False, stop=False)
                    pe.matmul(out, qT[1][:, q], kT[0][:, c0:c1], start=False, stop=False)
                    for a, c in PASSES:
                        mm = pe.matmul(out, qr[a][:, q], k.krT[c][0:ROPE, c0:c1], start=False, stop=(a == 1))
                mm.then_inc(sem("a_s"), 1)

            def turn(h, b):
                pe.wait_ge(sem("a_p"), NT * h + b + 1)
                if b == 0:
                    pe.wait_ge(sem("a_e_lo"), NE * h + NE)
                for i, (_, p0, np_) in of_block(b):
                    if i >= 2:
                        pe.wait_ge(sem("a_t_lo"), NB * h + i - 1)
                    for j in range(np_):
                        c0 = 0 if p0 + j == 0 else META + P * (p0 + j - 1)
                        mm = pe.transpose(ps[:, 5 + i % 2, P * j:P * j + P], prob[:, b % 2, c0:c0 + P], k.ident[:, :])
                    mm.then_inc(sem("a_t"), 1)

            def weigh(h, g):
                pe.wait_ge(sem("a_t_lo"), NB * h + (first_batch[4] if g == 0 else NB))
                pe.wait_ge(sem("a_o_lo"), 2 * h + g + 1)
                last = 4 * g + 3
                for j in range(-1, last + 1):
                    rows = slice(0, META if j < 0 else P)
                    vt = NT if j < 0 else j
                    c0 = P * max(0, j - 4 * g)
                    for a, b in PASSES:
                        mm = pe.matmul(ps[:, 7, c0:512], v[a][rows, vt, :], pT[b][rows, j + 1, c0:512],
                                       start=(j < 0 and (a, b) == (0, 0)), stop=(j == last and a == 1))
                mm.then_inc(sem("a_o"), 1)

            with pe.Fori(0, HEADS) as h:
                project(h)
                scores(h, 0)
                for b in range(1, NT):
                    scores(h, b)
                    turn(h, b - 1)
                    if b == 4:
                        weigh(h, 0)
                turn(h, NT - 1)
                weigh(h, 1)

        @block.scalar
        def _(act):
            def high(h, b):
                for i, (_, p0, np_) in of_block(b):
                    act.wait_ge(sem("a_t"), NB * h + i + 1)
                    act.activation(pT[0][:, p0:p0 + np_, P * (b % 4):P * (b % 4) + P],
                                   ps[:, 5 + i % 2, 0:P * np_].rearrange("p (a b) -> p a b", b=P), ACT.Copy).then_inc(sem("a_t_hi"), 1)

            def exp(h, b):
                n, s0 = width(b), SB[b % 2]
                act.wait_ge(sem("a_nb"), NT * h + b + 1)
                act.activation(prob[:, b % 2, 0:n], flat[:, s0:s0 + n], ACT.Exp, bias=nb[:, b:b + 1], scale=SCALE,
                               accum_out=sm[:, b:b + 1]).then_inc(sem("a_exp"), 1)

            def out(h, g):
                act.wait_ge(sem("a_o"), 2 * h + g + 1)
                act.wait_ge(sem(f"a_sent{g}"), 32 * h + 1)
                act.activation(oT[0][:, g, :], ps[:, 7, :], ACT.Copy).then_inc(sem("a_o_hi"), 1)

            with act.Fori(0, HEADS) as h:
                for i, (src, dst) in enumerate(EV):
                    act.wait_ge(sem("a_proj"), 3 * h + stage_of[i])
                    act.activation(dst[0], src, ACT.Copy).then_inc(sem("a_e_hi"), 1)
                exp(h, 0)
                for b in range(1, NT):
                    exp(h, b)
                    high(h, b - 1)
                    if b == 4:
                        out(h, 0)
                high(h, NT - 1)
                out(h, 1)

        @block.vector
        def _(dve):
            dve.memset(bias[:, 0:1], 0.0).then_inc(sem("a_o_lo"), 1)
            for g in range(2):
                dve.memset(bias[:, 1 + g:2 + g], 0.0).then_inc(sem(f"a_sent{g}"), 1)

            def most(h, b):
                n, s0 = width(b), SB[b % 2]
                dve.wait_ge(sem("a_s"), NT * h + b + 1)
                dve.tensor_reduce(mx[:, b:b + 1], flat[:, s0:s0 + n], AX.X, ALU.max).then_inc(sem("a_mx"), 1)
                dve.wait_ge(sem("a_mx"), NT * h + b + 1)
                dve.tensor_scalar(nb[:, b:b + 1], mx[:, b:b + 1], -SCALE, None, ALU.mult).then_inc(sem("a_nb"), 1)

            def normalise(h, b):
                n = width(b)
                dve.wait_ge(sem("a_exp"), NT * h + b + 1)
                dve.reciprocal(rs[:, b:b + 1], sm[:, b:b + 1]).then_inc(sem("a_rs"), 1)
                dve.wait_ge(sem("a_rs"), NT * h + b + 1)
                dve.tensor_scalar(prob[:, b % 2, 0:n], prob[:, b % 2, 0:n], rs[:, b:b + 1], None, ALU.mult).then_inc(sem("a_p"), 1)

            def low(h, b):
                for i, (_, p0, np_) in of_block(b):
                    dve.wait_ge(sem("a_t_hi"), NB * h + i + 1)
                    hi, lo = (x[:, p0:p0 + np_, P * (b % 4):P * (b % 4) + P] for x in pT)
                    dve.tensor_tensor(lo, ps[:, 5 + i % 2, 0:P * np_].rearrange("p (a b) -> p a b", b=P), hi.bitcast(F32),
                                      ALU.subtract).then_inc(sem("a_t_lo"), 1)

            def out(h, g):
                dve.wait_ge(sem("a_o_hi"), 2 * h + g + 1)
                dve.tensor_tensor(oT[1][:, g, :], ps[:, 7, :], oT[0][:, g, :].bitcast(F32), ALU.subtract).then_inc(sem("a_o_lo"), 1)

            with dve.Fori(0, HEADS) as h:
                for i, (src, dst) in enumerate(EV):
                    dve.wait_ge(sem("a_e_hi"), NE * h + (6 if i == 4 else i + 1))
                    dve.tensor_tensor(dst[1], src, dst[0].bitcast(F32), ALU.subtract).then_inc(sem("a_e_lo"), 1)
                most(h, 0)
                for b in range(1, NT):
                    most(h, b)
                    normalise(h, b - 1)
                    low(h, b - 1)
                    if b == 4:
                        out(h, 0)
                normalise(h, NT - 1)
                low(h, NT - 1)
                out(h, 1)



def phase_ssd(k):
    nc, sem, m, ps, io = k.nc, k.sem, k.map, k.ps, k.io
    k.fam = "u"
    wo = io["w_out"][0]
    k.wo_blocks = [wo[D * part + P * kk:D * part + P * kk + P, 512 * c:512 * c + 512] for part in range(2) for c in range(2) for kk in range(KD)]
    o = O_R

    def pair(name, shape, o):
        a, o = m.at(name + "hi", shape, F32R, o)
        b, o = m.at(name + "lo", shape, F32R, o)
        return (a, b), o

    xs, o = m.at("s_x", [P, 2, SSMW], F32, o)
    zs, o = m.at("s_z", [P, 2, SSMW], F32, o)
    bT, o = pair("s_bT", [P, 2, GROUPS, P], o)
    cT, o = pair("s_cT", [P, 2, GROUPS, P], o)
    bt, o = pair("s_bt", [P, 2, GROUPS * STATE], o)
    aT, o = pair("s_aT", [P, 2, KD, P], o)
    xdt, o = m.at("xdt", [P, SSMW], F32, o)
    xh, o = pair("xdt_", [P, SSMW], o)
    xw, o = m.at("xw", [P, SSMW], F32, o)
    xwh, o = pair("xw_", [P, SSMW], o)
    xd, o = m.at("xd", [P, SSMW], F32, o)
    state, o = m.at("state", [P, SSMW], F32, o)
    sth, o = pair("state_", [P, SSMW], o)
    es, o = m.at("es", [P, 2, 512], F32, o)
    wl, o = pair("wl", [P, 2, 4, P], o)
    cbs, o = m.at("cbs", [P, GROUPS, P], F32, o)
    y, o = m.at("y", [P, SSMW], F32, o)
    mixs, o = m.at("mixs", [P, 2, D], F32, o)
    sT, o = pair("sT", [P, KD, P], o)
    dac, o = pair("dac", [P, SH], o)
    assert o <= O_TABLES
    junk = xd
    dt = k.dt

    T9 = [P, NT + 1, SH]
    op = O_R
    pa, op = m.at("p_a", T9, F32, op)
    pb, op = m.at("p_b", T9, F32, op)
    pc, op = m.at("p_c", T9, F32, op)
    dtb, op = m.at("p_dtb", [P, SH], F32, op)
    av, op = m.at("p_a_log", [P, SH], F32, op)
    xm, op = m.at("p_xm", [META, SSMW], F32, op)
    bm, op = pair("p_bm", [META, GROUPS * STATE], op)
    od = O_TABLES
    da, od = pair("da", T9, od)
    acum, od = m.at("acum", T9, F32, od)
    ecum, od = m.at("ecum", T9, F32, od)
    dend, od = m.at("dend", T9, F32, od)
    cdec, od = m.at("cdec", T9, F32, od)
    dsk, od = m.at("dskip", [P, SH], F32, od)
    wrow, od = m.at("ssm_w", [P, SSMW], F32, od)
    ss, v, s_, r, t1 = k.st[0], k.st[1], k.st[2], k.st[3], k.st[4]
    PASSES = ((0, 0), (0, 1), (1, 0))
    W = (k.whi, k.wlo)
    heads = lambda a: a.rearrange("p (h c) -> p h c", c=SHD)
    flat9 = lambda a: a[:, :, :].rearrange("p a b -> p (a b)")
    by_head = lambda a, rows=P: a.unsqueeze(2).broadcast_to([rows, SH, SHD])
    N9 = (NT + 1) * SH

    with nc.Block() as block:
        @block.sync
        def _(sp):
            sp.dma_start(dtb[:, :], io["dt_bias"][0].partition_broadcast(P)).then_inc(sem("p_in"), 16)
            sp.dma_start(av[:, :], io["a_log"][0].partition_broadcast(P)).then_inc(sem("p_in"), 16)
            sp.dma_start(dsk[:, :], io["d_skip"][0].partition_broadcast(P)).then_inc(sem("p_in"), 16)
            sp.dma_start(xm[:, :], k.d_xm).then_inc(sem("p_in"), 16)
            for i in range(2):
                sp.dma_start(bm[i][:, :].bitcast(F32), k.d_bm[i]).then_inc(sem("p_in"), 16)
            sp.dma_start(wrow[:, :], io["ssm_norm"][0].partition_broadcast(P)).then_inc(sem("p_in"), 16)
            for n in range(RING):
                load_block(sp, k, n, k.wo_blocks[n])

            def loads(t, u):
                rows = lambda a: a.rearrange("(t p) n -> t p n", p=P)[t]
                cols = lambda a: a.rearrange("(k p) (t n) -> t p k n", p=P, n=P)[t]
                sp.dma_start(xs[:, u, :], rows(k.d_x)).then_inc(sem(f"s_x_in{u}"), 16)
                for i in range(2):
                    sp.dma_start(bT[i][:, u, :, :].bitcast(F32), cols(k.d_bt[i])).then_inc(sem(f"s_bc_in{u}"), 16)
                    sp.dma_start(cT[i][:, u, :, :].bitcast(F32), cols(k.d_ct[i])).then_inc(sem(f"s_bc_in{u}"), 16)
                    sp.dma_start(bt[i][:, u, :].bitcast(F32), rows(k.d_b[i])).then_inc(sem(f"s_bc_in{u}"), 16)
                for i in range(2):
                    sp.dma_start(aT[i][:, u, :, :].bitcast(F32), cols(k.d_att[i])).then_inc(sem(f"s_at_in{u}"), 16)
                sp.dma_start(zs[:, u, :], rows(k.d_z)).then_inc(sem(f"s_z_in{u}"), 16)

            def stores(t, u):
                sp.wait_ge(sem("s_mixc"), 2 * t + 3)
                sp.dma_start(k.d_mix.rearrange("(t p) n -> t p n", p=P)[t], mixs[:, u, :]).then_inc(sem(f"s_mix_sent{u}"), 16)
                sp.wait_ge(sem("s_end"), t + 2)
                for i in range(2):
                    sp.dma_start(k.d_ssm[i].rearrange("(k p) (t n) -> t p k n", p=P, n=P)[t], sT[i][:, :, :].bitcast(F32)).then_inc(sem("s_sent"), 16)

            sp.wait_ge(sem("s_ready"), 1)
            loads(0, 0)
            loads(1, 1)
            with sp.Fori(0, NT // 2 - 1) as i:
                for u in range(2):
                    stores(2 * i + u, u)
                    loads(2 * i + u + 2, u)
            for u in range(2):
                stores(NT - 2 + u, u)
            for n in range(RING, RING + STAGES):
                load_block(sp, k, n, k.wo_blocks[n])
            sp.wait_ge(sem("s_sent"), 32 * NT + 1)
            for u in range(2):
                sp.wait_ge(sem(f"s_mix_sent{u}"), 16 * NT // 2 + 1)

        @block.gpsimd
        def _(pool):
            for n in range(RING):
                cut_block(pool, k, n, 512)
            with pool.Fori(0, NT // 2) as i:
                for u in range(2):
                    t = 2 * i + u
                    pool.wait_ge(sem("s_xdt"), t + 1)
                    pool.tensor_tensor(heads(xw[:, :]), heads(xdt[:, :]), by_head(dend[:, t, :]), ALU.mult).then_inc(sem("s_xw"), 1)
                    pool.wait_ge(sem("s_xh"), t + 1)
                    pool.tensor_tensor(xh[1][:, :], xdt[:, :], xh[0][:, :].bitcast(F32), ALU.subtract).then_inc(sem("s_xlo"), 1)
                    pool.wait_ge(sem("s_xwh"), t + 1)
                    pool.tensor_tensor(xwh[1][:, :], xw[:, :], xwh[0][:, :].bitcast(F32), ALU.subtract).then_inc(sem("s_xwlo"), 1)
                    pool.tensor_tensor(heads(xd[:, :]), heads(xs[:, u, :]), by_head(dsk[:, :]), ALU.mult).then_inc(sem("s_xd"), 1)

        @block.tensor
        def _(pe):
            pe.wait_ge(sem("p_da"), 2)
            for bank, lhs in ((0, k.tri), (1, k.ones)):
                for a in range(2):
                    pe.matmul(ps[:, bank, 0:NT * SH], lhs[:, :], da[a][:, 0:NT, :].rearrange("p a b -> p (a b)"), start=(a == 0), stop=(a == 1))
                for a in range(2):
                    mm = pe.matmul(ps[:, bank, NT * SH:N9], lhs[0:META, :], da[a][0:META, NT, :], start=(a == 0), stop=(a == 1))
            mm.then_inc(sem("p_sums"), 1)
            pe.wait_ge(sem("p_xwlo"), 1)
            for g in range(GROUPS):
                for a, b in PASSES:
                    mm = pe.matmul(ps[:, 4 + g, :], bm[a][:, P * g:P * g + P], xwh[b][0:META, 512 * g:512 * g + 512], start=(a == 0 and b == 0), stop=(a == 1))
            mm.then_inc(sem("p_state"), 1)

            def decays(q):
                bank = 7 - q % 2
                pe.matmul(ps[:, bank, :], k.ident_b[:, :], k.mask_b[:, :].unsqueeze(1).broadcast_to([P, 4, P]), start=True, stop=False)
                for j in range(4):
                    for a in range(2):
                        mm = pe.matmul(ps[:, bank, P * j:P * j + P], dac[a][:, 4 * q + j:4 * q + j + 1].broadcast_to([P, P]), k.tri[:, :],
                                       start=False, stop=(a == 1 and j == 3))
                mm.then_inc(sem("s_eb"), 1)

            def mix(t, c):
                if c == 0:
                    pe.wait_ge(sem("s_st"), t + 2)
                for kk in range(KD):
                    for a, b in PASSES:
                        mm = pe.matmul(ps[:, 4 + c, :], aT[a][:, t_buf[0], kk, :], W[b][:, 8 * c + kk, :],
                                       start=(kk == 0 and (a, b) == (0, 0)), stop=(kk == KD - 1 and a == 1))
                mm.then_inc(sem("s_mix"), 1)

            t_buf = [0]
            with pe.Fori(0, NT // 2) as i:
                for u in range(2):
                    t = 2 * i + u
                    t_buf[0] = u
                    pe.wait_ge(sem("s_end"), t + 1)
                    pe.wait_ge(sem(f"s_bc_in{u}"), 96 * i + 96)
                    for g in range(GROUPS):
                        for a, b in PASSES:
                            mm = pe.matmul(ps[:, 6, P * g:P * g + P], bT[a][:, u, g, :], cT[b][:, u, g, :], start=(a == 0 and b == 0), stop=(a == 1))
                    mm.then_inc(sem("s_cb"), 1)
                    pe.wait_ge(sem("s_dac"), 2 * t + 2)
                    decays(0)
                    pe.wait_ge(sem("s_stlo"), t + 1)
                    for g in range(GROUPS):
                        for a, b in PASSES:
                            mm = pe.matmul(ps[:, g, :], cT[a][:, u, g, :], sth[b][:, 512 * g:512 * g + 512], start=(a == 0 and b == 0), stop=(a == 1))
                    mm.then_inc(sem("s_off"), 1)
                    pe.wait_ge(sem("s_cbs"), t + 1)
                    decays(1)
                    pe.wait_ge(sem("s_mixc"), 2 * t + 1)
                    pe.wait_ge(sem("s_xwlo"), t + 1)
                    for g in range(GROUPS):
                        for a, b in PASSES:
                            mm = pe.matmul(ps[:, 4 + g, :], bt[a][:, u, P * g:P * g + P], xwh[b][:, 512 * g:512 * g + 512],
                                           start=(a == 0 and b == 0), stop=(a == 1))
                    mm.then_inc(sem("s_stp"), 1)
                    for q in (2, 3):
                        pe.wait_ge(sem("s_sub"), 4 * t + q - 1)
                        decays(q)
                    pe.wait_ge(sem(f"s_at_in{u}"), 32 * i + 32)
                    if u == 0:
                        pe.wait_ge(sem("u_cut"), RING)
                    mix(t, 0)
                    pe.wait_ge(sem("s_xlo"), t + 1)
                    for q in range(4):
                        pe.wait_ge(sem("s_wlo"), 4 * t + q + 1)
                        for j in range(4):
                            h = 4 * q + j
                            out = ps[:, 2 + h // 8, SHD * (h % 8):SHD * (h % 8) + SHD]
                            for a, b in PASSES:
                                mm = pe.matmul(out, wl[a][:, q % 2, j, :], xh[b][:, SHD * h:SHD * h + SHD], start=(a == 0 and b == 0), stop=(a == 1))
                        mm.then_inc(sem("s_dg"), 1)
                    mix(t, 1)
                    pe.wait_ge(sem("s_g"), 2 * t + 2)
                    for c in range(2):
                        for j in range(4):
                            kk = 4 * c + j
                            mm = pe.transpose(ps[:, 6 + c, P * j:P * j + P], y[:, P * kk:P * kk + P], k.ident[:, :])
                        mm.then_inc(sem("s_tr"), 1)

        @block.scalar
        def _(act):
            act.wait_ge(sem("p_x"), 2)
            act.activation(flat9(pb), flat9(pa), ACT.Exp, scale=-1.0).then_inc(sem("p_u"), 1)
            act.activation(av[:, :], av[:, :], ACT.Exp).then_inc(sem("p_u"), 1)
            act.wait_ge(sem("p_w"), 1)
            act.activation(flat9(pc), flat9(pa), ACT.Ln).then_inc(sem("p_ln"), 1)
            act.wait_ge(sem("p_dt"), 1)
            act.activation(flat9(da[0]), flat9(pb), ACT.Copy).then_inc(sem("p_da"), 1)
            act.wait_ge(sem("p_diff"), 3)
            act.activation(flat9(ecum), flat9(acum), ACT.Exp).then_inc(sem("p_exp"), 1)
            act.activation(flat9(dend), flat9(pa), ACT.Exp).then_inc(sem("p_exp"), 1)
            act.activation(flat9(cdec), flat9(pc), ACT.Exp).then_inc(sem("p_exp"), 1)
            act.wait_ge(sem("p_xw"), 2)
            act.activation(xwh[0][0:META, :], xw[0:META, :], ACT.Copy).then_inc(sem("p_xwhi"), 1)
            act.wait_ge(sem("p_st0"), 1)
            act.activation(sth[0][:, :], state[:, :], ACT.Copy).then_inc(sem("s_sthi"), 1)

            with act.Fori(0, NT // 2) as i:
                for u in range(2):
                    t = 2 * i + u

                    def w_hi(q):
                        act.wait_ge(sem("s_wm"), 4 * t + q + 1)
                        if q >= 2:
                            act.wait_ge(sem("s_dg"), 4 * t + q - 1)
                        act.activation(wl[0][:, q % 2, :, :].rearrange("p a b -> p (a b)"), es[:, q % 2, :], ACT.Copy).then_inc(sem("s_whi"), 1)

                    def expo(q):
                        act.wait_ge(sem("s_sub"), 4 * t + q + 1)
                        act.activation(es[:, q % 2, :], es[:, q % 2, :], ACT.Exp).then_inc(sem("s_exp"), 1)

                    def mix_out(c):
                        act.wait_ge(sem("s_mix"), 2 * t + c + 1)
                        if c == 0:
                            act.wait_ge(sem(f"s_mix_sent{u}"), 16 * i + 1)
                        act.activation(mixs[:, u, 512 * c:512 * c + 512], ps[:, 4 + c, :], ACT.Copy).then_inc(sem("s_mixc"), 1)

                    act.wait_ge(sem("s_cb"), t + 1)
                    act.activation(cbs[:, :, :].rearrange("p a b -> p (a b)"), ps[:, 6, 0:GROUPS * P], ACT.Copy).then_inc(sem("s_cbs"), 1)
                    act.wait_ge(sem("s_xdt"), t + 1)
                    act.activation(xh[0][:, :], xdt[:, :], ACT.Copy).then_inc(sem("s_xh"), 1)
                    expo(0)
                    expo(1)
                    act.wait_ge(sem("s_xw"), t + 1)
                    act.activation(xwh[0][:, :], xw[:, :], ACT.Copy).then_inc(sem("s_xwh"), 1)
                    w_hi(0)
                    w_hi(1)
                    expo(2)
                    expo(3)
                    act.wait_ge(sem("s_st"), t + 2)
                    act.activation(sth[0][:, :], state[:, :], ACT.Copy).then_inc(sem("s_sthi"), 1)
                    w_hi(2)
                    w_hi(3)
                    mix_out(0)
                    act.wait_ge(sem("s_gz"), t + 1)
                    for g in range(GROUPS):
                        act.activation(junk[:, 512 * g:512 * g + 512], y[:, 512 * g:512 * g + 512], ACT.Square, accum_out=ss[:, g:g + 1]).then_inc(sem("s_sq"), 1)
                    act.wait_ge(sem("s_v"), t + 1)
                    act.activation(s_[:, 0:2], v[:, 0:2], ACT.Sqrt).then_inc(sem("s_sqrt"), 1)
                    mix_out(1)
                    act.wait_ge(sem("s_sent"), 32 * t + 1)
                    for c in range(2):
                        act.wait_ge(sem("s_tr"), 2 * t + c + 1)
                        act.activation(sT[0][:, 4 * c:4 * c + 4, :].rearrange("p a b -> p (a b)"), ps[:, 6 + c, :], ACT.Copy).then_inc(sem("s_gh"), 1)

        @block.vector
        def _(dve):
            d = sem("p_step")
            dve.wait_ge(sem("p_in"), 16 * 7)
            raw = dt[:, :, :]
            dve.tensor_tensor(raw, raw, dtb[:, :].unsqueeze(1).broadcast_to(T9), ALU.add).then_inc(sem("p_x"), 1)
            dve.wait_ge(sem("p_x"), 1)
            dve.scalar_tensor_tensor(flat9(pa), flat9(dt), -1.0, flat9(dt), ALU.mult, ALU.max).then_inc(sem("p_x"), 1)
            dve.wait_ge(sem("p_u"), 2)
            dve.tensor_scalar(flat9(pa), flat9(pb), 1.0, None, ALU.add).then_inc(sem("p_w"), 1)
            dve.wait_ge(sem("p_ln"), 1)
            dve.tensor_scalar(flat9(pa), flat9(pa), -1.0, None, ALU.add).then_inc(d, 1)
            dve.wait_ge(d, 1)
            dve.tensor_scalar(flat9(acum), flat9(pa), 0.0, None, ALU.is_equal).then_inc(d, 1)
            dve.wait_ge(d, 2)
            dve.tensor_tensor(flat9(pa), flat9(pa), flat9(acum), ALU.add).then_inc(d, 1)
            dve.tensor_tensor(flat9(pc), flat9(pc), flat9(acum), ALU.add).then_inc(d, 1)
            dve.wait_ge(d, 4)
            dve.tensor_tensor(flat9(pc), flat9(pc), flat9(pb), ALU.mult).then_inc(d, 1)
            dve.reciprocal(flat9(acum), flat9(pa)).then_inc(d, 1)
            dve.wait_ge(d, 6)
            dve.tensor_tensor(flat9(pc), flat9(pc), flat9(acum), ALU.mult).then_inc(d, 1)
            dve.wait_ge(d, 7)
            dve.scalar_tensor_tensor(flat9(dt), flat9(dt), 0.0, flat9(pc), ALU.max, ALU.add).then_inc(d, 1)
            dve.wait_ge(d, 8)
            dve.tensor_tensor(pc[:, :, :], raw, av[:, :].unsqueeze(1).broadcast_to(T9), ALU.mult).then_inc(d, 1)
            dve.wait_ge(d, 9)
            dve.tensor_scalar(flat9(pb), flat9(pc), -1.0, None, ALU.mult).then_inc(sem("p_dt"), 1)
            dve.wait_ge(sem("p_da"), 1)
            dve.tensor_tensor(flat9(da[1]), flat9(pb), flat9(da[0]).bitcast(F32), ALU.subtract).then_inc(sem("p_da"), 1)
            dve.wait_ge(sem("p_sums"), 1)
            dve.tensor_copy(flat9(acum), ps[:, 0, 0:N9]).then_inc(sem("p_diff"), 1)
            dve.tensor_copy(flat9(pc), ps[:, 1, 0:N9]).then_inc(sem("p_diff"), 1)
            dve.wait_ge(sem("p_diff"), 2)
            dve.tensor_tensor(flat9(pa), flat9(pc), flat9(acum), ALU.subtract).then_inc(sem("p_diff"), 1)
            dve.tensor_tensor(heads(xw[0:META, :]), heads(xm[:, :]), by_head(dt[0:META, NT, :], META), ALU.mult).then_inc(sem("p_xw"), 1)
            dve.wait_ge(sem("p_exp"), 3)
            dve.wait_ge(sem("p_xw"), 1)
            dve.tensor_tensor(heads(xw[0:META, :]), heads(xw[0:META, :]), by_head(dend[0:META, NT, :], META), ALU.mult).then_inc(sem("p_xw"), 1)
            dve.wait_ge(sem("p_xwhi"), 1)
            dve.tensor_tensor(xwh[1][0:META, :], xw[0:META, :], xwh[0][0:META, :].bitcast(F32), ALU.subtract).then_inc(sem("p_xwlo"), 1)
            dve.wait_ge(sem("p_state"), 1)
            dve.tensor_copy(state[:, :], ps[:, 4:6, :].rearrange("p a b -> p (a b)")).then_inc(sem("p_st0"), 1)
            dve.memset(r[:, 8:9], 0.0).then_inc(sem("s_mixc"), 1)
            dve.memset(r[:, 9:10], 0.0).then_inc(sem("s_mix_sent0"), 1)
            dve.memset(r[:, 10:11], 0.0).then_inc(sem("s_mix_sent1"), 1)
            dve.memset(r[:, 11:12], 0.0).then_inc(sem("s_sent"), 1)
            dve.memset(r[:, 12:13], 0.0).then_inc(sem("s_end"), 1)
            dve.memset(r[:, 13:14], 0.0).then_inc(sem("s_ready"), 1)
            dve.wait_ge(sem("s_sthi"), 1)
            dve.tensor_tensor(sth[1][:, :], state[:, :], sth[0][:, :].bitcast(F32), ALU.subtract).then_inc(sem("s_stlo"), 1)
            dve.memset(r[:, 14:15], 0.0).then_inc(sem("s_st"), 1)

            with dve.Fori(0, NT // 2) as i:
                for u in range(2):
                    t = 2 * i + u

                    def sub(q):
                        dve.wait_ge(sem("s_eb"), 4 * t + q + 1)
                        dve.tensor_tensor(es[:, q % 2, :].rearrange("p (a b) -> p a b", b=P), ps[:, 7 - q % 2, :].rearrange("p (a b) -> p a b", b=P),
                                          acum[:, t, 4 * q:4 * q + 4].unsqueeze(2).broadcast_to([P, 4, P]), ALU.subtract).then_inc(sem("s_sub"), 1)

                    def mul(q):
                        dve.wait_ge(sem("s_exp"), 4 * t + q + 1)
                        if q == 0:
                            dve.wait_ge(sem("s_cbs"), t + 1)
                        e = es[:, q % 2, :].rearrange("p (a b) -> p a b", b=P)
                        dve.tensor_tensor(e, e, cbs[:, q // 2, :].unsqueeze(1).broadcast_to([P, 4, P]), ALU.mult).then_inc(sem("s_wm"), 1)

                    def low(q):
                        dve.wait_ge(sem("s_whi"), 4 * t + q + 1)
                        hi, lo = (x[:, q % 2, :, :].rearrange("p a b -> p (a b)") for x in wl)
                        dve.tensor_tensor(lo, es[:, q % 2, :], hi.bitcast(F32), ALU.subtract).then_inc(sem("s_wlo"), 1)

                    dve.wait_ge(sem(f"s_x_in{u}"), 16 * i + 16)
                    dve.tensor_tensor(heads(xdt[:, :]), heads(xs[:, u, :]), by_head(dt[:, t, :]), ALU.mult).then_inc(sem("s_xdt"), 1)
                    for a in range(2):
                        dve.tensor_copy(dac[a][:, :], da[a][:, t, :].bitcast(F32)).then_inc(sem("s_dac"), 1)
                    sub(0)
                    sub(1)
                    mul(0)
                    mul(1)
                    low(0)
                    dve.wait_ge(sem("s_wlo"), 4 * t + 1)
                    sub(2)
                    low(1)
                    dve.wait_ge(sem("s_wlo"), 4 * t + 2)
                    sub(3)
                    dve.wait_ge(sem("s_off"), t + 1)
                    dve.tensor_tensor(heads(state[:, :]), heads(state[:, :]), by_head(cdec[:, t, :]), ALU.mult).then_inc(sem("s_dec"), 1)
                    dve.wait_ge(sem("s_stp"), t + 1)
                    dve.wait_ge(sem("s_dec"), t + 1)
                    dve.tensor_tensor(state[:, :], ps[:, 4:6, :].rearrange("p a b -> p (a b)"), state[:, :], ALU.add).then_inc(sem("s_st"), 1)
                    mul(2)
                    mul(3)
                    dve.wait_ge(sem("s_sthi"), t + 2)
                    dve.tensor_tensor(sth[1][:, :], state[:, :], sth[0][:, :].bitcast(F32), ALU.subtract).then_inc(sem("s_stlo"), 1)
                    low(2)
                    low(3)
                    n = 3 * t
                    dve.tensor_tensor(heads(y[:, :]), ps[:, 0:2, :].rearrange("p a (h c) -> p (a h) c", c=SHD), by_head(ecum[:, t, :]), ALU.mult).then_inc(sem("s_y"), 1)
                    dve.wait_ge(sem("s_y"), n + 1)
                    dve.wait_ge(sem("s_dg"), 4 * t + 4)
                    dve.tensor_tensor(y[:, :], ps[:, 2:4, :].rearrange("p a b -> p (a b)"), y[:, :], ALU.add).then_inc(sem("s_y"), 1)
                    dve.wait_ge(sem("s_y"), n + 2)
                    dve.wait_ge(sem("s_xd"), t + 1)
                    dve.tensor_tensor(y[:, :], xd[:, :], y[:, :], ALU.add).then_inc(sem("s_y"), 1)
                    dve.wait_ge(sem("s_y"), n + 3)
                    dve.wait_ge(sem(f"s_z_in{u}"), 16 * i + 16)
                    dve.tensor_tensor(y[:, :], y[:, :], zs[:, u, :], ALU.mult).then_inc(sem("s_gz"), 1)
                    dve.wait_ge(sem("s_sq"), 2 * t + 2)
                    rsqrt_before(dve, k, v[:, 0:2], ss[:, 0:2], 1.0 / (SSMW // GROUPS), "s_v", 1)
                    rsqrt_after(dve, k, r[:, 0:2], v[:, 0:2], s_[:, 0:2], t1[:, 0:2], "s_sqrt", t + 1, "s_rs", 5 * t)
                    for g in range(GROUPS):
                        part = slice(512 * g, 512 * g + 512)
                        dve.scalar_tensor_tensor(y[:, part], y[:, part], r[:, g:g + 1], wrow[:, part], ALU.mult, ALU.mult).then_inc(sem("s_g"), 1)
                    for c in range(2):
                        dve.wait_ge(sem("s_gh"), 2 * t + c + 1)
                        hi, lo = (x[:, 4 * c:4 * c + 4, :].rearrange("p a b -> p (a b)") for x in sT)
                        mm = dve.tensor_tensor(lo, ps[:, 6 + c, :], hi.bitcast(F32), ALU.subtract)
                        mm.then_inc(sem("s_end" if c else "s_half"), 1)



def cut_hi(act, k, n):
    act.wait_ge(k.sem(f"{k.fam}_landed{n % STAGES}"), 16 * (n // STAGES + 1))
    act.activation(k.whi[:, n % RING, :], k.stage[:, n % STAGES, :], ACT.Copy).then_inc(k.sem(k.fam + "_hi"), 1)


def cut_lo(dve, k, n):
    dve.wait_ge(k.sem(k.fam + "_hi"), n + 1)
    dve.tensor_tensor(k.wlo[:, n % RING, :], k.stage[:, n % STAGES, :], k.whi[:, n % RING, :].bitcast(F32), ALU.subtract).then_inc(k.sem(k.fam + "_cut"), 1)


def phase_mix(k):
    nc, sem, m, ps, io = k.nc, k.sem, k.map, k.ps, k.io
    o = O_R
    k.hmT = []
    for s in ("hi", "lo"):
        t, o = m.at("hmT" + s, [P, KD, SEQ], F32R, o)
        k.hmT.append(t)
    hmT = k.hmT
    sT = []
    for s in ("hi", "lo"):
        t, o = m.at("m_sT" + s, [P, 2, KD, P], F32R, o)
        sT.append(t)
    mix, o = m.at("m_mix", [P, 2, D], F32, o)
    h, o = m.at("m_h", [P, 2, D], F32, o)
    hn, o = m.at("m_hn", [P, 2, D], F32, o)
    junk, o = m.at("m_junk", [P, D], F32, o)
    wrow, o = m.at("m_wrow", [P, D], F32, o)
    ss, v, s_, r, t1 = k.st[0], k.st[1], k.st[2], k.st[3], k.st[4]
    W = (k.whi, k.wlo)
    PASSES = ((0, 0), (0, 1), (1, 0))
    PAIRS = NT // 2
    rows = lambda a, t: a.rearrange("(t p) n -> t p n", p=P)[t]
    cols = lambda a, t: a.rearrange("(k p) (t n) -> t p k n", p=P, n=P)[t]

    with nc.Block() as block:
        @block.sync
        def _(sp):
            def load_left(t, u):
                for i in range(2):
                    sp.dma_start(sT[i][:, u, :, :].bitcast(F32), cols(k.d_ssm[i], t)).then_inc(sem(f"m_s_in{u}"), 16)

            def load_mix(t, u):
                sp.dma_start(mix[:, u, :], rows(k.d_mix, t)).then_inc(sem(f"m_mix_in{u}"), 16)

            def load_h(t, u):
                sp.dma_start(h[:, u, :], rows(io["x"][0], t)).then_inc(sem(f"m_h_in{u}"), 16)

            def store(t, u):
                sp.wait_ge(sem("m_h"), t + 1)
                sp.dma_start(rows(k.d_h, t), h[:, u, :]).then_inc(sem(f"m_sent{u}"), 16)

            load_left(0, 0)
            for n in range(RING + STAGES, 2 * RING):
                load_block(sp, k, n, k.wo_blocks[n])
            load_left(1, 1)
            for u in range(2):
                load_mix(u, u)
                load_h(u, u)
            sp.dma_start(wrow[:, :], io["norm_mix_post"][0].partition_broadcast(P)).then_inc(sem("m_w_in"), 16)
            with sp.Fori(0, PAIRS - 1) as i:
                for u in range(2):
                    sp.wait_ge(sem("m_mm"), 4 * i + 2 * u + 2)
                    load_left(2 * i + u + 2, u)
                for u in range(2):
                    store(2 * i + u, u)
                    load_mix(2 * i + u + 2, u)
                for u in range(2):
                    sp.wait_ge(sem("m_hn"), 2 * i + u + 1)
                    sp.wait_ge(sem(f"m_sent{u}"), 16 * i + 16)
                    load_h(2 * i + u + 2, u)
            for u in range(2):
                store(NT - 2 + u, u)
            for u in range(2):
                sp.wait_ge(sem(f"m_sent{u}"), 16 * PAIRS)

        @block.tensor
        def _(pe):
            def mm_tile(t, u, first):
                pe.wait_ge(sem(f"m_s_in{u}"), 32 if first else 16 * (t - u) + 32)
                for c in range(2):
                    if not first:
                        pe.wait_ge(sem("m_add"), 2 * t + c - 3)
                    for kk in range(KD):
                        if first and u == 0:
                            pe.wait_ge(sem("u_cut"), RING + KD * c + kk + 1)
                        for a, b in PASSES:
                            mm = pe.matmul(ps[:, 2 * u + c, :], sT[a][:, u, kk, :], W[b][:, KD * c + kk, :],
                                           start=(kk == 0 and a == 0 and b == 0), stop=(kk == KD - 1 and a == 1))
                    mm.then_inc(sem("m_mm"), 1)

            def turn_pair(i):
                for u in range(2):
                    pe.wait_ge(sem("m_hn"), 2 * i + u + 1)
                    for c in range(2):
                        pe.wait_ge(sem("m_lo"), 4 * i + 2 * u + c + 1)
                        for j in range(4):
                            kk = 4 * c + j
                            mm = pe.transpose(ps[:, 4 + 2 * u + c, P * j:P * j + P], hn[:, u, P * kk:P * kk + P], k.ident[:, :])
                        mm.then_inc(sem("m_turned"), 1)

            for u in range(2):
                mm_tile(u, u, True)
            with pe.Fori(0, PAIRS - 1) as i:
                for u in range(2):
                    mm_tile(2 * i + u + 2, u, False)
                turn_pair(i)
            turn_pair(PAIRS - 1)

        @block.gpsimd
        def _(pool):
            with pool.Fori(0, PAIRS) as i:
                for u in range(2):
                    pool.wait_ge(sem("m_scaled"), 2 * i + u + 1)
                    pool.wait_ge(sem(f"m_h_in{u}"), 16 * i + 16)
                    pool.tensor_tensor(h[:, u, :], mix[:, u, :], h[:, u, :], ALU.add).then_inc(sem("m_h"), 1)

        @block.scalar
        def _(act):
            for n in range(RING, 2 * RING):
                cut_hi(act, k, n)
            with act.Fori(0, PAIRS) as i:
                for u in range(2):
                    act.wait_ge(sem("m_add"), 4 * i + 2 * u + 2)
                    act.wait_ge(sem("m_sq"), 4 * i + u + 1)
                    act.activation(junk[:, :], mix[:, u, :], ACT.Square, accum_out=ss[:, u:u + 1]).then_inc(sem("m_sq"), 1)
                act.wait_ge(sem("m_v"), 2 * i + 1)
                act.activation(s_[:, 0:2], v[:, 0:2], ACT.Sqrt).then_inc(sem("m_sqrt"), 1)
                for u in range(2):
                    act.wait_ge(sem("m_h"), 2 * i + u + 1)
                    act.wait_ge(sem("m_sq"), 4 * i + u + 3)
                    act.activation(junk[:, :], h[:, u, :], ACT.Square, accum_out=ss[:, 2 + u:3 + u]).then_inc(sem("m_sq"), 1)
                act.wait_ge(sem("m_v"), 2 * i + 2)
                act.activation(s_[:, 2:4], v[:, 2:4], ACT.Sqrt).then_inc(sem("m_sqrt"), 1)
                act.wait_ge(sem("m_r"), i + 1)
                for u in range(2):
                    act.wait_ge(sem("m_turned"), 4 * i + 2 * u + 2)
                    act.activation(hn[:, u, :], h[:, u, :], ACT.Copy, scale=r[:, 2 + u:3 + u]).then_inc(sem("m_hn"), 1)
                for n in range(4):
                    act.wait_ge(sem("m_turned"), 4 * i + n + 5)
                    for j in range(4):
                        kk = 4 * (n % 2) + j
                        act.activation(hmT[0][:, kk, bass.ds(P * (2 * i + n // 2), P)], ps[:, 4 + n, P * j:P * j + P], ACT.Copy, scale=col(k, "mlp", kk)).then_inc(sem("m_hi"), 1)

        @block.vector
        def _(dve):
            dve.memset(ss[:, :], 0.0).then_inc(sem("m_sq"), 1)
            dve.memset(v[:, :], 1.0).then_inc(sem("m_lo"), 4)
            dve.memset(t1[:, :], 0.0).then_inc(sem("m_turned"), 4)
            for n in range(RING, 2 * RING):
                cut_lo(dve, k, n)

            def add_pair(t, by_pairs):
                for u in range(2):
                    dve.wait_ge(sem(f"m_mix_in{u}"), by_pairs + 16)
                    for c in range(2):
                        dve.wait_ge(sem("m_mm"), 2 * t + 2 * u + c + 1)
                        part = mix[:, u, 512 * c:512 * c + 512]
                        dve.tensor_tensor(part, ps[:, 2 * u + c, :], part, ALU.add).then_inc(sem("m_add"), 1)

            def chain(i):
                dve.wait_ge(sem("m_sq"), 4 * i + 3)
                rsqrt_before(dve, k, v[:, 0:2], ss[:, 0:2], 1.0 / D, "m_v", 1)
                rsqrt_after(dve, k, r[:, 0:2], v[:, 0:2], s_[:, 0:2], t1[:, 0:2], "m_sqrt", 2 * i + 1, "m_rs", 10 * i)
                for u in range(2):
                    dve.scalar_tensor_tensor(mix[:, u, :], mix[:, u, :], r[:, u:u + 1], wrow[:, :], ALU.mult, ALU.mult).then_inc(sem("m_scaled"), 1)
                dve.wait_ge(sem("m_sq"), 4 * i + 5)
                rsqrt_before(dve, k, v[:, 2:4], ss[:, 2:4], 1.0 / D, "m_v", 1)
                rsqrt_after(dve, k, r[:, 2:4], v[:, 2:4], s_[:, 2:4], t1[:, 2:4], "m_sqrt", 2 * i + 2, "m_rs", 10 * i + 5)
                dve.tensor_copy(t1[:, 4:6], r[:, 2:4]).then_inc(sem("m_r"), 1)

            def low_pair(i):
                for n in range(4):
                    dve.wait_ge(sem("m_hi"), 16 * i + 4 * n + 4)
                    at = bass.ds(P * (2 * i + n // 2), P)
                    for j in range(4):
                        kk = 4 * (n % 2) + j
                        mm = dve.scalar_tensor_tensor(hmT[1][:, kk, at], ps[:, 4 + n, P * j:P * j + P], col(k, "mlp", kk), hmT[0][:, kk, at].bitcast(F32),
                                                      ALU.mult, ALU.subtract)
                    mm.then_inc(sem("m_lo"), 1)

            add_pair(0, 0)
            dve.wait_ge(sem("m_w_in"), 16)
            with dve.Fori(0, PAIRS - 1) as i:
                chain(i)
                add_pair(2 * i + 2, 16 * i + 16)
                low_pair(i)
            chain(PAIRS - 1)
            low_pair(PAIRS - 1)



def phase_mlp(k):
    nc, sem, m, ps, io = k.nc, k.sem, k.map, k.ps, k.io
    GRP = 512
    GRPS = DFF // GRP
    FT = GRP // P
    HALF = RING // 2
    PASSES = ((0, 0), (0, 1), (1, 0))
    W = (k.whi, k.wlo)
    hmT = k.hmT
    _, o = m.at("hmT_again", [P, 2, KD, SEQ], F32, O_R)
    f1 = []
    for s in ("hi", "lo"):
        t, o = m.at("f1" + s, [P, FT, SEQ], F32R, o)
        f1.append(t)
    acc, o = m.at("acc", [P, NT, D], F32, o)
    relu = (m.at("relu", [P, 512], F32, 0)[0], k.spare)
    h, oh = m.at("e_h", [P, NT, D], F32, O_R)
    wrow, oh = m.at("e_wrow", [P, D], F32, oh)
    junk, oh = m.at("e_junk", [P, D], F32, oh)
    ss, v, s_, r, t1 = k.st[0], k.st[1], k.st[2], k.st[3], k.st[4]
    up = io["w_mlp_up"][0].rearrange("(k p) (g n) -> g k p n", p=P, n=GRP)
    down = io["w_mlp_down"][0].rearrange("(g j p) (c n) -> g j c p n", p=P, j=FT, n=512)
    k.fam = "v"
    DN = 2 * NT
    UP = 2 * FT

    def block_of(g, n):
        return up[g, n] if n < HALF else down[g, (n - HALF) // 2, (n - HALF) % 2]

    with nc.Block() as block:
        @block.sync
        def _(sp):
            for n in range(RING):
                load_block(sp, k, n, block_of(0, n))
            with sp.Fori(1, GRPS) as g:
                for n in range(RING):
                    sp.wait_ge(sem("v_cut"), RING * g + n - STAGES + 1)
                    sp.dma_start(k.stage[:, n % STAGES, :], block_of(g, n)).then_inc(sem(f"v_landed{n % STAGES}"), 16)
            sp.wait_ge(sem("v_up"), UP * GRPS)
            sp.dma_start(wrow[:, :], io["norm_mlp_post"][0].partition_broadcast(P)).then_inc(sem("e_w_in"), 16)
            for t in range(NT):
                sp.dma_start(h[:, t, :], k.d_h[P * t:P * t + P]).then_inc(sem("e_h_in"), 16)
            for t in range(NT):
                sp.wait_ge(sem("e_out"), t + 1)
                sp.dma_start(io["out"][0, P * t:P * t + P, :], h[:, t, :]).then_inc(sem("e_sent"), 16)
            sp.wait_ge(sem("e_sent"), 16 * NT)

        @block.gpsimd
        def _(pool):
            for n in range(RING):
                cut_block(pool, k, n, 512)
            with pool.Fori(1, GRPS) as g:
                for n in range(RING):
                    if n == 0:
                        pool.wait_ge(sem("v_up"), UP * g)
                    if n == HALF:
                        pool.wait_ge(sem("v_down"), DN * g)
                    cut_block(pool, k, n, 512, RING * g, 16 * (RING // STAGES) * g)
            pool.wait_ge(sem("e_h_in"), 16 * NT)
            for t in range(NT):
                pool.wait_ge(sem("e_scaled"), t + 1)
                pool.tensor_tensor(h[:, t, :], acc[:, t, :], h[:, t, :], ALU.add).then_inc(sem("e_out"), 1)

        @block.tensor
        def _(pe):
            def group(g, first):
                for c in range(2):
                    for j in range(FT):
                        n = FT * c + j
                        pe.wait_ge(sem("v_sq_out"), UP * g + n + 1)
                        for kk in range(KD):
                            if c == 0 and j == 0:
                                pe.wait_ge(sem("v_cut"), RING * g + kk + 1)
                            for a, b in PASSES:
                                mm = pe.matmul(ps[:, n % 2, :], W[a][:, kk, P * j:P * j + P], hmT[b][:, kk, 512 * c:512 * c + 512],
                                               start=(kk == 0 and a == 0 and b == 0), stop=(kk == KD - 1 and a == 1))
                        mm.then_inc(sem("v_up"), 1)
                pe.wait_ge(sem("v_cut"), RING * g + RING)
                for n in range(DN):
                    t, c = n // 2, n % 2
                    if n % FT == 0 and t in (0, NT // 2):
                        pe.wait_ge(sem("v_sq_out"), UP * g + 2 + (FT if t == 0 else UP))
                    pe.wait_ge(sem("v_added"), DN * g + n + 1)
                    for j in range(FT):
                        for a, b in PASSES:
                            mm = pe.matmul(ps[:, 2 + n % 4, :], f1[a][:, j, P * t:P * t + P], W[b][:, HALF + 2 * j + c, :],
                                           start=(j == 0 and a == 0 and b == 0), stop=(j == FT - 1 and a == 1))
                    mm.then_inc(sem("v_down"), 1)

            with pe.Fori(0, GRPS) as g:
                group(g, False)

        def where(n):
            return n % FT, slice(512 * (n // FT), 512 * (n // FT) + 512)

        @block.scalar
        def _(act):
            def highs(g):
                for n in range(UP):
                    j, at = where(n)
                    act.wait_ge(sem("v_up"), UP * g + n + 1)
                    act.activation(relu[n % 2][:, :], ps[:, n % 2, :], ACT.Relu).then_inc(sem("v_relu"), 1)
                    act.wait_ge(sem("v_sq"), UP * g + n + 1)
                    act.activation(f1[0][:, j, at], ps[:, n % 2, :], ACT.Copy).then_inc(sem("v_f1hi"), 1)

            with act.Fori(0, GRPS) as g:
                highs(g)
            for t in range(NT):
                act.wait_ge(sem("v_added"), 4 + DN * (GRPS - 1) + 2 * t + 2)
                if t == 0:
                    act.wait_ge(sem("v_up"), UP * GRPS)
                else:
                    act.wait_ge(sem("e_sq"), t)
                act.activation(junk[:, :], acc[:, t, :], ACT.Square, accum_out=ss[:, t:t + 1]).then_inc(sem("e_sq"), 1)
                act.wait_ge(sem("e_v"), t + 1)
                act.activation(s_[:, t:t + 1], v[:, t:t + 1], ACT.Sqrt).then_inc(sem("e_sqrt"), 1)

        @block.vector
        def _(dve):
            for t in range(NT):
                dve.memset(acc[:, t, :], 0.0).then_inc(sem("acc_set"), 1)
            dve.memset(ss[:, :], 0.0).then_inc(sem("v_sq_out"), 2)
            dve.memset(v[:, :], 1.0).then_inc(sem("v_added"), 4)
            dve.wait_ge(sem("acc_set"), NT)

            def squares(g):
                def square(n):
                    dve.wait_ge(sem("v_relu"), UP * g + n + 1)
                    bank = ps[:, n % 2, :]
                    dve.tensor_tensor(bank, bank, relu[n % 2][:, :], ALU.mult).then_inc(sem("v_sq"), 1)

                for n in range(UP):
                    j, at = where(n)
                    square(n)
                    dve.wait_ge(sem("v_f1hi"), UP * g + n + 1)
                    dve.tensor_tensor(f1[1][:, j, at], ps[:, n % 2, :], f1[0][:, j, at].bitcast(F32), ALU.subtract).then_inc(sem("v_sq_out"), 1)

            def add(g, n):
                dve.wait_ge(sem("v_down"), DN * g + n + 1)
                t, c = n // 2, n % 2
                part = acc[:, t, 512 * c:512 * c + 512]
                dve.tensor_tensor(part, ps[:, 2 + n % 4, :], part, ALU.add).then_inc(sem("v_added"), 1)

            with dve.Fori(0, GRPS - 1) as g:
                squares(g)
                for n in range(DN):
                    add(g, n)
            g = GRPS - 1
            squares(g)
            for t in range(NT):
                add(g, 2 * t)
                add(g, 2 * t + 1)
                if t == 0:
                    dve.wait_ge(sem("e_w_in"), 16)
                dve.wait_ge(sem("e_sq"), t + 1)
                rsqrt_before(dve, k, v[:, t:t + 1], ss[:, t:t + 1], 1.0 / D, "e_v", 1)
                rsqrt_after(dve, k, r[:, t:t + 1], v[:, t:t + 1], s_[:, t:t + 1], t1[:, t:t + 1], "e_sqrt", t + 1, "e_rs", 5 * t)
                dve.scalar_tensor_tensor(acc[:, t, :], acc[:, t, :], r[:, t:t + 1], wrow[:, :], ALU.mult, ALU.mult).then_inc(sem("e_scaled"), 1)


def build(nc, io):
    k = setup(nc, io)
    phase_norm(k)
    phase_project(k)
    phase_attend(k)
    k.sem.renew()
    phase_ssd(k)
    phase_mix(k)
    phase_mlp(k)


_INS = ["x", "meta_tokens", "w_in", "w_q_up", "w_kv_up", "dt_bias", "a_log", "d_skip", "ssm_norm", "w_out",
        "norm_mix_post", "w_mlp_up", "w_mlp_down", "norm_mlp_post"]


def _constants():
    inv = np.float32(10000.0) ** (-np.arange(0, ROPE, 2, dtype=np.float32) / np.float32(ROPE))
    ang = np.arange(POS, dtype=np.float32)[:, None] * inv.astype(np.float32)[None, :]
    table = np.concatenate([np.cos(ang), np.sin(ang)], axis=1).astype(np.float32)
    rope = np.zeros((P, NT + 1, ROPE), np.float32)
    rope[:, :NT] = table[META:].reshape(NT, P, ROPE).transpose(1, 0, 2)
    rope[:META, NT] = table[:META]
    i = np.arange(P)
    ahead = i[:, None] <= i[None, :]
    return {
        "c_ident": np.eye(P, dtype=np.float32),
        "c_tri": ahead.astype(np.float32),
        "c_mask": np.where(ahead, 0.0, NEG).astype(np.float32),
        "c_rope": rope,
    }


def _arrays(inputs):
    arrays = {n: np.ascontiguousarray(inputs[n]) for n in _INS}
    columns = lambda a: np.asarray(a).reshape(-1, P).T
    arrays["c_par"] = np.ascontiguousarray(np.concatenate([
        columns(inputs["norm_mix_pre"]), columns(inputs["norm_mlp_pre"]), columns(inputs["q_a_norm"]), columns(inputs["kv_a_norm"]),
        np.asarray(inputs["conv_w"])[0].reshape(4, CONVW // P, P).transpose(2, 1, 0).reshape(P, -1), columns(inputs["conv_b"])], axis=1))
    return {**arrays, **_constants()}


def _declare(nc, arrays):
    io = {n: nc.dram_tensor(n, a.shape, mybir.dt.from_np(a.dtype), kind="ExternalInput").ap() for n, a in arrays.items()}
    io["out"] = nc.dram_tensor("out", (1, SEQ, D), F32, kind="ExternalOutput").ap()
    return io


def kernel(**inputs):
    import concourse.bacc as bacc
    from concourse.bass_utils import run_bass_kernel_spmd

    arrays = _arrays(inputs)
    nc = bacc.Bacc("TRN2", target_bir_lowering=False, num_devices=1)
    build(nc, _declare(nc, arrays))
    r = run_bass_kernel_spmd(nc, [arrays], core_ids=[0])
    return r.results[0]["out"]
```

```python
import numpy as np

import concourse.bass as bass
from concourse import mybir

F32 = mybir.dt.float32
F32R = mybir.dt.float32r
BF16 = mybir.dt.bfloat16
ALU = mybir.AluOpType
ACT = mybir.ActivationFunctionType
AX = mybir.AxisListType

P = 128
D = 1024
SEQ = 1024
META = 16
POS = SEQ + META
KD = D // P
NT = SEQ // P
QL, KVL, ROPE, NOPE, VH = 384, 256, 64, 128, 128
HEADS = 8
SSMW, GROUPS, STATE, SH, SHD = 1024, 2, 128, 16, 64
CONVW = SSMW + 2 * GROUPS * STATE
DFF = 4096
OFF_KV, OFF_KR, OFF_Z, OFF_X, OFF_DT = QL, QL + KVL, QL + KVL + ROPE, QL + KVL + ROPE + SSMW, QL + KVL + ROPE + SSMW + CONVW
SCALE = float((NOPE + ROPE) ** -0.5)
EPS = 1e-6
NEG = -1.0e30
TC = [(0, 348), (348, 346), (694, 346)]
RING = 16
STAGES = 4


class Sems:

    def __init__(self, nc):
        self.nc, self.of = nc, {}

    def __call__(self, name):
        if name not in self.of:
            self.of[name] = self.nc.alloc_semaphore(name)
        return self.of[name]

    def renew(self):
        self.nc.clear_and_free_semaphores(list(self.of.values()))
        self.of = {}
        self.nc.all_engine_barrier()


class Map:

    def __init__(self, nc):
        self.nc, self.base = nc, (nc.sbuf_base + 31) // 32 * 32

    def at(self, name, shape, dt, offset):
        size = (int(np.prod(shape[1:])) * mybir.dt.size(dt) + 31) // 32 * 32
        assert self.base + offset + size <= self.nc.sbuf_usable_end, (name, offset, size)
        return self.nc.alloc_sbuf_tensor_at(name, list(shape), dt, offset=self.base + offset), offset + size


PARAM = {}
_at = 0
for _n, _w in (("pre", KD), ("mlp", KD), ("qa", QL // P), ("kva", KVL // P), ("convw", 4 * CONVW // P), ("convb", CONVW // P)):
    PARAM[_n] = _at
    _at += _w
NPARAM = _at

O_RING = 6144
O_STAGE = O_RING + RING * 512 * 8
O_R = O_STAGE + STAGES * 512 * 4
O_DT = 212256
O_TABLES = O_DT - 7744


class K:
    pass


def setup(nc, io):
    k = K()
    k.nc, k.io, k.sem, m = nc, io, Sems(nc), Map(nc)
    k.map = m
    o = 0
    k.ident, o = m.at("ident", [P, P], F32, o)
    k.ident_b, o = m.at("ident_b", [P, P], BF16, o)
    k.mask_b, o = m.at("mask_b", [P, P], BF16, o)
    k.tri, o = m.at("tri", [P, P], F32R, o)
    k.ones, o = m.at("ones", [P, P], F32R, o)
    k.par, o = m.at("par", [P, NPARAM], F32, o)
    k.st = []
    for n in range(6):
        t, o = m.at(f"stat{n}", [P, 24], F32, o)
        k.st.append(t)
    k.zero, o = m.at("zero", [P, 8], F32, o)
    k.spare, o = m.at("spare", [P, 512], F32, o)
    assert o <= O_RING
    k.whi, o = m.at("whi", [P, RING, 512], F32R, O_RING)
    k.wlo, o = m.at("wlo", [P, RING, 512], F32R, o)
    k.stage, o = m.at("stage", [P, STAGES, 512], F32, O_STAGE)
    k.ps = nc.alloc_psum_tensor("ps", [P, 8, 512], F32)
    dr = lambda n, s, dt: nc.dram_tensor(n, s, dt, kind="Internal").ap()
    k.d_x = dr("d_x", (SEQ, SSMW), F32)
    k.d_xm = dr("d_xm", (META, SSMW), F32)
    k.d_z = dr("d_z", (SEQ, SSMW), F32)
    pair = lambda n, s: [dr(n + "hi", s, F32), dr(n + "lo", s, F32)]
    k.d_bt = pair("d_bt", (GROUPS * STATE, SEQ))
    k.d_ct = pair("d_ct", (GROUPS * STATE, SEQ))
    k.d_b = pair("d_b", (SEQ, GROUPS * STATE))
    k.d_bm = pair("d_bm", (META, GROUPS * STATE))
    k.d_qr = pair("d_qr", (HEADS * ROPE, SEQ))
    k.d_att = pair("d_att", (HEADS * VH, SEQ))
    k.d_ssm = pair("d_ssm", (SSMW, SEQ))
    k.d_mix = dr("d_mix", (SEQ, D), F32)
    k.d_h = dr("d_h", (SEQ, D), F32)
    k.blocks = []
    k.fam = "w"
    return k


def col(k, name, n):
    return k.par[:, PARAM[name] + n:PARAM[name] + n + 1]



def load_block(sp, k, n, src, base=0, turn=0):
    if n >= STAGES:
        sp.wait_ge(k.sem(k.fam + "_cut"), n - STAGES + 1 + turn)
    width = src.shape[-1]
    sp.dma_start(k.stage[:, n % STAGES, 0:width], src).then_inc(k.sem(f"{k.fam}_landed{n % STAGES}"), 16)


def cut_block(pool, k, n, width, turn=0, by_stages=0):
    pool.wait_ge(k.sem(f"{k.fam}_landed{n % STAGES}"), 16 * (n // STAGES + 1) + by_stages)
    src = k.stage[:, n % STAGES, 0:width]
    hi, lo = k.whi[:, n % RING, 0:width], k.wlo[:, n % RING, 0:width]
    pool.tensor_tensor(hi, src, k.zero[:, 0:1].broadcast_to([P, width]), ALU.add).then_inc(k.sem(k.fam + "_hi"), 1)
    pool.wait_ge(k.sem(k.fam + "_hi"), n + 1 + turn)
    pool.tensor_tensor(lo, src, hi.bitcast(F32), ALU.subtract).then_inc(k.sem(k.fam + "_cut"), 1)


def cut_hi(act, k, n):
    act.wait_ge(k.sem(f"{k.fam}_landed{n % STAGES}"), 16 * (n // STAGES + 1))
    act.activation(k.whi[:, n % RING, :], k.stage[:, n % STAGES, :], ACT.Copy).then_inc(k.sem(k.fam + "_hi"), 1)


def cut_lo(dve, k, n):
    dve.wait_ge(k.sem(k.fam + "_hi"), n + 1)
    dve.tensor_tensor(k.wlo[:, n % RING, :], k.stage[:, n % STAGES, :], k.whi[:, n % RING, :].bitcast(F32), ALU.subtract).then_inc(k.sem(k.fam + "_cut"), 1)


def mm3(pe, out, l, r, first, last):
    pe.matmul(out, l[0], r[0], start=first, stop=False)
    pe.matmul(out, l[0], r[1], start=False, stop=False)
    return pe.matmul(out, l[1], r[0], start=False, stop=last)



def phase_norm(k):
    nc, sem, m, ps, io = k.nc, k.sem, k.map, k.ps, k.io
    k.hT = []
    o = O_R
    for s in ("hi", "lo"):
        t, o = m.at("hT" + s, [P, KD, POS], F32R, o)
        k.hT.append(t)
    k.o_work = o
    xt, o = m.at("xt", [P, NT + 1, D], F32, o)
    cst, o = m.at("cst", [P, 2, P], F32, o)
    mtmp, o = m.at("mtmp", [P, KD, META], F32, o)
    ss, v, s_, r, t1 = k.st[0], k.st[1], k.st[2], k.st[3], k.st[4]
    hT = k.hT
    win = io["w_in"][0]
    wqu = io["w_q_up"][0]
    cols = [(OFF_X, 512), (OFF_X + 512, 512), (OFF_X + 1024, 512), (OFF_Z, 512), (OFF_Z + 512, 512), (0, QL), (OFF_KV, KVL + ROPE)]
    k.blocks = [win[P * kk:P * kk + P, c:c + w] for c, w in cols for kk in range(KD)]
    qr_view = wqu.rearrange("k (h c) -> k h c", h=HEADS)[:, :, NOPE:NOPE + ROPE]
    k.qr_blocks = [qr_view[P * kk:P * kk + P] for kk in range(QL // P)]

    with nc.Block() as block:
        @block.sync
        def _(sp):
            sp.dma_start(k.ident[:, :], io["c_ident"]).then_inc(sem("c_in"), 16)
            sp.dma_start(cst[:, 0, :], io["c_tri"]).then_inc(sem("c_in"), 16)
            sp.dma_start(cst[:, 1, :], io["c_mask"]).then_inc(sem("c_in"), 16)
            sp.dma_start(k.par[:, :], io["c_par"]).then_inc(sem("c_in"), 16)
            for t in range(NT):
                sp.dma_start(xt[:, t, :], io["x"][0, P * t:P * t + P, :]).then_inc(sem(f"x_in{t}"), 16)
            sp.dma_start(xt[0:META, NT, :], io["meta_tokens"]).then_inc(sem(f"x_in{NT}"), 16)
            for n in range(RING):
                load_block(sp, k, n, k.blocks[n])

        @block.gpsimd
        def _(pool):
            pool.memset(k.zero[:, :], 0.0).then_inc(sem("zeroed"), 1)
            pool.wait_ge(sem("zeroed"), 1)
            for n in range(RING):
                cut_block(pool, k, n, k.blocks[n].shape[-1])

        @block.scalar
        def _(act):
            for t in range(NT + 1):
                rows = P if t < NT else META
                act.wait_ge(sem(f"x_in{t}"), 16)
                if t == 0:
                    act.wait_ge(sem("ss_set"), 1)
                if t >= 1:
                    act.wait_ge(sem("sq"), t)
                act.activation(ps[0:rows, 6:8, :].rearrange("p a b -> p (a b)"), xt[0:rows, t, :], ACT.Square,
                               accum_out=ss[0:rows, t:t + 1]).then_inc(sem("sq"), 1)
            act.wait_ge(sem("v"), 1)
            act.activation(s_[:, 0:9], v[:, 0:9], ACT.Sqrt).then_inc(sem("sqrt"), 1)
            act.wait_ge(sem("c_in"), 64)
            for n in range(2 * KD):
                kk, half = n // 2, n % 2
                act.wait_ge(sem("turned"), n + 1)
                c0 = META + 512 * half
                act.activation(hT[0][:, kk, c0:c0 + 512], ps[:, n % 4, :], ACT.Copy, scale=col(k, "pre", kk)).then_inc(sem("t_hi"), 1)
            act.wait_ge(sem("mt"), 1)
            act.activation(hT[0][:, :, 0:META], mtmp[:, :, :], ACT.Copy).then_inc(sem("t_hi"), 1)

        @block.vector
        def _(dve):
            dve.memset(ss[:, :], 1.0).then_inc(sem("ss_set"), 1)
            dve.wait_ge(sem("c_in"), 64)
            dve.tensor_copy(k.ident_b[:, :], k.ident[:, :]).then_inc(sem("consts"), 1)
            dve.tensor_copy(k.mask_b[:, :], cst[:, 1, :]).then_inc(sem("consts"), 1)
            dve.tensor_copy(k.tri[:, :], cst[:, 0, :]).then_inc(sem("consts"), 1)
            dve.tensor_scalar(k.ones[:, :], cst[:, 0, :], 0.0, 1.0, ALU.mult, ALU.add).then_inc(sem("consts"), 1)
            dve.wait_ge(sem("sq"), NT + 1)
            rsqrt_before(dve, k, v[:, 0:9], ss[:, 0:9], 1.0 / D, "v", 1)
            rsqrt_after(dve, k, r[:, 0:9], v[:, 0:9], s_[:, 0:9], t1[:, 0:9], "sqrt", 1, "rs1")
            for t in range(NT + 1):
                rows = P if t < NT else META
                dve.tensor_scalar(xt[0:rows, t, :], xt[0:rows, t, :], r[0:rows, t:t + 1], None, ALU.mult).then_inc(sem("xn"), 1)
            for n in range(2 * KD):
                kk, half = n // 2, n % 2
                dve.wait_ge(sem("t_hi"), n + 1)
                c0 = META + 512 * half
                dve.scalar_tensor_tensor(hT[1][:, kk, c0:c0 + 512], ps[:, n % 4, :], col(k, "pre", kk), hT[0][:, kk, c0:c0 + 512].bitcast(F32),
                                         ALU.mult, ALU.subtract).then_inc(sem("t_lo"), 1)
            dve.wait_ge(sem("turned"), 2 * KD + 1)
            w = k.par[:, PARAM["pre"]:PARAM["pre"] + KD].unsqueeze(2).broadcast_to([P, KD, META])
            dve.tensor_tensor(mtmp[:, :, :], ps[:, 0, 0:P].rearrange("p (a b) -> p a b", a=KD), w, ALU.mult).then_inc(sem("mt"), 1)
            dve.wait_ge(sem("t_hi"), 2 * KD + 1)
            dve.wait_ge(sem("mt"), 1)
            dve.tensor_tensor(hT[1][:, :, 0:META], mtmp[:, :, :], hT[0][:, :, 0:META].bitcast(F32), ALU.subtract).then_inc(sem("t_lo"), 1)

        @block.tensor
        def _(pe):
            pe.wait_ge(sem("c_in"), 64)
            for n in range(2 * KD):
                kk, half = n // 2, n % 2
                pe.wait_ge(sem("xn"), 4 * half + 4)
                if n >= 4:
                    pe.wait_ge(sem("t_lo"), n - 3)
                for i in range(4):
                    mm = pe.transpose(ps[:, n % 4, P * i:P * i + P], xt[:, 4 * half + i, P * kk:P * kk + P], k.ident[:, :])
                mm.then_inc(sem("turned"), 1)
            pe.wait_ge(sem("xn"), NT + 1)
            pe.wait_ge(sem("t_lo"), 2 * KD - 3)
            for kk in range(KD):
                mm = pe.transpose(ps[:, 0, META * kk:META * kk + META], xt[0:META, NT, P * kk:P * kk + P], k.ident[0:META, 0:META])
            mm.then_inc(sem("turned"), 1)


def rsqrt_before(dve, k, v, ss, scale, name, count):
    dve.tensor_scalar(v, ss, scale, EPS, ALU.mult, ALU.add).then_inc(k.sem(name), 1)


def rsqrt_after(dve, k, r, v, s, t, name, count, own, base=0):
    c = k.sem(own)
    dve.wait_ge(k.sem(name), count)
    dve.reciprocal(r, s).then_inc(c, 1)
    dve.wait_ge(c, base + 1)
    dve.tensor_tensor(t, r, r, ALU.mult).then_inc(c, 1)
    dve.wait_ge(c, base + 2)
    dve.tensor_tensor(t, t, v, ALU.mult).then_inc(c, 1)
    dve.wait_ge(c, base + 3)
    dve.tensor_scalar(t, t, -0.5, 1.5, ALU.mult, ALU.add).then_inc(c, 1)
    dve.wait_ge(c, base + 4)
    dve.tensor_tensor(r, r, t, ALU.mult).then_inc(c, 1)
    dve.wait_ge(c, base + 5)



NX = CONVW // P
NXT = NX - GROUPS


def phase_project(k):
    nc, sem, m, ps, io, hT = k.nc, k.sem, k.map, k.ps, k.io, k.hT
    o = k.o_work
    pre, o = m.at("pre", [P, 2, POS + 4], F32, o)
    acc, o = m.at("conv_acc", [P, 2, POS], F32, o)
    xc, o = m.at("xc", [P, 2, POS], F32, o)
    o1 = o
    xt, o = m.at("x_tok", [P, 2, NT + 1, P], F32, o)
    fb, o = [], o
    for s in ("hi", "lo"):
        t, o = m.at("bc" + s, [P, SEQ], F32R, o)
        fb.append(t)
    zs, o = m.at("zs", [P, 4, 512], F32, o)
    o_top = o
    bt = []
    for s in ("hi", "lo"):
        t, o = m.at("btok" + s, [P, NT + 1, P], F32R, o)
        bt.append(t)
    oc = k.o_work
    cqs, oc = m.at("cqs", [P, NT, QL], F32, oc)
    cks, oc = m.at("cks", [P, NT + 1, KVL + ROPE], F32, oc)
    assert oc <= o1
    oc = o1
    kro, oc = m.at("kro", [P, NT + 1, P], F32, oc)
    ta, oc = m.at("rot_a", [P, 288], F32, oc)
    tb, oc = m.at("rot_b", [P, 288], F32, oc)
    junk, oc = m.at("junk", [P, QL], F32, oc)
    assert oc <= o_top
    rope, o = m.at("rope", [P, NT + 1, ROPE], F32, o)
    wdt, o = m.at("wdt", [P, KD, SH], F32, o)
    wd = []
    for s in ("hi", "lo"):
        t, o = m.at("wdt" + s, [P, KD, SH], F32R, o)
        wd.append(t)
    k.dt_at = m.base + O_DT
    assert o <= O_DT
    o = O_DT
    k.dt, o = m.at("dt", [P, NT + 1, SH], F32, o)
    oh = O_R
    k.cqT, k.ckT, k.krT, k.qrT = [], [], [], []
    for lst, name, shape in ((k.cqT, "cqT", [P, QL // P, SEQ]), (k.ckT, "ckT", [P, KVL // P, POS]), (k.krT, "krT", [P, POS])):
        for s in ("hi", "lo"):
            t, oh = m.at(name + s, shape, F32R, oh)
            lst.append(t)
    k.o_lat = oh
    mt, oh = m.at("mtmp2", [P, 3, META], F32, oh)
    qro, oh = m.at("qro", [P, HEADS, ROPE], F32, oh)
    for s in ("hi", "lo"):
        t, oh = m.at("qrT" + s, [P, 4, P], F32R, oh)
        k.qrT.append(t)
    assert oh <= k.o_work
    ss, v, s_, r, t1 = k.st[0], k.st[1], k.st[2], k.st[3], k.st[4]
    nb = len(k.blocks)
    W = (k.whi, k.wlo)
    PASSES = ((0, 0), (0, 1), (1, 0))
    NW = NT + NT + 1
    KQ, KK = QL // P, KVL // P

    def chunk_used(eng, c):
        if c < 3:
            eng.wait_ge(sem("x_done"), 4 * c + 4)
        elif c < 5:
            eng.wait_ge(sem("z_done"), NT * (c - 2))
        elif c == 5:
            eng.wait_ge(sem("cq_done"), NT)
        elif c == 6:
            eng.wait_ge(sem("ck_done"), NT + 1)

    with nc.Block() as block:
        @block.sync
        def _(sp):
            sp.dma_start(rope[:, :, :], io["c_rope"]).then_inc(sem("rope_in"), 16)
            sp.dma_start(wdt[:, :, :], io["w_in"][0, :, OFF_DT:OFF_DT + SH].rearrange("(k p) n -> p k n", p=P)).then_inc(sem("wdt_in"), 16)
            loaded = [RING]

            def loads(until):
                for n in range(loaded[0], until):
                    if n < nb:
                        load_block(sp, k, n, k.blocks[n])
                    else:
                        sp.wait_ge(sem("w_cut"), n - STAGES + 1)
                        sp.dma_start(k.stage[:, n % STAGES, :].rearrange("p (h c) -> p h c", h=HEADS),
                                     k.qr_blocks[n - nb]).then_inc(sem(f"w_landed{n % STAGES}"), 16)
                loaded[0] = until

            loads(RING + STAGES)
            for f in range(NX):
                q = f - 2
                if 0 <= q < NXT:
                    sp.wait_ge(sem("xt1_out"), q + 1)
                    sp.wait_ge(sem("xt2_out"), q + 1)
                if 0 <= q < KD:
                    sent = sem(f"xt_sent{q % 2}")
                    sp.dma_start(k.d_x[:, P * q:P * q + P].rearrange("(t p) n -> p t n", p=P), xt[:, q % 2, 0:NT, :]).then_inc(sent, 16)
                    sp.dma_start(k.d_xm[:, P * q:P * q + P], xt[0:META, q % 2, NT, :]).then_inc(sent, 16)
                elif 0 <= q < NXT:
                    g = q - KD
                    for i in range(2):
                        sp.dma_start(k.d_b[i][:, P * g:P * g + P].rearrange("(t p) n -> p t n", p=P),
                                     bt[i][:, 0:NT, :].bitcast(F32)).then_inc(sem("bt_sent"), 16)
                        sp.dma_start(k.d_bm[i][:, P * g:P * g + P], bt[i][0:META, NT, :].bitcast(F32)).then_inc(sem("bt_sent"), 16)
                if f >= KD:
                    sp.wait_ge(sem("bc_lo"), f - KD + 1)
                    d = k.d_bt if f < KD + GROUPS else k.d_ct
                    g = (f - KD) % GROUPS
                    for i in range(2):
                        sp.dma_start(d[i][P * g:P * g + P, :], fb[i][:, :].bitcast(F32)).then_inc(sem("bc_sent"), 16)
                if f in (4, 8, NX - 1):
                    loads(loaded[0] + 8)
            for g in range(2 * NT):
                c, t = g // NT, g % NT
                sp.wait_ge(sem("zs_done"), g + 1)
                sp.dma_start(k.d_z[P * t:P * t + P, 512 * c:512 * c + 512], zs[:, g % 4, :]).then_inc(sem(f"z_sent{g % 4}"), 16)
                if g == NT:
                    loads(loaded[0] + 8)
            loads(nb + KQ)
            for t in range(NT):
                sp.wait_ge(sem("qrT_lo"), t + 1)
                for i in range(2):
                    sp.dma_start(k.d_qr[i][:, P * t:P * t + P].rearrange("(a p) n -> p a n", p=P),
                                 k.qrT[i][:, :, :].bitcast(F32)).then_inc(sem("qr_sent"), 16)
            for q in range(4):
                sp.wait_ge(sem(f"z_sent{q}"), 16 * 4)
            sp.wait_ge(sem("bt_sent"), 64 * GROUPS)
            sp.wait_ge(sem("bc_sent"), 32 * 2 * GROUPS)
            sp.wait_ge(sem("qr_sent"), 32 * NT)

        @block.gpsimd
        def _(pool):
            for n in range(RING, nb + KQ):
                if n % 8 == 0:
                    chunk_used(pool, n // 8 - 2)
                cut_block(pool, k, n, k.blocks[n].shape[-1] if n < nb else 512)

        @block.tensor
        def _(pe):
            def turn_x(f, parts):
                pe.wait_ge(sem("xc_done"), f + 1)
                for part in parts:
                    bank = (6, 7, 6)[part]
                    if part == 0 and f:
                        pe.wait_ge(sem("xt2_out"), f)
                    if part == 1 and f:
                        pe.wait_ge(sem("xt1_out"), f)
                    if part == 2:
                        pe.wait_ge(sem("xt0_out"), f + 1)
                        mm = pe.transpose(ps[:, 6, 0:P], xc[:, f % 2, 0:P], k.ident[:, :])
                    else:
                        for i in range(4):
                            c0 = META + P * (4 * part + i)
                            mm = pe.transpose(ps[:, bank, P * i:P * i + P], xc[:, f % 2, c0:c0 + P], k.ident[:, :])
                    mm.then_inc(sem("x_turned"), 1)

            for f in range(NX):
                c, j = f // 4, f % 4
                base = 3 * (f % 2)
                if f >= 2:
                    pe.wait_ge(sem("pre_out"), 3 * (f - 1))
                for kk in range(KD):
                    if kk == 2 and 2 <= f <= NXT + 1:
                        turn_x(f - 2, (2,))
                    if j == 0:
                        pe.wait_ge(sem("w_cut"), 8 * c + kk + 1)
                    for a, b in PASSES:
                        for q, (c0, w) in enumerate(TC):
                            mm = pe.matmul(ps[:, base + q, 0:w], W[a][:, (8 * c + kk) % RING, P * j:P * j + P], hT[b][:, kk, c0:c0 + w],
                                           start=(kk == 0 and (a, b) == (0, 0)), stop=(kk == KD - 1 and a == 1))
                mm.then_inc(sem("x_done"), 1)
                if 1 <= f <= NXT:
                    turn_x(f - 1, (0, 1))
            for c in (3, 4):
                for t in range(NT):
                    g = NT * (c - 3) + t
                    if g < 4:
                        pe.wait_ge(sem("pre_out"), 3 * NX)
                    else:
                        pe.wait_ge(sem("zs_done"), g - 3)
                    for kk in range(KD):
                        if t == 0:
                            pe.wait_ge(sem("w_cut"), 8 * c + kk + 1)
                        for a, b in PASSES:
                            mm = pe.matmul(ps[:, g % 4, :], hT[a][:, kk, META + P * t:META + P * t + P], W[b][:, (8 * c + kk) % RING, :],
                                           start=(kk == 0 and (a, b) == (0, 0)), stop=(kk == KD - 1 and a == 1))
                    mm.then_inc(sem("z_done"), 1)
            for t in range(NT):
                if t < 4:
                    pe.wait_ge(sem("zs_done"), 2 * NT - 3 + t)
                else:
                    pe.wait_ge(sem("cq_out"), t - 3)
                for kk in range(KD):
                    if t == 0:
                        pe.wait_ge(sem("w_cut"), 40 + kk + 1)
                    for a, b in PASSES:
                        mm = pe.matmul(ps[:, t % 4, 0:QL], hT[a][:, kk, META + P * t:META + P * t + P], W[b][:, (40 + kk) % RING, 0:QL],
                                       start=(kk == 0 and (a, b) == (0, 0)), stop=(kk == KD - 1 and a == 1))
                mm.then_inc(sem("cq_done"), 1)
            pe.wait_ge(sem("wdt_cut"), 2)
            for t in range(NT + 1):
                if t < 4:
                    pe.wait_ge(sem("cq_out"), NT - 3 + t)
                else:
                    pe.wait_ge(sem("ck_out"), t - 3)
                c0 = META + P * t if t < NT else 0
                for part, w in ((0, KVL + ROPE), (1, SH)):
                    for kk in range(KD):
                        if t == 0:
                            pe.wait_ge(sem("w_cut"), 48 + kk + 1)
                        for a, b in PASSES:
                            rhs = W[b][:, (48 + kk) % RING, 0:w] if part == 0 else wd[b][:, kk, :]
                            mm = pe.matmul(ps[:, t % 4, (KVL + ROPE) * part:(KVL + ROPE) * part + w], hT[a][:, kk, c0:c0 + P], rhs,
                                           start=(kk == 0 and (a, b) == (0, 0)), stop=(kk == KD - 1 and a == 1))
                mm.then_inc(sem("ck_done"), 1)
            pe.wait_ge(sem("xt2_out"), NXT)
            for n in range(13):
                bank = 4 + n % 4
                if n >= 4:
                    pe.wait_ge(sem("lat_lo"), n - 3)
                if n < 6:
                    pe.wait_ge(sem("cq_scaled"), NT)
                elif n < 10:
                    pe.wait_ge(sem("ck_scaled"), NT + 1)
                else:
                    pe.wait_ge(sem("kro_done"), 2)
                half = n % 2
                if n < 12:
                    for i in range(4):
                        t = 4 * half + i
                        if n < 6:
                            src = cqs[:, t, P * (n // 2):P * (n // 2) + P]
                        elif n < 10:
                            kk = (n - 6) // 2
                            src = cks[:, t, P * kk:P * kk + P]
                        else:
                            src = kro[:, t, :]
                        mm = pe.transpose(ps[:, bank, P * i:P * i + P], src, k.ident[:, :])
                else:
                    for i in range(3):
                        src = cks[0:META, NT, P * i:P * i + P] if i < 2 else kro[0:META, NT, :]
                        mm = pe.transpose(ps[:, bank, META * i:META * i + META], src, k.ident[0:META, 0:META])
                mm.then_inc(sem("lat_turned"), 1)
            def turn_qr(t):
                pe.wait_ge(sem("qro_done"), 2 * t + 2)
                if t < 2:
                    pe.wait_ge(sem("lat_lo"), 13)
                else:
                    pe.wait_ge(sem("qrT_lo"), t - 1)
                for i in range(4):
                    mm = pe.transpose(ps[:, 4 + t % 2, P * i:P * i + P], qro[:, 2 * i:2 * i + 2, :].rearrange("p a b -> p (a b)"), k.ident[:, :])
                mm.then_inc(sem("qr_turned"), 1)

            pe.wait_ge(sem("lat_lo"), 13)
            for t in range(NT):
                if t < 4:
                    pe.wait_ge(sem("ck_out"), NT + 1)
                else:
                    pe.wait_ge(sem("qro_done"), 2 * (t - 3))
                for kk in range(KQ):
                    if t == 0:
                        pe.wait_ge(sem("w_cut"), nb + kk + 1)
                    for a, b in PASSES:
                        mm = pe.matmul(ps[:, t % 4, :], k.cqT[a][:, kk, P * t:P * t + P], W[b][:, (nb + kk) % RING, :],
                                       start=(kk == 0 and (a, b) == (0, 0)), stop=(kk == KQ - 1 and a == 1))
                mm.then_inc(sem("qr_done"), 1)
                if t:
                    turn_qr(t - 1)
            turn_qr(NT - 1)

        @block.scalar
        def _(act):
            def out_x(f, part):
                act.wait_ge(sem("x_turned"), 3 * f + part + 1)
                src = ps[:, 6, :].rearrange("p (a b) -> p a b", b=P) if part == 0 else ps[0:META, 6, 0:P]
                if f < KD:
                    if part == 0 and f >= 2:
                        act.wait_ge(sem(f"xt_sent{f % 2}"), 32 * (f // 2))
                    dst = xt[:, f % 2, 0:4, :] if part == 0 else xt[0:META, f % 2, NT, :]
                    act.activation(dst, src, ACT.Copy).then_inc(sem(f"xt{part}_out"), 1)
                else:
                    if part == 0 and f > KD:
                        act.wait_ge(sem("bt_sent"), 64 * (f - KD))
                    dst = bt[0][:, 0:4, :] if part == 0 else bt[0][0:META, NT, :]
                    act.activation(dst, src, ACT.Copy).then_inc(sem("bt_hi"), 1)
                    if part == 0:
                        act.wait_ge(sem("x_turned"), 3 * f + 2)
                        act.activation(bt[0][:, 4:8, :], ps[:, 7, :].rearrange("p (a b) -> p a b", b=P), ACT.Copy).then_inc(sem("bt_hi"), 1)

            for f in range(NX):
                act.wait_ge(sem("x_done"), f + 1)
                if f >= 2:
                    act.wait_ge(sem("conv_done"), f - 1)
                for q, (c0, w) in enumerate(TC):
                    act.activation(pre[:, f % 2, 4 + c0:4 + c0 + w], ps[:, 3 * (f % 2) + q, 0:w], ACT.Copy).then_inc(sem("pre_out"), 1)
                if 2 <= f <= NXT + 1:
                    out_x(f - 2, 2)
                if 1 <= f <= NXT:
                    out_x(f - 1, 0)
                act.wait_ge(sem("conv_done"), f + 1)
                if f >= 2:
                    if f - 2 < NXT:
                        act.wait_ge(sem("x_turned"), 3 * (f - 1))
                    if f - 2 >= KD:
                        act.wait_ge(sem("bc_lo"), f - 1 - KD)
                act.activation(xc[:, f % 2, :], acc[:, f % 2, :], ACT.Silu, bias=col(k, "convb", f)).then_inc(sem("xc_done"), 1)
                if f >= KD:
                    act.wait_ge(sem("xc_done"), f + 1)
                    if f > KD:
                        act.wait_ge(sem("bc_sent"), 32 * (f - KD))
                    act.activation(fb[0][:, :], xc[:, f % 2, META:POS], ACT.Copy).then_inc(sem("bc_hi"), 1)
            for g in range(2 * NT):
                act.wait_ge(sem("z_done"), g + 1)
                if g >= 4:
                    act.wait_ge(sem(f"z_sent{g % 4}"), 16 * (g // 4))
                act.activation(zs[:, g % 4, :], ps[:, g % 4, :], ACT.Silu).then_inc(sem("zs_done"), 1)
            act.wait_ge(sem("stat_set"), 1)
            for t in range(NW):
                if t < NT:
                    act.wait_ge(sem("cq_out"), t + 1)
                    rows, src = P, cqs[:, t, :]
                else:
                    act.wait_ge(sem("ck_out"), t - NT + 1)
                    rows = P if t < NW - 1 else META
                    src = cks[0:rows, t - NT, 0:KVL]
                if t:
                    act.wait_ge(sem("lat_sq"), t)
                act.activation(junk[0:rows, 0:src.shape[-1]], src, ACT.Square, accum_out=ss[0:rows, t:t + 1]).then_inc(sem("lat_sq"), 1)
            act.wait_ge(sem("lat_v"), 2)
            act.activation(s_[:, 0:NW], v[:, 0:NW], ACT.Sqrt).then_inc(sem("lat_sqrt"), 1)
            for n in range(13):
                act.wait_ge(sem("lat_turned"), n + 1)
                c0 = 512 * (n % 2)
                src = ps[:, 4 + n % 4, :]
                if n < 6:
                    act.activation(k.cqT[0][:, n // 2, c0:c0 + 512], src, ACT.Copy, scale=col(k, "qa", n // 2)).then_inc(sem("lat_hi"), 1)
                elif n < 10:
                    kk = (n - 6) // 2
                    act.activation(k.ckT[0][:, kk, META + c0:META + c0 + 512], src, ACT.Copy, scale=col(k, "kva", kk)).then_inc(sem("lat_hi"), 1)
                elif n < 12:
                    act.activation(k.krT[0][:, META + c0:META + c0 + 512], src, ACT.Copy).then_inc(sem("lat_hi"), 1)
                else:
                    act.wait_ge(sem("lat_mt"), 2)
                    act.activation(k.ckT[0][:, :, 0:META], mt[:, 0:2, :], ACT.Copy).then_inc(sem("lat_hi"), 1)
                    act.activation(k.krT[0][:, 0:META], mt[:, 2, :], ACT.Copy).then_inc(sem("lat_hi"), 1)
            for t in range(NT):
                act.wait_ge(sem("qr_turned"), t + 1)
                if t:
                    act.wait_ge(sem("qr_sent"), 32 * t)
                act.activation(k.qrT[0][:, :, :], ps[:, 4 + t % 2, :].rearrange("p (a b) -> p a b", b=P), ACT.Copy).then_inc(sem("qrT_hi"), 1)

        @block.vector
        def _(dve):
            dve.memset(pre[:, :, 0:4], 0.0).then_inc(sem("pad_set"), 1)
            dve.wait_ge(sem("wdt_in"), 16)
            dve.tensor_copy(wd[0][:, :, :], wdt[:, :, :]).then_inc(sem("wdt_cut"), 1)
            dve.wait_ge(sem("wdt_cut"), 1)
            dve.tensor_tensor(wd[1][:, :, :], wdt[:, :, :], wd[0][:, :, :].bitcast(F32), ALU.subtract).then_inc(sem("wdt_cut"), 1)
            dve.memset(ss[:, :], 1.0).then_inc(sem("stat_set"), 1)

            def out_x(f, parts):
                if f < KD and 1 in parts:
                    dve.wait_ge(sem("x_turned"), 3 * f + 2)
                    if f >= 2:
                        dve.wait_ge(sem(f"xt_sent{f % 2}"), 32 * (f // 2))
                    dve.tensor_copy(xt[:, f % 2, 4:8, :], ps[:, 7, :].rearrange("p (a b) -> p a b", b=P)).then_inc(sem("xt1_out"), 1)
                for part in parts:
                    if f < KD:
                        continue
                    name = ("xt0_out", "xt1_out", "xt2_out")[part]
                    dve.wait_ge(sem("bt_hi"), 3 * (f - KD) + part + 1)
                    if part == 0 and f > KD:
                        dve.wait_ge(sem("bt_sent"), 64 * (f - KD))
                    if part < 2:
                        src = ps[:, 6 + part, :].rearrange("p (a b) -> p a b", b=P)
                        hi, lo = (x[:, 4 * part:4 * part + 4, :] for x in bt)
                    else:
                        src = ps[0:META, 6, 0:P]
                        hi, lo = (x[0:META, NT, :] for x in bt)
                    dve.tensor_tensor(lo, src, hi.bitcast(F32), ALU.subtract).then_inc(sem(name), 1)

            for f in range(NX):
                if 2 <= f <= NXT + 1:
                    out_x(f - 2, (2,))
                if 1 <= f <= NXT:
                    out_x(f - 1, (0, 1))
                dve.wait_ge(sem("pre_out"), 3 * f + 3)
                if f == 0:
                    dve.wait_ge(sem("pad_set"), 1)
                if f >= 2:
                    dve.wait_ge(sem("xc_done"), f - 1)
                a = acc[:, f % 2, :]
                for i in range(4):
                    w = col(k, "convw", 4 * f + i)
                    src = pre[:, f % 2, 1 + i:1 + i + POS]
                    if i == 0:
                        dve.tensor_scalar(a, src, w, None, ALU.mult).then_inc(sem("conv_step"), 1)
                    else:
                        dve.wait_ge(sem("conv_step"), 3 * f + i)
                        mm = dve.scalar_tensor_tensor(a, src, w, a, ALU.mult, ALU.add)
                        mm.then_inc(sem("conv_done" if i == 3 else "conv_step"), 1)
                if f >= KD:
                    dve.wait_ge(sem("bc_hi"), f - KD + 1)
                    if f > KD:
                        dve.wait_ge(sem("bc_sent"), 32 * (f - KD))
                    dve.tensor_tensor(fb[1][:, :], xc[:, f % 2, META:POS], fb[0][:, :].bitcast(F32), ALU.subtract).then_inc(sem("bc_lo"), 1)
            dve.wait_ge(sem("xc_done"), NX)
            dve.wait_ge(sem("bc_lo"), NX - KD)
            dve.wait_ge(sem("bt_sent"), 64 * GROUPS)
            dve.wait_ge(sem("bc_sent"), 32 * 2 * GROUPS)
            for q in range(2):
                dve.wait_ge(sem(f"xt_sent{q}"), 32 * KD // 2)
            dve.memset(cks[:, NT, :], 0.0).then_inc(sem("rest_set"), 1)
            dve.memset(kro[:, :, ROPE:P], 0.0).then_inc(sem("rest_set"), 1)
            dve.memset(k.dt[:, NT, :], 0.0).then_inc(sem("rest_set"), 1)
            for t in range(NT):
                dve.wait_ge(sem("cq_done"), t + 1)
                dve.tensor_copy(cqs[:, t, :], ps[:, t % 4, 0:QL]).then_inc(sem("cq_out"), 1)
            dve.wait_ge(sem("rest_set"), 3)
            for t in range(NT + 1):
                rows = P if t < NT else META
                dve.wait_ge(sem("ck_done"), t + 1)
                dve.tensor_copy(cks[0:rows, t, :], ps[0:rows, t % 4, 0:KVL + ROPE]).then_inc(sem("ck_raw"), 1)
                dve.tensor_copy(k.dt[0:rows, t, :], ps[0:rows, t % 4, KVL + ROPE:KVL + ROPE + SH]).then_inc(sem("ck_out"), 1)
            dve.wait_ge(sem("lat_sq"), NW)
            rsqrt_before(dve, k, v[:, 0:NT], ss[:, 0:NT], 1.0 / QL, "lat_v", 1)
            rsqrt_before(dve, k, v[:, NT:NW], ss[:, NT:NW], 1.0 / KVL, "lat_v", 2)
            rsqrt_after(dve, k, r[:, 0:NW], v[:, 0:NW], s_[:, 0:NW], t1[:, 0:NW], "lat_sqrt", 1, "rs2")
            for t in range(NT):
                dve.tensor_scalar(cqs[:, t, :], cqs[:, t, :], r[:, t:t + 1], None, ALU.mult).then_inc(sem("cq_scaled"), 1)
            for t in range(NT + 1):
                rows = P if t < NT else META
                dve.tensor_scalar(cks[0:rows, t, 0:KVL], cks[0:rows, t, 0:KVL], r[0:rows, NT + t:NT + t + 1], None,
                                  ALU.mult).then_inc(sem("ck_scaled"), 1)
            dve.wait_ge(sem("rope_in"), 16)
            dve.wait_ge(sem("ck_out"), NT + 1)
            x1, x2 = cks[:, :, KVL:KVL + 32], cks[:, :, KVL + 32:KVL + 64]
            cos, sin = rope[:, :, 0:32], rope[:, :, 32:64]
            a3, b3 = ta[:, 0:288].rearrange("p (t c) -> p t c", c=32), tb[:, 0:288].rearrange("p (t c) -> p t c", c=32)
            rotate(dve, k, x1, x2, cos, sin, a3, b3, kro[:, :, 0:32], kro[:, :, 32:64], "kro", 0)
            for n in range(13):
                c0 = 512 * (n % 2)
                src = ps[:, 4 + n % 4, :]
                if n == 12:
                    dve.wait_ge(sem("lat_turned"), 13)
                    w = k.par[:, PARAM["kva"]:PARAM["kva"] + 2].unsqueeze(2).broadcast_to([P, 2, META])
                    dve.tensor_tensor(mt[:, 0:2, :], ps[:, 4, 0:2 * META].rearrange("p (a b) -> p a b", a=2), w, ALU.mult).then_inc(sem("lat_mt"), 1)
                    dve.tensor_copy(mt[:, 2, :], ps[:, 4, 2 * META:3 * META]).then_inc(sem("lat_mt"), 1)
                    dve.wait_ge(sem("lat_hi"), 14)
                    dve.wait_ge(sem("lat_mt"), 2)
                    dve.tensor_tensor(k.ckT[1][:, :, 0:META], mt[:, 0:2, :], k.ckT[0][:, :, 0:META].bitcast(F32), ALU.subtract).then_inc(sem("lat_m"), 1)
                    dve.tensor_tensor(k.krT[1][:, 0:META], mt[:, 2, :], k.krT[0][:, 0:META].bitcast(F32), ALU.subtract).then_inc(sem("lat_lo"), 1)
                    continue
                dve.wait_ge(sem("lat_hi"), n + 1)
                if n < 6:
                    hi, lo = (x[:, n // 2, c0:c0 + 512] for x in k.cqT)
                    w = col(k, "qa", n // 2)
                elif n < 10:
                    kk = (n - 6) // 2
                    hi, lo = (x[:, kk, META + c0:META + c0 + 512] for x in k.ckT)
                    w = col(k, "kva", kk)
                else:
                    hi, lo = (x[:, META + c0:META + c0 + 512] for x in k.krT)
                    w = 1.0
                dve.scalar_tensor_tensor(lo, src, w, hi.bitcast(F32), ALU.mult, ALU.subtract).then_inc(sem("lat_lo"), 1)

            def low_qr(t):
                dve.wait_ge(sem("qrT_hi"), t + 1)
                if t:
                    dve.wait_ge(sem("qr_sent"), 32 * t)
                dve.tensor_tensor(k.qrT[1][:, :, :], ps[:, 4 + t % 2, :].rearrange("p (a b) -> p a b", b=P), k.qrT[0][:, :, :].bitcast(F32),
                                  ALU.subtract).then_inc(sem("qrT_lo"), 1)

            a3, b3 = ta[:, 0:256].rearrange("p (t c) -> p t c", c=32), tb[:, 0:256].rearrange("p (t c) -> p t c", c=32)
            for t in range(NT):
                dve.wait_ge(sem("qr_done"), t + 1)
                if t:
                    dve.wait_ge(sem("qr_turned"), t)
                q = ps[:, t % 4, :].rearrange("p (h c) -> p h c", c=ROPE)
                cos = rope[:, t, 0:32].unsqueeze(1).broadcast_to([P, HEADS, 32])
                sin = rope[:, t, 32:64].unsqueeze(1).broadcast_to([P, HEADS, 32])
                rotate(dve, k, q[:, :, 0:32], q[:, :, 32:64], cos, sin, a3, b3, qro[:, :, 0:32], qro[:, :, 32:64], "qro", t)
                if t:
                    low_qr(t - 1)
            low_qr(NT - 1)


def rotate(dve, k, x1, x2, cos, sin, a, b, out1, out2, name, turn):
    c = k.sem(name + "_step")
    n = 4 * turn
    if turn:
        dve.wait_ge(k.sem(name + "_done"), 2 * turn)
    dve.tensor_tensor(a, x1, cos, ALU.mult).then_inc(c, 1)
    dve.tensor_tensor(b, x2, sin, ALU.mult).then_inc(c, 1)
    dve.wait_ge(c, n + 2)
    dve.tensor_tensor(out1, a, b, ALU.subtract).then_inc(k.sem(name + "_done"), 1)
    dve.wait_ge(k.sem(name + "_done"), 2 * turn + 1)
    dve.tensor_tensor(a, x2, cos, ALU.mult).then_inc(c, 1)
    dve.tensor_tensor(b, x1, sin, ALU.mult).then_inc(c, 1)
    dve.wait_ge(c, n + 4)
    dve.tensor_tensor(out2, a, b, ALU.add).then_inc(k.sem(name + "_done"), 1)



def phase_attend(k):
    nc, sem, m, ps, io = k.nc, k.sem, k.map, k.ps, k.io
    o = O_RING

    def pair(name, shape, o):
        a, o = m.at(name + "hi", shape, F32R, o)
        b, o = m.at(name + "lo", shape, F32R, o)
        return (a, b), o

    kT, v, qT, qr = {}, {}, {}, {}
    for u in range(2):
        kT[u], o = pair(f"kT{u}", [P, POS], o)
        v[u], o = pair(f"v{u}", [P, NT + 1, VH], o)
        qT[u], o = pair(f"qT{u}", [P, SEQ], o)
        qr[u], o = pair(f"qr{u}", [ROPE, SEQ], o)
    wq, o = pair("wq", [P, QL // P, NOPE], o)
    assert o <= O_R
    o = k.o_lat
    wkv, o = pair("wkv", [P, KVL // P, NOPE + VH], o)
    wq_f, o = m.at("wq_f", [P, QL // P, NOPE], F32, o)
    wkv_f, o = m.at("wkv_f", [P, KVL // P, NOPE + VH], F32, o)
    pT, o = pair("pT", [P, NT + 1, 512], o)
    oT, o = pair("oT", [P, 2, 512], o)
    prob, o = m.at("prob", [P, 4, POS], F32, o)
    assert m.base + o <= k.dt_at
    mx, nb, sm, rs, bias = k.st[0], k.st[1], k.st[2], k.st[3], k.st[4]
    flat = ps[:, :, :].rearrange("p a b -> p (a b)")
    KQ, KK = QL // P, KVL // P
    PASSES = ((0, 0), (0, 1), (1, 0))
    wqh = io["w_q_up"][0].rearrange("(k p) (h c) -> h p k c", p=P, h=HEADS)
    wkh = io["w_kv_up"][0].rearrange("(k p) (h c) -> h p k c", p=P, h=HEADS)
    width = lambda b: META + P * (b + 1)
    start = lambda b: 0 if b % 2 == 0 else 4 * 512 - width(b)
    TURN, OUT, PROJ = 4, 6, 7
    batches = [(b, p0, min(4, b + 2 - p0)) for b in range(NT) for p0 in range(0, b + 2, 4)]
    NB = len(batches)
    assert NB % 2 == 0
    first_batch = [next(i for i, x in enumerate(batches) if x[0] == b) for b in range(NT)]

    def of_block(b):
        return [(i, x) for i, x in enumerate(batches) if x[0] == b]

    pbank = ps[:, PROJ, :]

    def evacs(n, u):
        if n < 2:
            return [(pbank, [x[:, 512 * n:512 * n + 512] for x in qT[u]])]
        if n < 5:
            c0, w = TC[n - 2]
            e = [(ps[:, PROJ, 0:w], [x[:, c0:c0 + w] for x in kT[u]])]
            if n == 4:
                e.append((ps[0:META, PROJ, w:w + VH], [x[0:META, NT, :] for x in v[u]]))
            return e
        q = n - 5
        return [(pbank.rearrange("p (a b) -> p a b", b=VH), [x[:, 4 * q:4 * q + 4, :] for x in v[u]])]

    PIECES = 7
    NE = 8
    before = [n + (n > 4) for n in range(PIECES + 1)]

    with nc.Block() as block:
        @block.sync
        def _(sp):
            def weights(h):
                sp.dma_start(wq_f[:, :, :], wqh[h][:, :, 0:NOPE]).then_inc(sem("a_q_in"), 16)
                sp.dma_start(wkv_f[:, :, :], wkh[h]).then_inc(sem("a_kv_in"), 16)

            def rotated(h, u):
                for i in range(2):
                    sp.dma_start(qr[u][i][:, :].bitcast(F32), k.d_qr[i].rearrange("(h c) t -> h c t", c=ROPE)[h]).then_inc(sem("a_qr_in"), 16)

            def outputs(h, g):
                sp.wait_ge(sem("a_o_lo"), 2 * h + g + 2)
                for i in range(2):
                    sp.dma_start(k.d_att[i].rearrange("(h c) t -> h c t", c=VH)[h][:, 512 * g:512 * g + 512],
                                 oT[i][:, g, :].bitcast(F32)).then_inc(sem(f"a_sent{g}"), 16)

            def head(h, u, left):
                if left >= 2:
                    sp.wait_ge(sem("a_cut"), 4 * h + 8)
                    weights(h + 2)
                if left >= 1:
                    sp.wait_ge(sem("a_s"), NT * h + 1)
                    rotated(h + 1, 1 - u)
                for g in range(2):
                    outputs(h, g)

            weights(0)
            rotated(0, 0)
            sp.wait_ge(sem("a_cut"), 4)
            weights(1)
            with sp.Fori(0, HEADS // 2 - 1) as i:
                for u in range(2):
                    head(2 * i + u, u, 2)
            head(HEADS - 2, 0, 1)
            head(HEADS - 1, 1, 0)
            for g in range(2):
                sp.wait_ge(sem(f"a_sent{g}"), 32 * HEADS + 1)

        @block.gpsimd
        def _(pool):
            def cut(h, peeled):
                for src, dst, name in ((wq_f, wq, "a_q_in"), (wkv_f, wkv, "a_kv_in")):
                    n = 0 if name == "a_q_in" else 2
                    pool.wait_ge(sem(name), 16 * h + 16)
                    if not peeled:
                        pool.wait_ge(sem("a_proj"), PIECES * (h - 1) + (2 if n == 0 else PIECES))
                    a, hi, lo = (x[:, :, :].rearrange("p a b -> p (a b)") for x in (src, *dst))
                    pool.tensor_tensor(hi, a, k.zero[:, 0:1].broadcast_to([P, a.shape[-1]]), ALU.add).then_inc(sem("a_cut"), 1)
                    pool.wait_ge(sem("a_cut"), 4 * h + n + 1)
                    pool.tensor_tensor(lo, a, hi.bitcast(F32), ALU.subtract).then_inc(sem("a_cut"), 1)

            cut(0, True)
            with pool.Fori(1, HEADS) as h:
                cut(h, False)

        @block.tensor
        def _(pe):
            def piece(h, u, n, first=False):
                if n in (0, 2):
                    pe.wait_ge(sem("a_cut"), 4 * h + 2 + n)
                if n > 0 or not first:
                    pe.wait_ge(sem("a_e_lo"), NE * h + before[n])
                if n < 2:
                    for kk in range(KQ):
                        for a, b in PASSES:
                            mm = pe.matmul(pbank, wq[a][:, kk, :], k.cqT[b][:, kk, 512 * n:512 * n + 512],
                                           start=(kk == 0 and (a, b) == (0, 0)), stop=(kk == KQ - 1 and a == 1))
                elif n < 5:
                    c0, w = TC[n - 2]
                    for kk in range(KK):
                        for a, b in PASSES:
                            mm = pe.matmul(ps[:, PROJ, 0:w], wkv[a][:, kk, 0:NOPE], k.ckT[b][:, kk, c0:c0 + w],
                                           start=(kk == 0 and (a, b) == (0, 0)), stop=(kk == KK - 1 and a == 1))
                tiles = [(TC[2][1], 0)] if n == 4 else [(VH * j, META + P * (4 * (n - 5) + j)) for j in range(4)] if n > 4 else []
                for at, c0 in tiles:
                    for kk in range(KK):
                        for a, b in PASSES:
                            mm = pe.matmul(ps[:, PROJ, at:at + VH], k.ckT[a][:, kk, c0:c0 + P], wkv[b][:, kk, NOPE:NOPE + VH],
                                           start=(kk == 0 and (a, b) == (0, 0)), stop=(kk == KK - 1 and a == 1))
                mm.then_inc(sem("a_proj"), 1)

            def scores(h, u, b, first=False):
                n, s0 = width(b), start(b)
                if b == 0:
                    pe.wait_ge(sem("a_qr_in"), 32 * h + 32)
                need = {0: 3, 2: 4, 5: 5}.get(b)
                if need:
                    pe.wait_ge(sem("a_e_lo"), NE * h + need)
                if b >= 2 or not first:
                    pe.wait_ge(sem("a_exp"), NT * h + b - 1)
                cuts = sorted({s0, s0 + n} | {c for c in range(0, 2048, 512) if s0 < c < s0 + n})
                tiles = [(c - s0, d - s0) for c, d in zip(cuts[:-1], cuts[1:])][::-1]
                d0, d1 = n - P, n
                for i, (c0, c1) in enumerate(tiles):
                    if b == NT - 1 and i == len(tiles) - 1:
                        pe.wait_ge(sem("a_exp"), NT * h + b)
                    out = flat[:, s0 + c0:s0 + c1]
                    q = slice(P * b, P * b + P)
                    pe.matmul(out, qT[u][0][:, q], kT[u][0][:, c0:c1], start=True, stop=False)
                    lo, hi = max(c0, d0), min(c1, d1)
                    if lo < hi:
                        pe.matmul(flat[:, s0 + lo:s0 + hi], k.mask_b[:, :], k.ident_b[:, lo - d0:hi - d0], start=False, stop=False)
                    pe.matmul(out, qT[u][0][:, q], kT[u][1][:, c0:c1], start=False, stop=False)
                    pe.matmul(out, qT[u][1][:, q], kT[u][0][:, c0:c1], start=False, stop=False)
                    for a, c in PASSES:
                        mm = pe.matmul(out, qr[u][a][:, q], k.krT[c][0:ROPE, c0:c1], start=False, stop=(a == 1))
                mm.then_inc(sem("a_s"), 1)

            def turn(h, b):
                pe.wait_ge(sem("a_p"), NT * h + b + 1)
                for i, (_, p0, np_) in of_block(b):
                    if i >= 2:
                        pe.wait_ge(sem("a_t_lo"), NB * h + i - 1)
                    for j in range(np_):
                        c0 = 0 if p0 + j == 0 else META + P * (p0 + j - 1)
                        mm = pe.transpose(ps[:, TURN + i % 2, P * j:P * j + P], prob[:, b % 4, c0:c0 + P], k.ident[:, :])
                    mm.then_inc(sem("a_t"), 1)

            def weigh(h, u, g):
                pe.wait_ge(sem("a_t_lo"), NB * h + (first_batch[4] if g == 0 else NB))
                pe.wait_ge(sem("a_o_lo"), 2 * h + g + 1)
                if g == 0:
                    pe.wait_ge(sem("a_e_lo"), NE * h + NE)
                last = 4 * g + 3
                for j in range(-1, last + 1):
                    rows = slice(0, META if j < 0 else P)
                    vt = NT if j < 0 else j
                    c0 = P * max(0, j - 4 * g)
                    for a, b in PASSES:
                        mm = pe.matmul(ps[:, OUT, c0:512], v[u][a][rows, vt, :], pT[b][rows, j + 1, c0:512],
                                       start=(j < 0 and (a, b) == (0, 0)), stop=(j == last and a == 1))
                mm.then_inc(sem("a_o"), 1)

            def late(h, u, more):
                for b in range(3, NT):
                    scores(h, u, b)
                    if more:
                        piece(h + 1, 1 - u, b - 3)
                    if b == 6:
                        weigh(h, u, 0)
                    turn(h, b - 2)

            def next_early(h, u):
                for b in range(3):
                    scores(h + 1, 1 - u, b)
                    if b < 2:
                        piece(h + 1, 1 - u, 5 + b)
                        turn(h, NT - 2 + b)
                weigh(h, u, 1)
                turn(h + 1, 0)

            for n in range(PIECES):
                piece(0, 0, n, True)
            for b in range(3):
                scores(0, 0, b, True)
            turn(0, 0)
            with pe.Fori(0, HEADS // 2 - 1) as i:
                for u in range(2):
                    late(2 * i + u, u, True)
                    next_early(2 * i + u, u)
            late(HEADS - 2, 0, True)
            next_early(HEADS - 2, 0)
            late(HEADS - 1, 1, False)
            for b in (NT - 2, NT - 1):
                turn(HEADS - 1, b)
            weigh(HEADS - 1, 1, 1)

        @block.scalar
        def _(act):
            def high(h, b):
                for i, (_, p0, np_) in of_block(b):
                    act.wait_ge(sem("a_t"), NB * h + i + 1)
                    act.activation(pT[0][:, p0:p0 + np_, P * (b % 4):P * (b % 4) + P],
                                   ps[:, TURN + i % 2, 0:P * np_].rearrange("p (a b) -> p a b", b=P), ACT.Copy).then_inc(sem("a_t_hi"), 1)

            def exp(h, b):
                n, s0 = width(b), start(b)
                act.wait_ge(sem("a_nb"), NT * h + b + 1)
                act.activation(prob[:, b % 4, 0:n], flat[:, s0:s0 + n], ACT.Exp, bias=nb[:, b:b + 1], scale=SCALE,
                               accum_out=sm[:, b:b + 1]).then_inc(sem("a_exp"), 1)

            def out(h, g):
                act.wait_ge(sem("a_o"), 2 * h + g + 1)
                act.wait_ge(sem(f"a_sent{g}"), 32 * h + 1)
                act.activation(oT[0][:, g, :], ps[:, OUT, :], ACT.Copy).then_inc(sem("a_o_hi"), 1)

            def piece(h, u, n):
                act.wait_ge(sem("a_proj"), PIECES * h + n + 1)
                for src, dst in evacs(n, u):
                    act.activation(dst[0], src, ACT.Copy).then_inc(sem("a_e_hi"), 1)

            def late(h, u, more):
                for b in range(3, NT):
                    exp(h, b)
                    if more:
                        piece(h + 1, 1 - u, b - 3)
                    high(h, b - 2)
                    if b == 6:
                        out(h, 0)

            def next_early(h, u):
                for b in range(3):
                    exp(h + 1, b)
                    if b < 2:
                        piece(h + 1, 1 - u, 5 + b)
                        high(h, NT - 2 + b)
                out(h, 1)
                high(h + 1, 0)

            for n in range(PIECES):
                piece(0, 0, n)
            for b in range(3):
                exp(0, b)
            high(0, 0)
            with act.Fori(0, HEADS // 2 - 1) as i:
                for u in range(2):
                    late(2 * i + u, u, True)
                    next_early(2 * i + u, u)
            late(HEADS - 2, 0, True)
            next_early(HEADS - 2, 0)
            late(HEADS - 1, 1, False)
            for b in (NT - 2, NT - 1):
                high(HEADS - 1, b)
            out(HEADS - 1, 1)

        @block.vector
        def _(dve):
            dve.memset(bias[:, 0:1], 0.0).then_inc(sem("a_o_lo"), 1)
            for g in range(2):
                dve.memset(bias[:, 1 + g:2 + g], 0.0).then_inc(sem(f"a_sent{g}"), 1)

            def most(h, b):
                n, s0 = width(b), start(b)
                dve.wait_ge(sem("a_s"), NT * h + b + 1)
                dve.tensor_reduce(mx[:, b:b + 1], flat[:, s0:s0 + n], AX.X, ALU.max).then_inc(sem("a_mx"), 1)
                dve.wait_ge(sem("a_mx"), NT * h + b + 1)
                dve.tensor_scalar(nb[:, b:b + 1], mx[:, b:b + 1], -SCALE, None, ALU.mult).then_inc(sem("a_nb"), 1)

            def normalise(h, b):
                n = width(b)
                dve.wait_ge(sem("a_exp"), NT * h + b + 1)
                dve.reciprocal(rs[:, b:b + 1], sm[:, b:b + 1]).then_inc(sem("a_rs"), 1)
                dve.wait_ge(sem("a_rs"), NT * h + b + 1)
                dve.tensor_scalar(prob[:, b % 4, 0:n], prob[:, b % 4, 0:n], rs[:, b:b + 1], None, ALU.mult).then_inc(sem("a_p"), 1)

            def low(h, b):
                for i, (_, p0, np_) in of_block(b):
                    dve.wait_ge(sem("a_t_hi"), NB * h + i + 1)
                    hi, lo = (x[:, p0:p0 + np_, P * (b % 4):P * (b % 4) + P] for x in pT)
                    dve.tensor_tensor(lo, ps[:, TURN + i % 2, 0:P * np_].rearrange("p (a b) -> p a b", b=P), hi.bitcast(F32),
                                      ALU.subtract).then_inc(sem("a_t_lo"), 1)

            def out(h, g):
                dve.wait_ge(sem("a_o_hi"), 2 * h + g + 1)
                dve.tensor_tensor(oT[1][:, g, :], ps[:, OUT, :], oT[0][:, g, :].bitcast(F32), ALU.subtract).then_inc(sem("a_o_lo"), 1)

            def piece(h, u, n):
                e = evacs(n, u)
                dve.wait_ge(sem("a_e_hi"), NE * h + before[n] + len(e))
                for src, dst in e:
                    dve.tensor_tensor(dst[1], src, dst[0].bitcast(F32), ALU.subtract).then_inc(sem("a_e_lo"), 1)

            def late(h, u, more):
                for b in range(3, NT):
                    most(h, b)
                    normalise(h, b - 1)
                    if more:
                        piece(h + 1, 1 - u, b - 3)
                    low(h, b - 2)
                    if b == 6:
                        out(h, 0)

            def next_early(h, u):
                for b in range(3):
                    most(h + 1, b)
                    if b == 0:
                        normalise(h, NT - 1)
                    else:
                        normalise(h + 1, b - 1)
                    if b < 2:
                        piece(h + 1, 1 - u, 5 + b)
                        low(h, NT - 2 + b)
                out(h, 1)
                low(h + 1, 0)

            for n in range(PIECES):
                piece(0, 0, n)
            for b in range(3):
                most(0, b)
                if b:
                    normalise(0, b - 1)
            low(0, 0)
            with dve.Fori(0, HEADS // 2 - 1) as i:
                for u in range(2):
                    late(2 * i + u, u, True)
                    next_early(2 * i + u, u)
            late(HEADS - 2, 0, True)
            next_early(HEADS - 2, 0)
            late(HEADS - 1, 1, False)
            normalise(HEADS - 1, NT - 1)
            for b in (NT - 2, NT - 1):
                low(HEADS - 1, b)
            out(HEADS - 1, 1)



def phase_ssd(k):
    nc, sem, m, ps, io = k.nc, k.sem, k.map, k.ps, k.io
    k.fam = "u"
    wo = io["w_out"][0]
    k.wo_blocks = [wo[D * part + P * kk:D * part + P * kk + P, 512 * c:512 * c + 512] for part in range(2) for c in range(2) for kk in range(KD)]
    o = O_R

    def pair(name, shape, o):
        a, o = m.at(name + "hi", shape, F32R, o)
        b, o = m.at(name + "lo", shape, F32R, o)
        return (a, b), o

    xs, o = m.at("s_x", [P, 2, SSMW], F32, o)
    zs, o = m.at("s_z", [P, 2, SSMW], F32, o)
    bT, o = pair("s_bT", [P, 2, GROUPS, P], o)
    cT, o = pair("s_cT", [P, 2, GROUPS, P], o)
    bt, o = pair("s_bt", [P, 2, GROUPS * STATE], o)
    aT, o = pair("s_aT", [P, 2, KD, P], o)
    xdt, o = m.at("xdt", [P, SSMW], F32, o)
    xh, o = pair("xdt_", [P, SSMW], o)
    xw, o = m.at("xw", [P, SSMW], F32, o)
    xwh, o = pair("xw_", [P, SSMW], o)
    xd, o = m.at("xd", [P, SSMW], F32, o)
    state, o = m.at("state", [P, SSMW], F32, o)
    sth, o = pair("state_", [P, SSMW], o)
    es, o = m.at("es", [P, 2, 512], F32, o)
    wl, o = pair("wl", [P, 2, 4, P], o)
    cbs, o = m.at("cbs", [P, GROUPS, P], F32, o)
    mixs, o = m.at("mixs", [P, D], F32, o)
    dac, o = pair("dac", [P, SH], o)
    op = o
    y, o = m.at("y", [P, 2, SSMW], F32, o)
    sT, o = pair("sT", [P, KD, P], o)
    assert o <= O_TABLES
    junk = k.spare
    dt = k.dt

    T9 = [P, NT + 1, SH]
    pa, op = m.at("p_a", T9, F32, op)
    pb, op = m.at("p_b", T9, F32, op)
    pc, op = m.at("p_c", T9, F32, op)
    dtb, op = m.at("p_dtb", [P, SH], F32, op)
    av, op = m.at("p_a_log", [P, SH], F32, op)
    xm, op = m.at("p_xm", [META, SSMW], F32, op)
    bm, op = pair("p_bm", [META, GROUPS * STATE], op)
    od = O_TABLES
    da, od = pair("da", T9, od)
    acum, od = m.at("acum", T9, F32, od)
    ecum, od = m.at("ecum", T9, F32, od)
    dend, od = m.at("dend", T9, F32, od)
    cdec, od = m.at("cdec", T9, F32, od)
    dsk, od = m.at("dskip", [P, SH], F32, od)
    wrow, od = m.at("ssm_w", [P, SSMW], F32, od)
    ss, v, s_, r, t1 = k.st[0], k.st[1], k.st[2], k.st[3], k.st[4]
    PASSES = ((0, 0), (0, 1), (1, 0))
    W = (k.whi, k.wlo)
    heads = lambda a: a.rearrange("p (h c) -> p h c", c=SHD)
    flat9 = lambda a: a[:, :, :].rearrange("p a b -> p (a b)")
    by_head = lambda a, rows=P: a.unsqueeze(2).broadcast_to([rows, SH, SHD])
    N9 = (NT + 1) * SH

    LAST = NT - 1
    QUARTER = KD // 2

    with nc.Block() as block:
        @block.sync
        def _(sp):
            rows = lambda a, t: a.rearrange("(t p) n -> t p n", p=P)[t]
            cols = lambda a, t: a.rearrange("(k p) (t n) -> t p k n", p=P, n=P)[t]

            def load_x(t, u):
                sp.dma_start(xs[:, u, :], rows(k.d_x, t)).then_inc(sem(f"s_x_in{u}"), 16)

            def load_z(t, u):
                sp.dma_start(zs[:, u, :], rows(k.d_z, t)).then_inc(sem(f"s_z_in{u}"), 16)

            def load_bc(t, u):
                for i in range(2):
                    sp.dma_start(bT[i][:, u, :, :].bitcast(F32), cols(k.d_bt[i], t)).then_inc(sem(f"s_bc_in{u}"), 16)
                    sp.dma_start(cT[i][:, u, :, :].bitcast(F32), cols(k.d_ct[i], t)).then_inc(sem(f"s_bc_in{u}"), 16)
                    sp.dma_start(bt[i][:, u, :].bitcast(F32), rows(k.d_b[i], t)).then_inc(sem(f"s_bc_in{u}"), 16)

            def load_at(t, u):
                for i in range(2):
                    sp.dma_start(aT[i][:, u, :, :].bitcast(F32), cols(k.d_att[i], t)).then_inc(sem(f"s_at_in{u}"), 16)

            def store_mix(t, c):
                sp.wait_ge(sem("s_mixc"), 2 * t + c + 1)
                sp.dma_start(rows(k.d_mix, t)[:, 512 * c:512 * c + 512], mixs[:, 512 * c:512 * c + 512]).then_inc(sem(f"s_mix_sent{c}"), 16)

            def store_ssm(t):
                sp.wait_ge(sem("s_end"), t + 2)
                for i in range(2):
                    sp.dma_start(cols(k.d_ssm[i], t), sT[i][:, :, :].bitcast(F32)).then_inc(sem("s_sent"), 16)

            def turn(t, u, first, left):
                store_mix(t, 0)
                if left >= 2:
                    sp.wait_ge(sem("s_stp"), t + 1)
                    load_bc(t + 2, u)
                if not first:
                    if left >= 1:
                        sp.wait_ge(sem("s_gz"), t)
                        load_z(t + 1, 1 - u)
                    store_ssm(t - 1)
                if left >= 2:
                    sp.wait_ge(sem("s_xd"), t + 1)
                    load_x(t + 2, u)
                    sp.wait_ge(sem("s_mix"), 2 * t + 2)
                    load_at(t + 2, u)
                store_mix(t, 1)

            sp.dma_start(dtb[:, :], io["dt_bias"][0].partition_broadcast(P)).then_inc(sem("p_in"), 16)
            sp.dma_start(av[:, :], io["a_log"][0].partition_broadcast(P)).then_inc(sem("p_in"), 16)
            sp.dma_start(xm[:, :], k.d_xm).then_inc(sem("p_in"), 16)
            for i in range(2):
                sp.dma_start(bm[i][:, :].bitcast(F32), k.d_bm[i]).then_inc(sem("p_in"), 16)
            sp.dma_start(wrow[:, :], io["ssm_norm"][0].partition_broadcast(P)).then_inc(sem("p_in"), 16)
            sp.dma_start(dsk[:, :], io["d_skip"][0].partition_broadcast(P)).then_inc(sem("p_in"), 16)
            load_x(0, 0)
            load_bc(0, 0)
            for n in range(STAGES):
                load_block(sp, k, n, k.wo_blocks[n])
            load_at(0, 0)
            for n in range(STAGES, RING):
                load_block(sp, k, n, k.wo_blocks[n])
            load_z(0, 0)
            load_x(1, 1)
            load_bc(1, 1)
            load_at(1, 1)
            load_z(1, 1)
            turn(0, 0, True, LAST)
            with sp.Fori(0, NT // 2 - 2) as i:
                for u in (1, 0):
                    turn(2 * i + 2 - u, u, False, 2)
            for t in range(NT - 3, NT):
                turn(t, t % 2, False, LAST - t)
            for n in range(RING, RING + STAGES):
                load_block(sp, k, n, k.wo_blocks[n])
            store_ssm(LAST)
            sp.wait_ge(sem("s_sent"), 32 * NT + 1)
            for c in range(2):
                sp.wait_ge(sem(f"s_mix_sent{c}"), 16 * NT)

        @block.gpsimd
        def _(pool):
            def gate(t, u):
                pool.wait_ge(sem("s_yd"), t + 1)
                pool.tensor_tensor(y[:, u, :], y[:, u, :], xd[:, :], ALU.add).then_inc(sem("s_ya"), 1)
                pool.wait_ge(sem("s_ya"), t + 1)
                pool.wait_ge(sem(f"s_z_in{u}"), 8 * (t - u) + 16)
                pool.tensor_tensor(y[:, u, :], y[:, u, :], zs[:, u, :], ALU.mult).then_inc(sem("s_gz"), 1)

            def chunk(t, u, first):
                if not first:
                    pool.wait_ge(sem("s_xwlo"), t)
                pool.wait_ge(sem("s_xdt"), t + 1)
                pool.tensor_tensor(heads(xw[:, :]), heads(xdt[:, :]), by_head(dend[:, t, :]), ALU.mult).then_inc(sem("s_xw"), 1)
                if not first:
                    gate(t - 1, 1 - u)
                pool.wait_ge(sem("s_xwh"), t + 1)
                pool.tensor_tensor(xwh[1][:, :], xw[:, :], xwh[0][:, :].bitcast(F32), ALU.subtract).then_inc(sem("s_xwlo"), 1)
                pool.wait_ge(sem("s_xh"), t + 1)
                pool.tensor_tensor(xh[1][:, :], xdt[:, :], xh[0][:, :].bitcast(F32), ALU.subtract).then_inc(sem("s_xlo"), 1)
                pool.tensor_tensor(heads(xd[:, :]), heads(xs[:, u, :]), by_head(dsk[:, :]), ALU.mult).then_inc(sem("s_xd"), 1)

            pool.wait_ge(sem("p_in"), 16 * 7)
            chunk(0, 0, True)
            with pool.Fori(0, NT // 2 - 1) as i:
                for u in (1, 0):
                    chunk(2 * i + 2 - u, u, False)
            chunk(LAST, 1, False)
            gate(LAST, 1)

        @block.tensor
        def _(pe):
            pe.wait_ge(sem("p_da"), 2)
            for bank, lhs in ((0, k.tri), (1, k.ones)):
                for a in range(2):
                    pe.matmul(ps[:, bank, 0:NT * SH], lhs[:, :], da[a][:, 0:NT, :].rearrange("p a b -> p (a b)"), start=(a == 0), stop=(a == 1))
                for a in range(2):
                    mm = pe.matmul(ps[:, bank, NT * SH:N9], lhs[0:META, :], da[a][0:META, NT, :], start=(a == 0), stop=(a == 1))
            mm.then_inc(sem("p_sums"), 1)
            pe.wait_ge(sem("p_xwlo"), 1)
            for g in range(GROUPS):
                for a, b in PASSES:
                    mm = pe.matmul(ps[:, 4 + g, :], bm[a][:, P * g:P * g + P], xwh[b][0:META, 512 * g:512 * g + 512], start=(a == 0 and b == 0), stop=(a == 1))
            mm.then_inc(sem("p_state"), 1)

            def decays(q):
                bank = 7 - q % 2
                pe.matmul(ps[:, bank, :], k.ident_b[:, :], k.mask_b[:, :].unsqueeze(1).broadcast_to([P, 4, P]), start=True, stop=False)
                for j in range(4):
                    for a in range(2):
                        mm = pe.matmul(ps[:, bank, P * j:P * j + P], dac[a][:, 4 * q + j:4 * q + j + 1].broadcast_to([P, P]), k.tri[:, :],
                                       start=False, stop=(a == 1 and j == 3))
                mm.then_inc(sem("s_eb"), 1)

            def mix(t, u, c, half, first):
                if half == 0 and not first:
                    pe.wait_ge(sem("s_mixc"), 2 * t - 1 + c)
                for kk in range(QUARTER * half, QUARTER * half + QUARTER):
                    if first:
                        pe.wait_ge(sem("u_cut"), KD * c + kk + 1)
                    for a, b in PASSES:
                        mm = pe.matmul(ps[:, 4 + c, :], aT[a][:, u, kk, :], W[b][:, KD * c + kk, :],
                                       start=(kk == 0 and (a, b) == (0, 0)), stop=(kk == KD - 1 and a == 1))
                if half == 1:
                    mm.then_inc(sem("s_mix"), 1)

            def diag(t, q):
                pe.wait_ge(sem("s_wlo"), 4 * t + q + 1)
                for j in range(4):
                    h = 4 * q + j
                    out = ps[:, 2 + h // 8, SHD * (h % 8):SHD * (h % 8) + SHD]
                    for a, b in PASSES:
                        mm = pe.matmul(out, wl[a][:, q % 2, j, :], xh[b][:, SHD * h:SHD * h + SHD], start=(a == 0 and b == 0), stop=(a == 1))
                mm.then_inc(sem("s_dg"), 1)

            def turned(t, u):
                pe.wait_ge(sem("s_g"), 2 * t + 2)
                for c in range(2):
                    for j in range(4):
                        kk = 4 * c + j
                        mm = pe.transpose(ps[:, c, P * j:P * j + P], y[:, u, P * kk:P * kk + P], k.ident[:, :])
                    mm.then_inc(sem("s_tr"), 1)

            def chunk(t, u, first):
                pe.wait_ge(sem(f"s_bc_in{u}"), 48 * (t - u) + 96)
                if not first:
                    pe.wait_ge(sem("s_sub"), 4 * t)
                for g in range(GROUPS):
                    for a, b in PASSES:
                        mm = pe.matmul(ps[:, 6, P * g:P * g + P], bT[a][:, u, g, :], cT[b][:, u, g, :], start=(a == 0 and b == 0), stop=(a == 1))
                mm.then_inc(sem("s_cb"), 1)
                pe.wait_ge(sem("s_dac"), 2 * t + 2)
                decays(0)
                pe.wait_ge(sem("s_stlo"), t + 1)
                if not first:
                    pe.wait_ge(sem("s_end"), t)
                for g in range(GROUPS):
                    for a, b in PASSES:
                        mm = pe.matmul(ps[:, g, :], cT[a][:, u, g, :], sth[b][:, 512 * g:512 * g + 512], start=(a == 0 and b == 0), stop=(a == 1))
                mm.then_inc(sem("s_off"), 1)
                pe.wait_ge(sem("s_cbs"), t + 1)
                decays(1)
                pe.wait_ge(sem(f"s_at_in{u}"), 16 * (t - u) + 32)
                mix(t, u, 0, 0, first)
                for q in (2, 3):
                    pe.wait_ge(sem("s_sub"), 4 * t + q - 1)
                    decays(q)
                mix(t, u, 0, 1, first)
                mix(t, u, 1, 0, first)
                pe.wait_ge(sem("s_xwlo"), t + 1)
                pe.wait_ge(sem("s_yo"), t + 1)
                for g in range(GROUPS):
                    for a, b in PASSES:
                        mm = pe.matmul(ps[:, g, :], bt[a][:, u, P * g:P * g + P], xwh[b][:, 512 * g:512 * g + 512],
                                       start=(a == 0 and b == 0), stop=(a == 1))
                mm.then_inc(sem("s_stp"), 1)
                pe.wait_ge(sem("s_xlo"), t + 1)
                if not first:
                    pe.wait_ge(sem("s_yd"), t)
                diag(t, 0)
                diag(t, 1)
                pe.wait_ge(sem("s_st"), t + 2)
                if not first:
                    turned(t - 1, 1 - u)
                mix(t, u, 1, 1, first)
                diag(t, 2)
                diag(t, 3)

            chunk(0, 0, True)
            with pe.Fori(0, NT // 2 - 1) as i:
                for u in (1, 0):
                    chunk(2 * i + 2 - u, u, False)
            chunk(LAST, 1, False)
            turned(LAST, 1)

        @block.scalar
        def _(act):
            def cuts(n0, n1):
                for n in range(n0, n1):
                    cut_hi(act, k, n)

            act.wait_ge(sem("p_x"), 2)
            act.activation(flat9(pb), flat9(pa), ACT.Exp, scale=-1.0).then_inc(sem("p_u"), 1)
            act.activation(av[:, :], av[:, :], ACT.Exp).then_inc(sem("p_u"), 1)
            act.wait_ge(sem("p_w"), 1)
            act.activation(flat9(pc), flat9(pa), ACT.Ln).then_inc(sem("p_ln"), 1)
            cuts(0, 3)
            act.wait_ge(sem("p_dt"), 1)
            act.activation(flat9(da[0]), flat9(pb), ACT.Copy).then_inc(sem("p_da"), 1)
            cuts(3, 7)
            act.wait_ge(sem("p_diff"), 3)
            act.activation(flat9(ecum), flat9(acum), ACT.Exp).then_inc(sem("p_exp"), 1)
            act.activation(flat9(dend), flat9(pa), ACT.Exp).then_inc(sem("p_exp"), 1)
            act.activation(flat9(cdec), flat9(pc), ACT.Exp).then_inc(sem("p_exp"), 1)
            act.wait_ge(sem("p_xw"), 2)
            act.activation(xwh[0][0:META, :], xw[0:META, :], ACT.Copy).then_inc(sem("p_xwhi"), 1)
            cuts(7, 10)
            act.wait_ge(sem("p_st0"), 1)
            act.activation(sth[0][:, :], state[:, :], ACT.Copy).then_inc(sem("s_sthi"), 1)
            cuts(10, 16)

            def squares(t, u):
                act.wait_ge(sem("s_gz"), t + 1)
                for g in range(GROUPS):
                    act.wait_ge(sem("s_sq"), 2 * t + g + 1)
                    act.activation(junk[:, :], y[:, u, 512 * g:512 * g + 512], ACT.Square, accum_out=ss[:, g:g + 1]).then_inc(sem("s_sq"), 1)

            def root(t):
                act.wait_ge(sem("s_v"), t + 1)
                act.activation(s_[:, 0:2], v[:, 0:2], ACT.Sqrt).then_inc(sem("s_sqrt"), 1)

            def turned(t):
                act.wait_ge(sem("s_sent"), 32 * t + 1)
                for c in range(2):
                    act.wait_ge(sem("s_tr"), 2 * t + c + 1)
                    act.activation(sT[0][:, 4 * c:4 * c + 4, :].rearrange("p a b -> p (a b)"), ps[:, c, :], ACT.Copy).then_inc(sem("s_gh"), 1)

            def chunk(t, u, first):
                def w_hi(q):
                    act.wait_ge(sem("s_wm"), 4 * t + q + 1)
                    if q >= 2:
                        act.wait_ge(sem("s_dg"), 4 * t + q - 1)
                    act.activation(wl[0][:, q % 2, :, :].rearrange("p a b -> p (a b)"), es[:, q % 2, :], ACT.Copy).then_inc(sem("s_whi"), 1)

                def expo(q):
                    act.wait_ge(sem("s_sub"), 4 * t + q + 1)
                    act.activation(es[:, q % 2, :], es[:, q % 2, :], ACT.Exp).then_inc(sem("s_exp"), 1)

                def mix_out(c):
                    act.wait_ge(sem("s_mix"), 2 * t + c + 1)
                    if not first:
                        act.wait_ge(sem(f"s_mix_sent{c}"), 16 * t)
                    act.activation(mixs[:, 512 * c:512 * c + 512], ps[:, 4 + c, :], ACT.Copy).then_inc(sem("s_mixc"), 1)

                act.wait_ge(sem("s_cb"), t + 1)
                act.activation(cbs[:, :, :].rearrange("p a b -> p (a b)"), ps[:, 6, 0:GROUPS * P], ACT.Copy).then_inc(sem("s_cbs"), 1)
                expo(0)
                act.wait_ge(sem("s_xdt"), t + 1)
                if not first:
                    act.wait_ge(sem("s_dg"), 4 * t)
                act.activation(xh[0][:, :], xdt[:, :], ACT.Copy).then_inc(sem("s_xh"), 1)
                expo(1)
                w_hi(0)
                act.wait_ge(sem("s_xw"), t + 1)
                if not first:
                    act.wait_ge(sem("s_stp"), t)
                act.activation(xwh[0][:, :], xw[:, :], ACT.Copy).then_inc(sem("s_xwh"), 1)
                w_hi(1)
                expo(2)
                if not first:
                    squares(t - 1, 1 - u)
                expo(3)
                if not first:
                    root(t - 1)
                mix_out(0)
                act.wait_ge(sem("s_st"), t + 2)
                act.activation(sth[0][:, :], state[:, :], ACT.Copy).then_inc(sem("s_sthi"), 1)
                w_hi(2)
                w_hi(3)
                if not first:
                    turned(t - 1)
                mix_out(1)

            chunk(0, 0, True)
            with act.Fori(0, NT // 2 - 1) as i:
                for u in (1, 0):
                    chunk(2 * i + 2 - u, u, False)
            chunk(LAST, 1, False)
            squares(LAST, 1)
            root(LAST)
            turned(LAST)

        @block.vector
        def _(dve):
            def cuts(n0, n1):
                for n in range(n0, n1):
                    cut_lo(dve, k, n)

            d = sem("p_step")
            dve.wait_ge(sem("p_in"), 16 * 7)
            raw = dt[:, :, :]
            dve.tensor_tensor(raw, raw, dtb[:, :].unsqueeze(1).broadcast_to(T9), ALU.add).then_inc(sem("p_x"), 1)
            dve.wait_ge(sem("p_x"), 1)
            dve.scalar_tensor_tensor(flat9(pa), flat9(dt), -1.0, flat9(dt), ALU.mult, ALU.max).then_inc(sem("p_x"), 1)
            dve.wait_ge(sem("p_u"), 2)
            dve.tensor_scalar(flat9(pa), flat9(pb), 1.0, None, ALU.add).then_inc(sem("p_w"), 1)
            dve.wait_ge(sem("p_ln"), 1)
            dve.tensor_scalar(flat9(pa), flat9(pa), -1.0, None, ALU.add).then_inc(d, 1)
            dve.wait_ge(d, 1)
            dve.tensor_scalar(flat9(acum), flat9(pa), 0.0, None, ALU.is_equal).then_inc(d, 1)
            dve.wait_ge(d, 2)
            dve.tensor_tensor(flat9(pa), flat9(pa), flat9(acum), ALU.add).then_inc(d, 1)
            dve.tensor_tensor(flat9(pc), flat9(pc), flat9(acum), ALU.add).then_inc(d, 1)
            dve.wait_ge(d, 4)
            dve.tensor_tensor(flat9(pc), flat9(pc), flat9(pb), ALU.mult).then_inc(d, 1)
            dve.reciprocal(flat9(acum), flat9(pa)).then_inc(d, 1)
            dve.wait_ge(d, 6)
            dve.tensor_tensor(flat9(pc), flat9(pc), flat9(acum), ALU.mult).then_inc(d, 1)
            dve.wait_ge(d, 7)
            dve.scalar_tensor_tensor(flat9(dt), flat9(dt), 0.0, flat9(pc), ALU.max, ALU.add).then_inc(d, 1)
            dve.wait_ge(d, 8)
            dve.tensor_tensor(pc[:, :, :], raw, av[:, :].unsqueeze(1).broadcast_to(T9), ALU.mult).then_inc(d, 1)
            dve.wait_ge(d, 9)
            dve.tensor_scalar(flat9(pb), flat9(pc), -1.0, None, ALU.mult).then_inc(sem("p_dt"), 1)
            dve.wait_ge(sem("p_da"), 1)
            dve.tensor_tensor(flat9(da[1]), flat9(pb), flat9(da[0]).bitcast(F32), ALU.subtract).then_inc(sem("p_da"), 1)
            cuts(0, 3)
            dve.wait_ge(sem("p_sums"), 1)
            dve.tensor_copy(flat9(acum), ps[:, 0, 0:N9]).then_inc(sem("p_diff"), 1)
            dve.tensor_copy(flat9(pc), ps[:, 1, 0:N9]).then_inc(sem("p_diff"), 1)
            dve.wait_ge(sem("p_diff"), 2)
            dve.tensor_tensor(flat9(pa), flat9(pc), flat9(acum), ALU.subtract).then_inc(sem("p_diff"), 1)
            dve.tensor_tensor(heads(xw[0:META, :]), heads(xm[:, :]), by_head(dt[0:META, NT, :], META), ALU.mult).then_inc(sem("p_xw"), 1)
            cuts(3, 7)
            dve.wait_ge(sem("p_exp"), 3)
            dve.wait_ge(sem("p_xw"), 1)
            dve.tensor_tensor(heads(xw[0:META, :]), heads(xw[0:META, :]), by_head(dend[0:META, NT, :], META), ALU.mult).then_inc(sem("p_xw"), 1)
            dve.wait_ge(sem("p_xwhi"), 1)
            dve.tensor_tensor(xwh[1][0:META, :], xw[0:META, :], xwh[0][0:META, :].bitcast(F32), ALU.subtract).then_inc(sem("p_xwlo"), 1)
            cuts(7, 10)
            dve.wait_ge(sem("p_state"), 1)
            dve.tensor_copy(state[:, :], ps[:, 4:6, :].rearrange("p a b -> p (a b)")).then_inc(sem("p_st0"), 1)
            dve.memset(r[:, 11:12], 0.0).then_inc(sem("s_sent"), 1)
            dve.memset(r[:, 12:13], 0.0).then_inc(sem("s_end"), 1)
            dve.memset(r[:, 13:14], 0.0).then_inc(sem("s_sq"), 1)
            dve.memset(r[:, 14:15], 0.0).then_inc(sem("s_st"), 1)
            dve.wait_ge(sem("s_sthi"), 1)
            dve.tensor_tensor(sth[1][:, :], state[:, :], sth[0][:, :].bitcast(F32), ALU.subtract).then_inc(sem("s_stlo"), 1)

            def sums(t):
                for a in range(2):
                    dve.tensor_copy(dac[a][:, :], da[a][:, t, :].bitcast(F32)).then_inc(sem("s_dac"), 1)

            def norm(t, u):
                dve.wait_ge(sem("s_sq"), 2 * t + 3)
                rsqrt_before(dve, k, v[:, 0:2], ss[:, 0:2], 1.0 / (SSMW // GROUPS), "s_v", 1)
                rsqrt_after(dve, k, r[:, 0:2], v[:, 0:2], s_[:, 0:2], t1[:, 0:2], "s_sqrt", t + 1, "s_rs", 5 * t)
                for g in range(GROUPS):
                    part = slice(512 * g, 512 * g + 512)
                    dve.scalar_tensor_tensor(y[:, u, part], y[:, u, part], r[:, g:g + 1], wrow[:, part], ALU.mult, ALU.mult).then_inc(sem("s_g"), 1)

            def turned(t):
                for c in range(2):
                    dve.wait_ge(sem("s_gh"), 2 * t + c + 1)
                    hi, lo = (x[:, 4 * c:4 * c + 4, :].rearrange("p a b -> p (a b)") for x in sT)
                    mm = dve.tensor_tensor(lo, ps[:, c, :], hi.bitcast(F32), ALU.subtract)
                mm.then_inc(sem("s_end"), 1)

            def chunk(t, u, first):
                def sub(q):
                    if q >= 2 or not first:
                        dve.wait_ge(sem("s_wlo"), 4 * t + q - 1)
                    dve.wait_ge(sem("s_eb"), 4 * t + q + 1)
                    dve.tensor_tensor(es[:, q % 2, :].rearrange("p (a b) -> p a b", b=P), ps[:, 7 - q % 2, :].rearrange("p (a b) -> p a b", b=P),
                                      acum[:, t, 4 * q:4 * q + 4].unsqueeze(2).broadcast_to([P, 4, P]), ALU.subtract).then_inc(sem("s_sub"), 1)

                def mul(q):
                    dve.wait_ge(sem("s_exp"), 4 * t + q + 1)
                    if q == 0:
                        dve.wait_ge(sem("s_cbs"), t + 1)
                    e = es[:, q % 2, :].rearrange("p (a b) -> p a b", b=P)
                    dve.tensor_tensor(e, e, cbs[:, q // 2, :].unsqueeze(1).broadcast_to([P, 4, P]), ALU.mult).then_inc(sem("s_wm"), 1)

                def low(q):
                    dve.wait_ge(sem("s_whi"), 4 * t + q + 1)
                    hi, lo = (x[:, q % 2, :, :].rearrange("p a b -> p (a b)") for x in wl)
                    dve.tensor_tensor(lo, es[:, q % 2, :], hi.bitcast(F32), ALU.subtract).then_inc(sem("s_wlo"), 1)

                dve.wait_ge(sem(f"s_x_in{u}"), 8 * (t - u) + 16)
                if not first:
                    dve.wait_ge(sem("s_xlo"), t)
                dve.tensor_tensor(heads(xdt[:, :]), heads(xs[:, u, :]), by_head(dt[:, t, :]), ALU.mult).then_inc(sem("s_xdt"), 1)
                sub(0)
                sub(1)
                mul(0)
                dve.wait_ge(sem("s_off"), t + 1)
                dve.tensor_tensor(heads(y[:, u, :]), ps[:, 0:2, :].rearrange("p a (h c) -> p (a h) c", c=SHD), by_head(ecum[:, t, :]), ALU.mult).then_inc(sem("s_yo"), 1)
                mul(1)
                low(0)
                low(1)
                sub(2)
                sub(3)
                sums(t + 1)
                dve.tensor_tensor(heads(state[:, :]), heads(state[:, :]), by_head(cdec[:, t, :]), ALU.mult).then_inc(sem("s_dec"), 1)
                mul(2)
                if not first:
                    norm(t - 1, 1 - u)
                dve.wait_ge(sem("s_stp"), t + 1)
                dve.wait_ge(sem("s_dec"), t + 1)
                dve.tensor_tensor(state[:, :], ps[:, 0:2, :].rearrange("p a b -> p (a b)"), state[:, :], ALU.add).then_inc(sem("s_st"), 1)
                mul(3)
                dve.wait_ge(sem("s_sthi"), t + 2)
                dve.tensor_tensor(sth[1][:, :], state[:, :], sth[0][:, :].bitcast(F32), ALU.subtract).then_inc(sem("s_stlo"), 1)
                low(2)
                low(3)
                if not first:
                    turned(t - 1)
                dve.wait_ge(sem("s_xd"), t + 1)
                dve.wait_ge(sem("s_dg"), 4 * t + 4)
                dve.tensor_tensor(xd[:, :], ps[:, 2:4, :].rearrange("p a b -> p (a b)"), xd[:, :], ALU.add).then_inc(sem("s_yd"), 1)

            sums(0)
            cuts(10, RING)
            chunk(0, 0, True)
            with dve.Fori(0, NT // 2 - 1) as i:
                for u in (1, 0):
                    chunk(2 * i + 2 - u, u, False)
            chunk(LAST, 1, False)
            norm(LAST, 1)
            turned(LAST)



def phase_mix(k):
    nc, sem, m, ps, io = k.nc, k.sem, k.map, k.ps, k.io
    o = O_R
    k.hmT = []
    for s in ("hi", "lo"):
        t, o = m.at("hmT" + s, [P, KD, SEQ], F32R, o)
        k.hmT.append(t)
    hmT = k.hmT
    sT = []
    for s in ("hi", "lo"):
        t, o = m.at("m_sT" + s, [P, 2, KD, P], F32R, o)
        sT.append(t)
    mix, o = m.at("m_mix", [P, 2, D], F32, o)
    h, o = m.at("m_h", [P, 2, D], F32, o)
    hn, o = m.at("m_hn", [P, 2, D], F32, o)
    junk, o = m.at("m_junk", [P, D], F32, o)
    wrow, o = m.at("m_wrow", [P, D], F32, o)
    ss, v, s_, r, t1 = k.st[0], k.st[1], k.st[2], k.st[3], k.st[4]
    W = (k.whi, k.wlo)
    PASSES = ((0, 0), (0, 1), (1, 0))
    PAIRS = NT // 2
    rows = lambda a, t: a.rearrange("(t p) n -> t p n", p=P)[t]
    cols = lambda a, t: a.rearrange("(k p) (t n) -> t p k n", p=P, n=P)[t]

    with nc.Block() as block:
        @block.sync
        def _(sp):
            def load_left(t, u):
                for i in range(2):
                    sp.dma_start(sT[i][:, u, :, :].bitcast(F32), cols(k.d_ssm[i], t)).then_inc(sem(f"m_s_in{u}"), 16)

            def load_mix(t, u):
                sp.dma_start(mix[:, u, :], rows(k.d_mix, t)).then_inc(sem(f"m_mix_in{u}"), 16)

            def load_h(t, u):
                sp.dma_start(h[:, u, :], rows(io["x"][0], t)).then_inc(sem(f"m_h_in{u}"), 16)

            def store(t, u):
                sp.wait_ge(sem("m_h"), t + 1)
                sp.dma_start(rows(k.d_h, t), h[:, u, :]).then_inc(sem(f"m_sent{u}"), 16)

            load_left(0, 0)
            for n in range(RING + STAGES, 2 * RING):
                load_block(sp, k, n, k.wo_blocks[n])
            load_left(1, 1)
            for u in range(2):
                load_mix(u, u)
                load_h(u, u)
            sp.dma_start(wrow[:, :], io["norm_mix_post"][0].partition_broadcast(P)).then_inc(sem("m_w_in"), 16)
            with sp.Fori(0, PAIRS - 1) as i:
                for u in range(2):
                    sp.wait_ge(sem("m_mm"), 4 * i + 2 * u + 2)
                    load_left(2 * i + u + 2, u)
                for u in range(2):
                    store(2 * i + u, u)
                    load_mix(2 * i + u + 2, u)
                for u in range(2):
                    sp.wait_ge(sem("m_hn"), 2 * i + u + 1)
                    sp.wait_ge(sem(f"m_sent{u}"), 16 * i + 16)
                    load_h(2 * i + u + 2, u)
            for u in range(2):
                store(NT - 2 + u, u)
            for u in range(2):
                sp.wait_ge(sem(f"m_sent{u}"), 16 * PAIRS)

        @block.tensor
        def _(pe):
            def mm_tile(t, u, first):
                pe.wait_ge(sem(f"m_s_in{u}"), 32 if first else 16 * (t - u) + 32)
                for c in range(2):
                    if not first:
                        pe.wait_ge(sem("m_add"), 2 * t + c - 3)
                    for kk in range(KD):
                        if first and u == 0:
                            pe.wait_ge(sem("u_cut"), RING + KD * c + kk + 1)
                        for a, b in PASSES:
                            mm = pe.matmul(ps[:, 2 * u + c, :], sT[a][:, u, kk, :], W[b][:, KD * c + kk, :],
                                           start=(kk == 0 and a == 0 and b == 0), stop=(kk == KD - 1 and a == 1))
                    mm.then_inc(sem("m_mm"), 1)

            def turn_pair(i):
                for u in range(2):
                    pe.wait_ge(sem("m_hn"), 2 * i + u + 1)
                    for c in range(2):
                        pe.wait_ge(sem("m_lo"), 4 * i + 2 * u + c + 1)
                        for j in range(4):
                            kk = 4 * c + j
                            mm = pe.transpose(ps[:, 4 + 2 * u + c, P * j:P * j + P], hn[:, u, P * kk:P * kk + P], k.ident[:, :])
                        mm.then_inc(sem("m_turned"), 1)

            for u in range(2):
                mm_tile(u, u, True)
            with pe.Fori(0, PAIRS - 1) as i:
                for u in range(2):
                    mm_tile(2 * i + u + 2, u, False)
                turn_pair(i)
            turn_pair(PAIRS - 1)

        @block.gpsimd
        def _(pool):
            with pool.Fori(0, PAIRS) as i:
                for u in range(2):
                    pool.wait_ge(sem("m_scaled"), 2 * i + u + 1)
                    pool.wait_ge(sem(f"m_h_in{u}"), 16 * i + 16)
                    pool.tensor_tensor(h[:, u, :], mix[:, u, :], h[:, u, :], ALU.add).then_inc(sem("m_h"), 1)

        @block.scalar
        def _(act):
            for n in range(RING, 2 * RING):
                cut_hi(act, k, n)
            with act.Fori(0, PAIRS) as i:
                for u in range(2):
                    act.wait_ge(sem("m_add"), 4 * i + 2 * u + 2)
                    act.wait_ge(sem("m_sq"), 4 * i + u + 1)
                    act.activation(junk[:, :], mix[:, u, :], ACT.Square, accum_out=ss[:, u:u + 1]).then_inc(sem("m_sq"), 1)
                act.wait_ge(sem("m_v"), 2 * i + 1)
                act.activation(s_[:, 0:2], v[:, 0:2], ACT.Sqrt).then_inc(sem("m_sqrt"), 1)
                for u in range(2):
                    act.wait_ge(sem("m_h"), 2 * i + u + 1)
                    act.wait_ge(sem("m_sq"), 4 * i + u + 3)
                    act.activation(junk[:, :], h[:, u, :], ACT.Square, accum_out=ss[:, 2 + u:3 + u]).then_inc(sem("m_sq"), 1)
                act.wait_ge(sem("m_v"), 2 * i + 2)
                act.activation(s_[:, 2:4], v[:, 2:4], ACT.Sqrt).then_inc(sem("m_sqrt"), 1)
                act.wait_ge(sem("m_r"), i + 1)
                for u in range(2):
                    act.wait_ge(sem("m_turned"), 4 * i + 2 * u + 2)
                    act.activation(hn[:, u, :], h[:, u, :], ACT.Copy, scale=r[:, 2 + u:3 + u]).then_inc(sem("m_hn"), 1)
                for n in range(4):
                    act.wait_ge(sem("m_turned"), 4 * i + n + 5)
                    for j in range(4):
                        kk = 4 * (n % 2) + j
                        act.activation(hmT[0][:, kk, bass.ds(P * (2 * i + n // 2), P)], ps[:, 4 + n, P * j:P * j + P], ACT.Copy, scale=col(k, "mlp", kk)).then_inc(sem("m_hi"), 1)

        @block.vector
        def _(dve):
            dve.memset(ss[:, :], 0.0).then_inc(sem("m_sq"), 1)
            dve.memset(v[:, :], 1.0).then_inc(sem("m_lo"), 4)
            dve.memset(t1[:, :], 0.0).then_inc(sem("m_turned"), 4)
            for n in range(RING, 2 * RING):
                cut_lo(dve, k, n)

            def add_pair(t, by_pairs):
                for u in range(2):
                    dve.wait_ge(sem(f"m_mix_in{u}"), by_pairs + 16)
                    for c in range(2):
                        dve.wait_ge(sem("m_mm"), 2 * t + 2 * u + c + 1)
                        part = mix[:, u, 512 * c:512 * c + 512]
                        dve.tensor_tensor(part, ps[:, 2 * u + c, :], part, ALU.add).then_inc(sem("m_add"), 1)

            def chain(i):
                dve.wait_ge(sem("m_sq"), 4 * i + 3)
                rsqrt_before(dve, k, v[:, 0:2], ss[:, 0:2], 1.0 / D, "m_v", 1)
                rsqrt_after(dve, k, r[:, 0:2], v[:, 0:2], s_[:, 0:2], t1[:, 0:2], "m_sqrt", 2 * i + 1, "m_rs", 10 * i)
                for u in range(2):
                    dve.scalar_tensor_tensor(mix[:, u, :], mix[:, u, :], r[:, u:u + 1], wrow[:, :], ALU.mult, ALU.mult).then_inc(sem("m_scaled"), 1)
                dve.wait_ge(sem("m_sq"), 4 * i + 5)
                rsqrt_before(dve, k, v[:, 2:4], ss[:, 2:4], 1.0 / D, "m_v", 1)
                rsqrt_after(dve, k, r[:, 2:4], v[:, 2:4], s_[:, 2:4], t1[:, 2:4], "m_sqrt", 2 * i + 2, "m_rs", 10 * i + 5)
                dve.tensor_copy(t1[:, 4:6], r[:, 2:4]).then_inc(sem("m_r"), 1)

            def low_pair(i):
                for n in range(4):
                    dve.wait_ge(sem("m_hi"), 16 * i + 4 * n + 4)
                    at = bass.ds(P * (2 * i + n // 2), P)
                    for j in range(4):
                        kk = 4 * (n % 2) + j
                        mm = dve.scalar_tensor_tensor(hmT[1][:, kk, at], ps[:, 4 + n, P * j:P * j + P], col(k, "mlp", kk), hmT[0][:, kk, at].bitcast(F32),
                                                      ALU.mult, ALU.subtract)
                    mm.then_inc(sem("m_lo"), 1)

            add_pair(0, 0)
            dve.wait_ge(sem("m_w_in"), 16)
            with dve.Fori(0, PAIRS - 1) as i:
                chain(i)
                add_pair(2 * i + 2, 16 * i + 16)
                low_pair(i)
            chain(PAIRS - 1)
            low_pair(PAIRS - 1)



def phase_mlp(k):
    nc, sem, m, ps, io = k.nc, k.sem, k.map, k.ps, k.io
    GRP = 512
    GRPS = DFF // GRP
    FT = GRP // P
    HALF = RING // 2
    PASSES = ((0, 0), (0, 1), (1, 0))
    W = (k.whi, k.wlo)
    hmT = k.hmT
    _, o = m.at("hmT_again", [P, 2, KD, SEQ], F32, O_R)
    f1 = []
    for s in ("hi", "lo"):
        t, o = m.at("f1" + s, [P, FT, SEQ], F32R, o)
        f1.append(t)
    acc, o = m.at("acc", [P, NT, D], F32, o)
    relu = (m.at("relu", [P, 512], F32, 0)[0], k.spare)
    h, oh = m.at("e_h", [P, NT, D], F32, O_R)
    wrow, oh = m.at("e_wrow", [P, D], F32, oh)
    junk, oh = m.at("e_junk", [P, D], F32, oh)
    ss, v, s_, r, t1 = k.st[0], k.st[1], k.st[2], k.st[3], k.st[4]
    up = io["w_mlp_up"][0].rearrange("(k p) (g n) -> g k p n", p=P, n=GRP)
    down = io["w_mlp_down"][0].rearrange("(g j p) (c n) -> g j c p n", p=P, j=FT, n=512)
    k.fam = "v"
    DN = 2 * NT
    UP = 2 * FT

    def block_of(g, n):
        return up[g, n] if n < HALF else down[g, (n - HALF) // 2, (n - HALF) % 2]

    with nc.Block() as block:
        @block.sync
        def _(sp):
            for n in range(RING):
                load_block(sp, k, n, block_of(0, n))
            with sp.Fori(1, GRPS) as g:
                for n in range(RING):
                    sp.wait_ge(sem("v_cut"), RING * g + n - STAGES + 1)
                    sp.dma_start(k.stage[:, n % STAGES, :], block_of(g, n)).then_inc(sem(f"v_landed{n % STAGES}"), 16)
            sp.wait_ge(sem("v_up"), UP * GRPS)
            sp.dma_start(wrow[:, :], io["norm_mlp_post"][0].partition_broadcast(P)).then_inc(sem("e_w_in"), 16)
            for t in range(NT):
                sp.dma_start(h[:, t, :], k.d_h[P * t:P * t + P]).then_inc(sem("e_h_in"), 16)
            for t in range(NT):
                sp.wait_ge(sem("e_out"), t + 1)
                sp.dma_start(io["out"][0, P * t:P * t + P, :], h[:, t, :]).then_inc(sem("e_sent"), 16)
            sp.wait_ge(sem("e_sent"), 16 * NT)

        @block.gpsimd
        def _(pool):
            for n in range(RING):
                cut_block(pool, k, n, 512)
            with pool.Fori(1, GRPS) as g:
                for n in range(RING):
                    if n == 0:
                        pool.wait_ge(sem("v_up"), UP * g)
                    if n == HALF:
                        pool.wait_ge(sem("v_down"), DN * g)
                    cut_block(pool, k, n, 512, RING * g, 16 * (RING // STAGES) * g)
            pool.wait_ge(sem("e_h_in"), 16 * NT)
            for t in range(NT):
                pool.wait_ge(sem("e_scaled"), t + 1)
                pool.tensor_tensor(h[:, t, :], acc[:, t, :], h[:, t, :], ALU.add).then_inc(sem("e_out"), 1)

        @block.tensor
        def _(pe):
            def group(g, first):
                for c in range(2):
                    for j in range(FT):
                        n = FT * c + j
                        pe.wait_ge(sem("v_sq_out"), UP * g + n + 1)
                        for kk in range(KD):
                            if c == 0 and j == 0:
                                pe.wait_ge(sem("v_cut"), RING * g + kk + 1)
                            for a, b in PASSES:
                                mm = pe.matmul(ps[:, n % 2, :], W[a][:, kk, P * j:P * j + P], hmT[b][:, kk, 512 * c:512 * c + 512],
                                               start=(kk == 0 and a == 0 and b == 0), stop=(kk == KD - 1 and a == 1))
                        mm.then_inc(sem("v_up"), 1)
                pe.wait_ge(sem("v_cut"), RING * g + RING)
                for n in range(DN):
                    t, c = n // 2, n % 2
                    if n % FT == 0 and t in (0, NT // 2):
                        pe.wait_ge(sem("v_sq_out"), UP * g + 2 + (FT if t == 0 else UP))
                    pe.wait_ge(sem("v_added"), DN * g + n + 1)
                    for j in range(FT):
                        for a, b in PASSES:
                            mm = pe.matmul(ps[:, 2 + n % 4, :], f1[a][:, j, P * t:P * t + P], W[b][:, HALF + 2 * j + c, :],
                                           start=(j == 0 and a == 0 and b == 0), stop=(j == FT - 1 and a == 1))
                    mm.then_inc(sem("v_down"), 1)

            with pe.Fori(0, GRPS) as g:
                group(g, False)

        def where(n):
            return n % FT, slice(512 * (n // FT), 512 * (n // FT) + 512)

        @block.scalar
        def _(act):
            def highs(g):
                for n in range(UP):
                    j, at = where(n)
                    act.wait_ge(sem("v_up"), UP * g + n + 1)
                    act.activation(relu[n % 2][:, :], ps[:, n % 2, :], ACT.Relu).then_inc(sem("v_relu"), 1)
                    act.wait_ge(sem("v_sq"), UP * g + n + 1)
                    act.activation(f1[0][:, j, at], ps[:, n % 2, :], ACT.Copy).then_inc(sem("v_f1hi"), 1)

            with act.Fori(0, GRPS) as g:
                highs(g)
            for t in range(NT):
                act.wait_ge(sem("v_added"), 4 + DN * (GRPS - 1) + 2 * t + 2)
                if t == 0:
                    act.wait_ge(sem("v_up"), UP * GRPS)
                else:
                    act.wait_ge(sem("e_sq"), t)
                act.activation(junk[:, :], acc[:, t, :], ACT.Square, accum_out=ss[:, t:t + 1]).then_inc(sem("e_sq"), 1)
                act.wait_ge(sem("e_v"), t + 1)
                act.activation(s_[:, t:t + 1], v[:, t:t + 1], ACT.Sqrt).then_inc(sem("e_sqrt"), 1)

        @block.vector
        def _(dve):
            for t in range(NT):
                dve.memset(acc[:, t, :], 0.0).then_inc(sem("acc_set"), 1)
            dve.memset(ss[:, :], 0.0).then_inc(sem("v_sq_out"), 2)
            dve.memset(v[:, :], 1.0).then_inc(sem("v_added"), 4)
            dve.wait_ge(sem("acc_set"), NT)

            def squares(g):
                def square(n):
                    dve.wait_ge(sem("v_relu"), UP * g + n + 1)
                    bank = ps[:, n % 2, :]
                    dve.tensor_tensor(bank, bank, relu[n % 2][:, :], ALU.mult).then_inc(sem("v_sq"), 1)

                for n in range(UP):
                    j, at = where(n)
                    square(n)
                    dve.wait_ge(sem("v_f1hi"), UP * g + n + 1)
                    dve.tensor_tensor(f1[1][:, j, at], ps[:, n % 2, :], f1[0][:, j, at].bitcast(F32), ALU.subtract).then_inc(sem("v_sq_out"), 1)

            def add(g, n):
                dve.wait_ge(sem("v_down"), DN * g + n + 1)
                t, c = n // 2, n % 2
                part = acc[:, t, 512 * c:512 * c + 512]
                dve.tensor_tensor(part, ps[:, 2 + n % 4, :], part, ALU.add).then_inc(sem("v_added"), 1)

            with dve.Fori(0, GRPS - 1) as g:
                squares(g)
                for n in range(DN):
                    add(g, n)
            g = GRPS - 1
            squares(g)
            for t in range(NT):
                add(g, 2 * t)
                add(g, 2 * t + 1)
                if t == 0:
                    dve.wait_ge(sem("e_w_in"), 16)
                dve.wait_ge(sem("e_sq"), t + 1)
                rsqrt_before(dve, k, v[:, t:t + 1], ss[:, t:t + 1], 1.0 / D, "e_v", 1)
                rsqrt_after(dve, k, r[:, t:t + 1], v[:, t:t + 1], s_[:, t:t + 1], t1[:, t:t + 1], "e_sqrt", t + 1, "e_rs", 5 * t)
                dve.scalar_tensor_tensor(acc[:, t, :], acc[:, t, :], r[:, t:t + 1], wrow[:, :], ALU.mult, ALU.mult).then_inc(sem("e_scaled"), 1)


def build(nc, io):
    k = setup(nc, io)
    phase_norm(k)
    phase_project(k)
    phase_attend(k)
    k.sem.renew()
    phase_ssd(k)
    phase_mix(k)
    phase_mlp(k)


_INS = ["x", "meta_tokens", "w_in", "w_q_up", "w_kv_up", "dt_bias", "a_log", "d_skip", "ssm_norm", "w_out",
        "norm_mix_post", "w_mlp_up", "w_mlp_down", "norm_mlp_post"]


def _constants():
    inv = np.float32(10000.0) ** (-np.arange(0, ROPE, 2, dtype=np.float32) / np.float32(ROPE))
    ang = np.arange(POS, dtype=np.float32)[:, None] * inv.astype(np.float32)[None, :]
    table = np.concatenate([np.cos(ang), np.sin(ang)], axis=1).astype(np.float32)
    rope = np.zeros((P, NT + 1, ROPE), np.float32)
    rope[:, :NT] = table[META:].reshape(NT, P, ROPE).transpose(1, 0, 2)
    rope[:META, NT] = table[:META]
    i = np.arange(P)
    ahead = i[:, None] <= i[None, :]
    return {
        "c_ident": np.eye(P, dtype=np.float32),
        "c_tri": ahead.astype(np.float32),
        "c_mask": np.where(ahead, 0.0, NEG).astype(np.float32),
        "c_rope": rope,
    }


def _arrays(inputs):
    arrays = {n: np.ascontiguousarray(inputs[n]) for n in _INS}
    columns = lambda a: np.asarray(a).reshape(-1, P).T
    arrays["c_par"] = np.ascontiguousarray(np.concatenate([
        columns(inputs["norm_mix_pre"]), columns(inputs["norm_mlp_pre"]), columns(inputs["q_a_norm"]), columns(inputs["kv_a_norm"]),
        np.asarray(inputs["conv_w"])[0].reshape(4, CONVW // P, P).transpose(2, 1, 0).reshape(P, -1), columns(inputs["conv_b"])], axis=1))
    return {**arrays, **_constants()}


def _declare(nc, arrays):
    io = {n: nc.dram_tensor(n, a.shape, mybir.dt.from_np(a.dtype), kind="ExternalInput").ap() for n, a in arrays.items()}
    io["out"] = nc.dram_tensor("out", (1, SEQ, D), F32, kind="ExternalOutput").ap()
    return io


def kernel(**inputs):
    import concourse.bacc as bacc
    from concourse.bass_utils import run_bass_kernel_spmd

    arrays = _arrays(inputs)
    nc = bacc.Bacc("TRN2", target_bir_lowering=False, num_devices=1)
    build(nc, _declare(nc, arrays))
    r = run_bass_kernel_spmd(nc, [arrays], core_ids=[0])
    return r.results[0]["out"]
```

```python
import numpy as np

import concourse.bass as bass
from concourse import mybir

F32 = mybir.dt.float32
F32R = mybir.dt.float32r
BF16 = mybir.dt.bfloat16
ALU = mybir.AluOpType
ACT = mybir.ActivationFunctionType
AX = mybir.AxisListType

P = 128
D = 1024
SEQ = 1024
META = 16
POS = SEQ + META
KD = D // P
NT = SEQ // P
QL, KVL, ROPE, NOPE, VH = 384, 256, 64, 128, 128
HEADS = 8
SSMW, GROUPS, STATE, SH, SHD = 1024, 2, 128, 16, 64
CONVW = SSMW + 2 * GROUPS * STATE
DFF = 4096
OFF_KV, OFF_KR, OFF_Z, OFF_X, OFF_DT = QL, QL + KVL, QL + KVL + ROPE, QL + KVL + ROPE + SSMW, QL + KVL + ROPE + SSMW + CONVW
SCALE = float((NOPE + ROPE) ** -0.5)
EPS = 1e-6
NEG = -1.0e30
TC = [(0, 348), (348, 346), (694, 346)]
RING = 16
STAGES = 4
AHEAD = KD


class Sems:

    def __init__(self, nc):
        self.nc, self.of = nc, {}

    def __call__(self, name):
        if name not in self.of:
            self.of[name] = self.nc.alloc_semaphore(name)
        return self.of[name]

    def renew(self, keep):
        self.nc.clear_and_free_semaphores([s for n, s in self.of.items() if n not in keep])
        self.of = {n: s for n, s in self.of.items() if n in keep}
        self.nc.all_engine_barrier()


class Map:

    def __init__(self, nc):
        self.nc, self.base = nc, (nc.sbuf_base + 31) // 32 * 32

    def at(self, name, shape, dt, offset):
        size = (int(np.prod(shape[1:])) * mybir.dt.size(dt) + 31) // 32 * 32
        assert self.base + offset + size <= self.nc.sbuf_usable_end, (name, offset, size)
        return self.nc.alloc_sbuf_tensor_at(name, list(shape), dt, offset=self.base + offset), offset + size


PARAM = {}
_at = 0
for _n, _w in (("pre", KD), ("mlp", KD), ("qa", QL // P), ("kva", KVL // P), ("convw", 4 * CONVW // P), ("convb", CONVW // P)):
    PARAM[_n] = _at
    _at += _w
NPARAM = _at

O_RING = 6144
O_STAGE = O_RING + RING * 512 * 8
O_R = O_STAGE + STAGES * 512 * 4
O_DT = 212256
O_TABLES = O_DT - 3520


class K:
    pass


def setup(nc, io):
    k = K()
    k.nc, k.io, k.sem, m = nc, io, Sems(nc), Map(nc)
    k.map = m
    o = 0
    k.ident, o = m.at("ident", [P, P], F32, o)
    k.par, o = m.at("par", [P, NPARAM], F32, o)
    k.st = []
    for n in range(6):
        t, o = m.at(f"stat{n}", [P, 24], F32, o)
        k.st.append(t)
    k.zero, o = m.at("zero", [P, 8], F32, o)
    k.heads, o = m.at("heads", [P, SH + NT], F32, o)
    k.o_relu = o
    k.ident_b, o = m.at("ident_b", [P, P], BF16, o)
    k.mask_b, o = m.at("mask_b", [P, P], BF16, o)
    k.tri, o = m.at("tri", [P, P], F32R, o)
    k.ones, o = m.at("ones", [P, P], F32R, o)
    k.spare, o = m.at("spare", [P, 640], F32, o)
    assert o <= O_RING
    ring, o = m.at("ring", [P, RING, 2, 512], F32R, O_RING)
    k.whi, k.wlo = ring[:, :, 0, :], ring[:, :, 1, :]
    k.stage, o = m.at("stage", [P, STAGES, 512], F32, O_STAGE)
    k.ps = nc.alloc_psum_tensor("ps", [P, 8, 512], F32)
    dr = lambda n, s, dt: nc.dram_tensor(n, s, dt, kind="Internal").ap()
    k.d_x = dr("d_x", (SEQ, SSMW), F32)
    k.d_xm = dr("d_xm", (META, SSMW), F32)
    k.d_z = dr("d_z", (SEQ, SSMW), F32)
    pair = lambda n, s: [dr(n + "hi", s, F32), dr(n + "lo", s, F32)]
    k.d_bt = pair("d_bt", (GROUPS * STATE, SEQ))
    k.d_ct = pair("d_ct", (GROUPS * STATE, SEQ))
    k.d_b = pair("d_b", (SEQ, GROUPS * STATE))
    k.d_bm = pair("d_bm", (META, GROUPS * STATE))
    k.d_qr = pair("d_qr", (HEADS * ROPE, SEQ))
    k.d_att = pair("d_att", (HEADS * VH, SEQ))
    k.d_ssm = pair("d_ssm", (SSMW, SEQ))
    k.d_mix = dr("d_mix", (SEQ, D), F32)
    k.d_h = dr("d_h", (SEQ, D), F32)
    k.blocks = []
    return k


def col(k, name, n):
    return k.par[:, PARAM[name] + n:PARAM[name] + n + 1]



def load_block(sp, k, fam, n, src):
    if n >= STAGES:
        sp.wait_ge(k.sem(fam + "_cut"), n - STAGES + 1)
    width = src.shape[-1]
    sp.dma_start(k.stage[:, n % STAGES, 0:width], src).then_inc(k.sem(f"{fam}_landed{n % STAGES}"), 16)


def cut_block(pool, k, fam, n, width, turn=0, by_stages=0):
    pool.wait_ge(k.sem(f"{fam}_landed{n % STAGES}"), 16 * (n // STAGES + 1) + by_stages)
    src = k.stage[:, n % STAGES, 0:width]
    hi, lo = k.whi[:, n % RING, 0:width], k.wlo[:, n % RING, 0:width]
    pool.tensor_tensor(hi, src, k.zero[:, 0:1].broadcast_to([P, width]), ALU.add).then_inc(k.sem(fam + "_hi"), 1)
    pool.wait_ge(k.sem(fam + "_hi"), n + 1 + turn)
    pool.tensor_tensor(lo, src, hi.bitcast(F32), ALU.subtract).then_inc(k.sem(fam + "_cut"), 1)


def cut_hi(act, k, fam, n):
    act.wait_ge(k.sem(f"{fam}_landed{n % STAGES}"), 16 * (n // STAGES + 1))
    act.activation(k.whi[:, n % RING, :], k.stage[:, n % STAGES, :], ACT.Copy).then_inc(k.sem(fam + "_hi"), 1)


def cut_lo(dve, k, fam, n):
    dve.wait_ge(k.sem(fam + "_hi"), n + 1)
    dve.tensor_tensor(k.wlo[:, n % RING, :], k.stage[:, n % STAGES, :], k.whi[:, n % RING, :].bitcast(F32), ALU.subtract).then_inc(k.sem(fam + "_cut"), 1)


def head_weights(sp, k, h):
    wqh = k.io["w_q_up"][0].rearrange("(k p) (h c) -> h p k c", p=P, h=HEADS)
    wkh = k.io["w_kv_up"][0].rearrange("(k p) (h c) -> h p k c", p=P, h=HEADS)
    sp.dma_start(k.wq_f[:, :, :], wqh[h][:, :, 0:NOPE]).then_inc(k.sem("a_q_in"), 16)
    sp.dma_start(k.wkv_f[:, :, :], wkh[h]).then_inc(k.sem("a_kv_in"), 16)


def cut_head(pool, k, h, used=None):
    for n, (src, dst, name) in enumerate(((k.wq_f, k.wq, "a_q_in"), (k.wkv_f, k.wkv, "a_kv_in"))):
        pool.wait_ge(k.sem(name), 16 * h + 16)
        if used:
            used(n)
        a, hi, lo = (x[:, :, :].rearrange("p a b -> p (a b)") for x in (src, *dst))
        pool.tensor_tensor(hi, a, k.zero[:, 0:1].broadcast_to([P, a.shape[-1]]), ALU.add).then_inc(k.sem("a_cut"), 1)
        pool.wait_ge(k.sem("a_cut"), 4 * h + 2 * n + 1)
        pool.tensor_tensor(lo, a, hi.bitcast(F32), ALU.subtract).then_inc(k.sem("a_cut"), 1)



def phase_norm(k):
    nc, sem, m, ps, io = k.nc, k.sem, k.map, k.ps, k.io
    k.hT = []
    o = O_R
    for s in ("hi", "lo"):
        t, o = m.at("hT" + s, [P, KD, POS], F32R, o)
        k.hT.append(t)
    k.o_work = o
    xt, o = m.at("xt", [P, NT + 1, D], F32, o)
    cst, o = m.at("cst", [P, 2, P], F32, o)
    mtmp, o = m.at("mtmp", [P, KD, META], F32, o)
    ss, v, s_, r, t1 = k.st[0], k.st[1], k.st[2], k.st[3], k.st[4]
    hT = k.hT
    win = io["w_in"][0]
    wqu = io["w_q_up"][0]
    cols = [(OFF_X, 512), (OFF_X + 512, 512), (OFF_X + 1024, 512), (0, QL), (OFF_KV, KVL + ROPE), (OFF_Z, 512), (OFF_Z + 512, 512)]
    k.blocks = [win[P * kk:P * kk + P, c:c + w] for c, w in cols for kk in range(KD)]
    qr_view = wqu.rearrange("k (h c) -> k h c", h=HEADS)[:, :, NOPE:NOPE + ROPE]
    k.qr_blocks = [qr_view[P * kk:P * kk + P] for kk in range(QL // P)]

    with nc.Block() as block:
        @block.sync
        def _(sp):
            sp.dma_start(k.ident[:, :], io["c_ident"]).then_inc(sem("c_in"), 16)
            sp.dma_start(cst[:, 0, :], io["c_tri"]).then_inc(sem("c_in"), 16)
            sp.dma_start(cst[:, 1, :], io["c_mask"]).then_inc(sem("c_in"), 16)
            sp.dma_start(k.par[:, :], io["c_par"]).then_inc(sem("c_in"), 16)
            sp.dma_start(k.heads[:, :], io["c_heads"]).then_inc(sem("c_in"), 16)
            def load_x(t):
                sp.dma_start(xt[:, t, :], io["x"][0, P * t:P * t + P, :]).then_inc(sem(f"x_in{t}"), 16)

            for t in range(NT):
                load_x(t)
            sp.dma_start(xt[0:META, NT, :], io["meta_tokens"]).then_inc(sem(f"x_in{NT}"), 16)
            for n in range(AHEAD + STAGES):
                load_block(sp, k, "w", n, k.blocks[n])

        @block.gpsimd
        def _(pool):
            pool.memset(k.zero[:, :], 0.0).then_inc(sem("zeroed"), 1)
            pool.wait_ge(sem("zeroed"), 1)
            for n in range(AHEAD):
                cut_block(pool, k, "w", n, k.blocks[n].shape[-1])

        @block.scalar
        def _(act):
            def square(t):
                rows = P if t < NT else META
                act.wait_ge(sem(f"x_in{t}"), 16)
                if t == 0:
                    act.wait_ge(sem("ss_set"), 1)
                if t >= 1:
                    act.wait_ge(sem("sq"), t)
                act.activation(ps[0:rows, 6:8, :].rearrange("p a b -> p (a b)"), xt[0:rows, t, :], ACT.Square,
                               accum_out=ss[0:rows, t:t + 1]).then_inc(sem("sq"), 1)

            def root(half, part):
                act.wait_ge(sem("v"), half + 1)
                act.activation(s_[:, part], v[:, part], ACT.Sqrt).then_inc(sem("sqrt"), 1)

            for t in range(NT // 2):
                square(t)
            root(0, slice(0, NT // 2))
            act.wait_ge(sem("c_in"), 80)
            after = {1: 4, 3: 5, 4: 6, 5: 7, 7: 8}
            for n in range(2 * KD):
                half, kk = n // KD, n % KD
                act.wait_ge(sem("turned"), n + 1)
                c0 = META + 512 * half
                act.activation(hT[0][:, kk, c0:c0 + 512], ps[:, n % 4, :], ACT.Copy, scale=col(k, "pre", kk)).then_inc(sem("t_hi"), 1)
                if n in after:
                    square(after[n])
                if n == KD - 1:
                    root(1, slice(NT // 2, NT + 1))
            act.wait_ge(sem("mt"), 1)
            act.activation(hT[0][:, :, 0:META], mtmp[:, :, :], ACT.Copy).then_inc(sem("t_hi"), 1)

        @block.vector
        def _(dve):
            dve.memset(ss[:, :], 1.0).then_inc(sem("ss_set"), 1)
            dve.wait_ge(sem("c_in"), 80)
            dve.tensor_copy(k.ident_b[:, :], k.ident[:, :]).then_inc(sem("consts"), 1)
            dve.tensor_copy(k.mask_b[:, :], cst[:, 1, :]).then_inc(sem("consts"), 1)
            dve.tensor_copy(k.tri[:, :], cst[:, 0, :]).then_inc(sem("consts"), 1)
            dve.tensor_scalar(k.ones[:, :], cst[:, 0, :], 0.0, 1.0, ALU.mult, ALU.add).then_inc(sem("consts"), 1)
            def scaled(half):
                part = slice(0, NT // 2) if half == 0 else slice(NT // 2, NT + 1)
                dve.wait_ge(sem("sq"), part.stop)
                rsqrt_before(dve, k, v[:, part], ss[:, part], 1.0 / D, "v", 1)
                rsqrt_after(dve, k, r[:, part], v[:, part], s_[:, part], t1[:, part], "sqrt", half + 1, "rs1", 5 * half)
                for t in range(part.start, part.stop):
                    rows = P if t < NT else META
                    dve.tensor_scalar(xt[0:rows, t, :], xt[0:rows, t, :], r[0:rows, t:t + 1], None, ALU.mult).then_inc(sem("xn"), 1)

            scaled(0)
            for n in range(2 * KD):
                if n == KD:
                    scaled(1)
                half, kk = n // KD, n % KD
                dve.wait_ge(sem("t_hi"), n + 1)
                c0 = META + 512 * half
                dve.scalar_tensor_tensor(hT[1][:, kk, c0:c0 + 512], ps[:, n % 4, :], col(k, "pre", kk), hT[0][:, kk, c0:c0 + 512].bitcast(F32),
                                         ALU.mult, ALU.subtract).then_inc(sem("t_lo"), 1)
            dve.wait_ge(sem("turned"), 2 * KD + 1)
            w = k.par[:, PARAM["pre"]:PARAM["pre"] + KD].unsqueeze(2).broadcast_to([P, KD, META])
            dve.tensor_tensor(mtmp[:, :, :], ps[:, 0, 0:P].rearrange("p (a b) -> p a b", a=KD), w, ALU.mult).then_inc(sem("mt"), 1)
            dve.wait_ge(sem("t_hi"), 2 * KD + 1)
            dve.wait_ge(sem("mt"), 1)
            dve.tensor_tensor(hT[1][:, :, 0:META], mtmp[:, :, :], hT[0][:, :, 0:META].bitcast(F32), ALU.subtract).then_inc(sem("t_lo"), 1)

        @block.tensor
        def _(pe):
            pe.wait_ge(sem("c_in"), 80)
            for n in range(2 * KD):
                half, kk = n // KD, n % KD
                pe.wait_ge(sem("xn"), 4 * half + 4)
                if n >= 4:
                    pe.wait_ge(sem("t_lo"), n - 3)
                for i in range(4):
                    mm = pe.transpose(ps[:, n % 4, P * i:P * i + P], xt[:, 4 * half + i, P * kk:P * kk + P], k.ident[:, :])
                mm.then_inc(sem("turned"), 1)
            pe.wait_ge(sem("xn"), NT + 1)
            pe.wait_ge(sem("t_lo"), 2 * KD - 3)
            for kk in range(KD):
                mm = pe.transpose(ps[:, 0, META * kk:META * kk + META], xt[0:META, NT, P * kk:P * kk + P], k.ident[0:META, 0:META])
            mm.then_inc(sem("turned"), 1)


def rsqrt_before(dve, k, v, ss, scale, name, count):
    dve.tensor_scalar(v, ss, scale, EPS, ALU.mult, ALU.add).then_inc(k.sem(name), 1)


def rsqrt_after(dve, k, r, v, s, t, name, count, own, base=0):
    c = k.sem(own)
    dve.wait_ge(k.sem(name), count)
    dve.reciprocal(r, s).then_inc(c, 1)
    dve.wait_ge(c, base + 1)
    dve.tensor_tensor(t, r, r, ALU.mult).then_inc(c, 1)
    dve.wait_ge(c, base + 2)
    dve.tensor_tensor(t, t, v, ALU.mult).then_inc(c, 1)
    dve.wait_ge(c, base + 3)
    dve.tensor_scalar(t, t, -0.5, 1.5, ALU.mult, ALU.add).then_inc(c, 1)
    dve.wait_ge(c, base + 4)
    dve.tensor_tensor(r, r, t, ALU.mult).then_inc(c, 1)
    dve.wait_ge(c, base + 5)



NX = CONVW // P
NXT = NX - GROUPS


def phase_project(k):
    nc, sem, m, ps, io, hT = k.nc, k.sem, k.map, k.ps, k.io, k.hT
    o = k.o_work
    pre, o = m.at("pre", [P, 2, POS + 4], F32, o)
    acc, o = m.at("conv_acc", [P, 2, POS], F32, o)
    xc, o = m.at("xc", [P, 2, POS], F32, o)
    o1 = o
    xt, o = m.at("x_tok", [P, 2, NT + 1, P], F32, o)
    fb, o = [], o
    for s in ("hi", "lo"):
        t, o = m.at("bc" + s, [P, SEQ], F32R, o)
        fb.append(t)
    zs, o = m.at("zs", [P, 4, 512], F32, o)
    o_top = o
    bt = []
    for s in ("hi", "lo"):
        t, o = m.at("btok" + s, [P, NT + 1, P], F32R, o)
        bt.append(t)
    oc = k.o_work
    cqs, oc = m.at("cqs", [P, NT, QL], F32, oc)
    cks, oc = m.at("cks", [P, NT + 1, KVL + ROPE], F32, oc)
    assert oc <= o1
    oc = o1
    kro, oc = m.at("kro", [P, NT + 1, P], F32, oc)
    ta, oc = m.at("rot_a", [P, 288], F32, oc)
    tb, oc = m.at("rot_b", [P, 288], F32, oc)
    junk, oc = m.at("junk", [P, QL], F32, oc)
    T9 = [P, NT + 1, SH]
    pa, oc = m.at("p_a", T9, F32, oc)
    pb, oc = m.at("p_b", T9, F32, oc)
    pc, oc = m.at("p_c", T9, F32, oc)
    tc, oc = m.at("rot_c", [P, 256], F32, oc)
    td, oc = m.at("rot_d", [P, 256], F32, oc)
    assert oc <= o_top
    k.da = []
    od = O_TABLES
    for s in ("hi", "lo"):
        t, od = m.at("da" + s, T9, F32R, od)
        k.da.append(t)
    k.acum, od = m.at("acum", T9, F32, od)
    k.ecum, od = m.at("ecum", T9, F32, od)
    k.dend, od = m.at("dend", T9, F32, od)
    k.cdec, od = m.at("cdec", T9, F32, od)
    k.dsk, od = m.at("dskip", [P, SH], F32, od)
    assert od <= O_DT
    rope, o = m.at("rope", [P, NT + 1, ROPE], F32, o)
    assert o <= O_TABLES
    wdt = k.spare[:, 0:P].rearrange("p (k n) -> p k n", n=SH)
    dtb, av = k.spare[:, P:P + SH], k.spare[:, P + SH:P + 2 * SH]
    o = O_DT
    k.dt, o = m.at("dt", [P, NT + 1, SH], F32, o)
    oh = O_R
    k.cqT, k.ckT, k.krT, k.qrT = [], [], [], []
    for lst, name, shape in ((k.cqT, "cqT", [P, QL // P, SEQ]), (k.ckT, "ckT", [P, KVL // P, POS]), (k.krT, "krT", [P, POS])):
        for s in ("hi", "lo"):
            t, oh = m.at(name + s, shape, F32R, oh)
            lst.append(t)
    k.o_lat = oh
    k.wq, k.wkv = [], []
    ow = O_RING + 59648
    for s in ("hi", "lo"):
        t, ow = m.at("wq" + s, [P, QL // P, NOPE], F32R, ow)
        k.wq.append(t)
    k.wq_f, ow = m.at("wq_f", [P, QL // P, NOPE], F32, ow)
    assert ow <= O_STAGE
    ow = O_R + 120192
    k.o_wkv = ow
    for s in ("hi", "lo"):
        t, ow = m.at("wkv" + s, [P, KVL // P, NOPE + VH], F32R, ow)
        k.wkv.append(t)
    k.wkv_f, ow = m.at("wkv_f", [P, KVL // P, NOPE + VH], F32, ow)
    assert ow <= O_TABLES
    mt, oh = m.at("mtmp2", [P, 3, META], F32, oh)
    qro, oh = m.at("qro", [P, 2, HEADS, ROPE], F32, oh)
    for s in ("hi", "lo"):
        t, oh = m.at("qrT" + s, [P, 2, 4, P], F32R, oh)
        k.qrT.append(t)
    assert oh <= k.o_work
    ss, v, s_, r, t1 = k.st[0], k.st[1], k.st[2], k.st[3], k.st[4]
    nb = len(k.blocks)
    W = (k.whi, k.wlo)
    PASSES = ((0, 0), (0, 1), (1, 0))
    NW = NT + NT + 1
    KQ, KK = QL // P, KVL // P

    def chunk_used(eng, c):
        if c < 3:
            eng.wait_ge(sem("x_done"), 4 * c + 4)
        elif c == 3:
            eng.wait_ge(sem("cq_done"), NT)
        elif c == 4:
            eng.wait_ge(sem("ck_done"), NT + 1)
        else:
            eng.wait_ge(sem("z_done"), NT * (c - 4))

    def rotate_half(eng, t, half, a, b):
        eng.wait_ge(sem("qr_raw"), t + 1)
        if t == 0:
            eng.wait_ge(sem("rope_in"), 16)
            eng.wait_ge(sem("kro_done"), 2)
        q = zs[:, t % 4, :].rearrange("p (h c) -> p h c", c=ROPE)
        x = (q[:, :, 0:32], q[:, :, 32:64])
        cos = rope[:, t, 0:32].unsqueeze(1).broadcast_to([P, HEADS, 32])
        sin = rope[:, t, 32:64].unsqueeze(1).broadcast_to([P, HEADS, 32])
        step, done = sem(f"qro_step{half}"), sem(f"qro_done{half}")
        a3, b3 = (s[:, 0:256].rearrange("p (t c) -> p t c", c=32) for s in (a, b))
        if t:
            eng.wait_ge(done, t)
        if t >= 2:
            eng.wait_ge(sem("qr_turned"), t - 1)
        eng.tensor_tensor(a3, x[half], cos, ALU.mult).then_inc(step, 1)
        eng.tensor_tensor(b3, x[1 - half], sin, ALU.mult).then_inc(step, 1)
        eng.wait_ge(step, 2 * t + 2)
        eng.tensor_tensor(qro[:, t % 2, :, 32 * half:32 * half + 32], a3, b3, ALU.add if half else ALU.subtract).then_inc(done, 1)

    with nc.Block() as block:
        @block.sync
        def _(sp):
            sp.dma_start(rope[:, :, :], io["c_rope"]).then_inc(sem("rope_in"), 16)
            sp.dma_start(wdt, io["w_in"][0, :, OFF_DT:OFF_DT + SH].rearrange("(k p) n -> p k n", p=P)).then_inc(sem("wdt_in"), 16)
            sp.dma_start(dtb, io["dt_bias"][0].partition_broadcast(P)).then_inc(sem("p_in"), 16)
            sp.dma_start(av, io["a_log"][0].partition_broadcast(P)).then_inc(sem("p_in"), 16)
            sp.dma_start(k.dsk[:, :], io["d_skip"][0].partition_broadcast(P)).then_inc(sem("p_in"), 16)
            loaded = [AHEAD + STAGES]

            def loads(until):
                for n in range(loaded[0], until):
                    if n < nb:
                        load_block(sp, k, "w", n, k.blocks[n])
                    else:
                        sp.wait_ge(sem("w_cut"), n - STAGES + 1)
                        sp.dma_start(k.stage[:, n % STAGES, :].rearrange("p (h c) -> p h c", h=HEADS),
                                     k.qr_blocks[n - nb]).then_inc(sem(f"w_landed{n % STAGES}"), 16)
                loaded[0] = max(until, loaded[0])

            loads(RING + STAGES)
            for f in range(NX):
                q = f - 2
                if 0 <= q < NXT:
                    sp.wait_ge(sem("xt1_out"), q + 1)
                    sp.wait_ge(sem("xt2_out"), q + 1)
                if 0 <= q < KD:
                    sent = sem(f"xt_sent{q % 2}")
                    sp.dma_start(k.d_x[:, P * q:P * q + P].rearrange("(t p) n -> p t n", p=P), xt[:, q % 2, 0:NT, :]).then_inc(sent, 16)
                    sp.dma_start(k.d_xm[:, P * q:P * q + P], xt[0:META, q % 2, NT, :]).then_inc(sent, 16)
                elif 0 <= q < NXT:
                    for i in range(2):
                        sp.dma_start(k.d_bm[i][:, P * (q - KD):P * (q - KD) + P], bt[i][0:META, NT, :].bitcast(F32)).then_inc(sem("btm_sent"), 16)
                g = f - 1 - KD
                if 0 <= g < GROUPS:
                    sp.wait_ge(sem("xt0_out"), f)
                    sp.wait_ge(sem("xt1_out"), f)
                    for i in range(2):
                        sp.dma_start(k.d_b[i][:, P * g:P * g + P].rearrange("(t p) n -> p t n", p=P),
                                     bt[i][:, 0:NT, :].bitcast(F32)).then_inc(sem("bt_sent"), 16)
                if f >= KD:
                    sp.wait_ge(sem("bc_lo"), f - KD + 1)
                    d = k.d_bt if f < KD + GROUPS else k.d_ct
                    g = (f - KD) % GROUPS
                    for i in range(2):
                        sp.dma_start(d[i][P * g:P * g + P, :], fb[i][:, :].bitcast(F32)).then_inc(sem("bc_sent"), 16)
                loads({4: 24, 5: 28, 8: 30, 9: 33, 10: 36}.get(f, 0))
            loads(nb)
            for g in range(2 * NT):
                c, t = g // NT, g % NT
                sp.wait_ge(sem("zs_done"), g + 1)
                sp.dma_start(k.d_z[P * t:P * t + P, 512 * c:512 * c + 512], zs[:, g % 4, :]).then_inc(sem(f"z_sent{g % 4}"), 16)
                if g == NT:
                    loads(nb + KQ)
            for name in ("bt_sent", "btm_sent"):
                sp.wait_ge(sem(name), 32 * GROUPS)
            head_weights(sp, k, 0)
            for t in range(NT):
                sp.wait_ge(sem("qrT_lo"), t + 1)
                for i in range(2):
                    sp.dma_start(k.d_qr[i][:, P * t:P * t + P].rearrange("(a p) n -> p a n", p=P),
                                 k.qrT[i][:, t % 2, :, :].bitcast(F32)).then_inc(sem(f"qr_sent{t % 2}"), 16)
            for q in range(4):
                sp.wait_ge(sem(f"z_sent{q}"), 16 * 4)
            for name in ("bt_sent", "btm_sent"):
                sp.wait_ge(sem(name), 32 * GROUPS)
            sp.wait_ge(sem("bc_sent"), 32 * 2 * GROUPS)


        @block.gpsimd
        def _(pool):
            for n in range(AHEAD, nb + KQ):
                if n % 8 == 0 and n >= RING:
                    chunk_used(pool, n // 8 - 2)
                cut_block(pool, k, "w", n, k.blocks[n].shape[-1] if n < nb else 512)
            cut_head(pool, k, 0)
            for t in range(NT):
                rotate_half(pool, t, 1, tc, td)

        @block.tensor
        def _(pe):
            def turn_x(f, parts):
                pe.wait_ge(sem("xc_done"), f + 1)
                for part in parts:
                    bank = (6, 7, 6)[part]
                    if part == 0 and f:
                        pe.wait_ge(sem("xt2_out"), f)
                    if part == 1 and f:
                        pe.wait_ge(sem("xt1_out"), f)
                    if part == 2:
                        pe.wait_ge(sem("xt0_out"), f + 1)
                        mm = pe.transpose(ps[:, 6, 0:P], xc[:, f % 2, 0:P], k.ident[:, :])
                    else:
                        for i in range(4):
                            c0 = META + P * (4 * part + i)
                            mm = pe.transpose(ps[:, bank, P * i:P * i + P], xc[:, f % 2, c0:c0 + P], k.ident[:, :])
                    mm.then_inc(sem("x_turned"), 1)

            for f in range(NX):
                c, j = f // 4, f % 4
                base = 3 * (f % 2)
                if f >= 2:
                    pe.wait_ge(sem("pre_out"), 3 * (f - 1))
                for kk in range(KD):
                    if kk == 2 and 2 <= f <= NXT + 1:
                        turn_x(f - 2, (2,))
                    if j == 0:
                        pe.wait_ge(sem("w_cut"), 8 * c + kk + 1)
                    for a, b in PASSES:
                        for q, (c0, w) in enumerate(TC):
                            mm = pe.matmul(ps[:, base + q, 0:w], W[a][:, (8 * c + kk) % RING, P * j:P * j + P], hT[b][:, kk, c0:c0 + w],
                                           start=(kk == 0 and (a, b) == (0, 0)), stop=(kk == KD - 1 and a == 1))
                mm.then_inc(sem("x_done"), 1)
                if 1 <= f <= NXT:
                    turn_x(f - 1, (0, 1))
            for t in range(NT):
                if t < 4:
                    pe.wait_ge(sem("pre_out"), 3 * NX - (3 if t < 3 else 0))
                else:
                    pe.wait_ge(sem("cq_out"), t - 3)
                for kk in range(KD):
                    if t == 0:
                        pe.wait_ge(sem("w_cut"), 24 + kk + 1)
                    for a, b in PASSES:
                        mm = pe.matmul(ps[:, t % 4, 0:QL], hT[a][:, kk, META + P * t:META + P * t + P], W[b][:, (24 + kk) % RING, 0:QL],
                                       start=(kk == 0 and (a, b) == (0, 0)), stop=(kk == KD - 1 and a == 1))
                mm.then_inc(sem("cq_done"), 1)
            pe.wait_ge(sem("wdt_cut"), 2)
            for t in range(NT + 1):
                if t < 4:
                    pe.wait_ge(sem("cq_out"), NT - 3 + t)
                else:
                    pe.wait_ge(sem("ck_out"), t - 3)
                c0 = META + P * t if t < NT else 0
                w = KVL + ROPE + SH
                for kk in range(KD):
                    if t == 0:
                        pe.wait_ge(sem("w_cut"), 32 + kk + 1)
                    for a, b in PASSES:
                        mm = pe.matmul(ps[:, t % 4, 0:w], hT[a][:, kk, c0:c0 + P], W[b][:, (32 + kk) % RING, 0:w],
                                       start=(kk == 0 and (a, b) == (0, 0)), stop=(kk == KD - 1 and a == 1))
                mm.then_inc(sem("ck_done"), 1)
            def dt_sums():
                pe.wait_ge(sem("p_da"), 2)
                pe.wait_ge(sem("pre_out"), 3 * NX)
                n = NT * SH
                for bank, lhs in ((4, k.tri), (5, k.ones)):
                    for a in range(2):
                        pe.matmul(ps[:, bank, 0:n], lhs[:, :], k.da[a][:, 0:NT, :].rearrange("p a b -> p (a b)"), start=(a == 0), stop=(a == 1))
                    for a in range(2):
                        mm = pe.matmul(ps[:, bank, n:n + SH], lhs[0:META, :], k.da[a][0:META, NT, :], start=(a == 0), stop=(a == 1))
                mm.then_inc(sem("p_sums"), 1)

            for c in (5, 6):
                for t in range(NT):
                    g = NT * (c - 5) + t
                    if g < 4:
                        pe.wait_ge(sem("ck_out"), NT + 1)
                    else:
                        pe.wait_ge(sem("zs_done"), g - 3)
                    for kk in range(KD):
                        if t == 0:
                            pe.wait_ge(sem("w_cut"), 8 * c + kk + 1)
                        for a, b in PASSES:
                            mm = pe.matmul(ps[:, g % 4, :], hT[a][:, kk, META + P * t:META + P * t + P], W[b][:, (8 * c + kk) % RING, :],
                                           start=(kk == 0 and (a, b) == (0, 0)), stop=(kk == KD - 1 and a == 1))
                    mm.then_inc(sem("z_done"), 1)
                    if g == 11:
                        dt_sums()
            pe.wait_ge(sem("xt2_out"), NXT)
            pe.wait_ge(sem("p_diff"), 2)
            pe.wait_ge(sem("z_done"), 2 * NT)
            for n in range(13):
                bank = 4 + n % 4
                if n >= 4:
                    pe.wait_ge(sem("lat_lo"), n - 3)
                if n < 6:
                    pe.wait_ge(sem("cq_scaled"), NT)
                elif n < 10:
                    pe.wait_ge(sem("ck_scaled"), NT + 1)
                else:
                    pe.wait_ge(sem("kro_done"), 2)
                half = n % 2
                if n < 12:
                    for i in range(4):
                        t = 4 * half + i
                        if n < 6:
                            src = cqs[:, t, P * (n // 2):P * (n // 2) + P]
                        elif n < 10:
                            kk = (n - 6) // 2
                            src = cks[:, t, P * kk:P * kk + P]
                        else:
                            src = kro[:, t, :]
                        mm = pe.transpose(ps[:, bank, P * i:P * i + P], src, k.ident[:, :])
                else:
                    for i in range(3):
                        src = cks[0:META, NT, P * i:P * i + P] if i < 2 else kro[0:META, NT, :]
                        mm = pe.transpose(ps[:, bank, META * i:META * i + META], src, k.ident[0:META, 0:META])
                mm.then_inc(sem("lat_turned"), 1)
            def turn_qr(t):
                for half in range(2):
                    pe.wait_ge(sem(f"qro_done{half}"), t + 1)
                if t < 2:
                    pe.wait_ge(sem("lat_lo"), 13)
                else:
                    pe.wait_ge(sem("qrT_lo"), t - 1)
                for i in range(4):
                    mm = pe.transpose(ps[:, 4 + t % 2, P * i:P * i + P], qro[:, t % 2, 2 * i:2 * i + 2, :].rearrange("p a b -> p (a b)"), k.ident[:, :])
                mm.then_inc(sem("qr_turned"), 1)

            pe.wait_ge(sem("lat_lo"), 13)
            for t in range(NT):
                if t < 4:
                    pe.wait_ge(sem("zs_done"), 2 * NT)
                else:
                    pe.wait_ge(sem("qr_raw"), t - 3)
                for kk in range(KQ):
                    if t == 0:
                        pe.wait_ge(sem("w_cut"), nb + kk + 1)
                    for a, b in PASSES:
                        mm = pe.matmul(ps[:, t % 4, :], k.cqT[a][:, kk, P * t:P * t + P], W[b][:, (nb + kk) % RING, :],
                                       start=(kk == 0 and (a, b) == (0, 0)), stop=(kk == KQ - 1 and a == 1))
                mm.then_inc(sem("qr_done"), 1)
                if t:
                    turn_qr(t - 1)
            turn_qr(NT - 1)

        @block.scalar
        def _(act):
            def out_x(f, part):
                act.wait_ge(sem("x_turned"), 3 * f + part + 1)
                src = ps[:, 6, :].rearrange("p (a b) -> p a b", b=P) if part == 0 else ps[0:META, 6, 0:P]
                if f < KD:
                    if part == 0 and f >= 2:
                        act.wait_ge(sem(f"xt_sent{f % 2}"), 32 * (f // 2))
                    dst = xt[:, f % 2, 0:4, :] if part == 0 else xt[0:META, f % 2, NT, :]
                    act.activation(dst, src, ACT.Copy).then_inc(sem(f"xt{part}_out"), 1)
                else:
                    if f > KD:
                        act.wait_ge(sem("btm_sent" if part == 2 else "bt_sent"), 32 * (f - KD))
                    dst = bt[0][:, 0:4, :] if part == 0 else bt[0][0:META, NT, :]
                    act.activation(dst, src, ACT.Copy).then_inc(sem("bt_hi"), 1)
                    if part == 0:
                        act.wait_ge(sem("x_turned"), 3 * f + 2)
                        act.activation(bt[0][:, 4:8, :], ps[:, 7, :].rearrange("p (a b) -> p a b", b=P), ACT.Copy).then_inc(sem("bt_hi"), 1)

            for f in range(NX):
                if 2 <= f <= NXT + 1:
                    out_x(f - 2, 2)
                act.wait_ge(sem("x_done"), f + 1)
                if f >= 2:
                    act.wait_ge(sem("conv_done"), f - 1)
                for q, (c0, w) in enumerate(TC):
                    act.activation(pre[:, f % 2, 4 + c0:4 + c0 + w], ps[:, 3 * (f % 2) + q, 0:w], ACT.Copy).then_inc(sem("pre_out"), 1)
                if 1 <= f <= NXT:
                    out_x(f - 1, 0)
                act.wait_ge(sem("conv_done"), f + 1)
                if f >= 2:
                    if f - 2 < NXT:
                        act.wait_ge(sem("x_turned"), 3 * (f - 1))
                    if f - 2 >= KD:
                        act.wait_ge(sem("bc_lo"), f - 1 - KD)
                act.activation(xc[:, f % 2, :], acc[:, f % 2, :], ACT.Silu, bias=col(k, "convb", f)).then_inc(sem("xc_done"), 1)
                if f >= KD:
                    act.wait_ge(sem("xc_done"), f + 1)
                    if f > KD:
                        act.wait_ge(sem("bc_sent"), 32 * (f - KD))
                    act.activation(fb[0][:, :], xc[:, f % 2, META:POS], ACT.Copy).then_inc(sem("bc_hi"), 1)
            act.wait_ge(sem("stat_set"), 1)
            for t in range(NW):
                if t < NT:
                    act.wait_ge(sem("cq_out"), t + 1)
                    rows, src = P, cqs[:, t, :]
                else:
                    act.wait_ge(sem("ck_out"), t - NT + 1)
                    rows = P if t < NW - 1 else META
                    src = cks[0:rows, t - NT, 0:KVL]
                if t:
                    act.wait_ge(sem("lat_sq"), t)
                act.activation(junk[0:rows, 0:src.shape[-1]], src, ACT.Square, accum_out=ss[0:rows, t:t + 1]).then_inc(sem("lat_sq"), 1)
            act.wait_ge(sem("lat_v"), 2)
            act.activation(s_[:, 0:NW], v[:, 0:NW], ACT.Sqrt).then_inc(sem("lat_sqrt"), 1)
            flat9 = lambda a: a[:, :, :].rearrange("p a b -> p (a b)")
            for g in range(2 * NT):
                if g == 6:
                    act.wait_ge(sem("p_x"), 2)
                    act.activation(flat9(pb), flat9(pa), ACT.Exp, scale=-1.0).then_inc(sem("p_u"), 1)
                    act.activation(av, av, ACT.Exp).then_inc(sem("p_u"), 1)
                if g == 8:
                    act.wait_ge(sem("p_w"), 1)
                    act.activation(flat9(pc), flat9(pa), ACT.Ln).then_inc(sem("p_ln"), 1)
                if g == 10:
                    act.wait_ge(sem("p_dt"), 1)
                    act.activation(flat9(k.da[0]), flat9(pb), ACT.Copy).then_inc(sem("p_da"), 1)
                if g == 14:
                    act.wait_ge(sem("p_diff"), 3)
                    act.activation(flat9(k.ecum), flat9(k.acum), ACT.Exp).then_inc(sem("p_exp"), 1)
                    act.activation(flat9(k.dend), flat9(pa), ACT.Exp).then_inc(sem("p_exp"), 1)
                    act.activation(flat9(k.cdec), flat9(pc), ACT.Exp).then_inc(sem("p_exp"), 1)
                act.wait_ge(sem("z_done"), g + 1)
                if g >= 4:
                    act.wait_ge(sem(f"z_sent{g % 4}"), 16 * (g // 4))
                act.activation(zs[:, g % 4, :], ps[:, g % 4, :], ACT.Silu).then_inc(sem("zs_done"), 1)
            for n in range(13):
                act.wait_ge(sem("lat_turned"), n + 1)
                c0 = 512 * (n % 2)
                src = ps[:, 4 + n % 4, :]
                if n < 6:
                    act.activation(k.cqT[0][:, n // 2, c0:c0 + 512], src, ACT.Copy, scale=col(k, "qa", n // 2)).then_inc(sem("lat_hi"), 1)
                elif n < 10:
                    kk = (n - 6) // 2
                    act.activation(k.ckT[0][:, kk, META + c0:META + c0 + 512], src, ACT.Copy, scale=col(k, "kva", kk)).then_inc(sem("lat_hi"), 1)
                elif n < 12:
                    act.activation(k.krT[0][:, META + c0:META + c0 + 512], src, ACT.Copy).then_inc(sem("lat_hi"), 1)
                else:
                    act.wait_ge(sem("lat_mt"), 2)
                    act.activation(k.ckT[0][:, :, 0:META], mt[:, 0:2, :], ACT.Copy).then_inc(sem("lat_hi"), 1)
                    act.activation(k.krT[0][:, 0:META], mt[:, 2, :], ACT.Copy).then_inc(sem("lat_hi"), 1)
            def raw_qr(t):
                act.wait_ge(sem("qr_done"), t + 1)
                if t < 4:
                    act.wait_ge(sem(f"z_sent{t}"), 64)
                else:
                    for half in range(2):
                        act.wait_ge(sem(f"qro_done{half}"), t - 3)
                act.activation(zs[:, t % 4, :], ps[:, t % 4, :], ACT.Copy).then_inc(sem("qr_raw"), 1)

            for t in range(2):
                raw_qr(t)
            for t in range(NT):
                if t + 2 < NT:
                    raw_qr(t + 2)
                act.wait_ge(sem("qr_turned"), t + 1)
                if t >= 2:
                    act.wait_ge(sem(f"qr_sent{t % 2}"), 32 * (t // 2))
                act.activation(k.qrT[0][:, t % 2, :, :], ps[:, 4 + t % 2, :].rearrange("p (a b) -> p a b", b=P), ACT.Copy).then_inc(sem("qrT_hi"), 1)

        @block.vector
        def _(dve):
            dve.memset(pre[:, :, 0:4], 0.0).then_inc(sem("pad_set"), 1)
            dve.memset(ss[:, :], 1.0).then_inc(sem("stat_set"), 1)

            def out_x(f, parts):
                if f < KD and 1 in parts:
                    dve.wait_ge(sem("x_turned"), 3 * f + 2)
                    if f >= 2:
                        dve.wait_ge(sem(f"xt_sent{f % 2}"), 32 * (f // 2))
                    dve.tensor_copy(xt[:, f % 2, 4:8, :], ps[:, 7, :].rearrange("p (a b) -> p a b", b=P)).then_inc(sem("xt1_out"), 1)
                for part in parts:
                    if f < KD:
                        continue
                    name = ("xt0_out", "xt1_out", "xt2_out")[part]
                    dve.wait_ge(sem("bt_hi"), 3 * (f - KD) + part + 1)
                    if f > KD:
                        dve.wait_ge(sem("btm_sent" if part == 2 else "bt_sent"), 32 * (f - KD))
                    if part < 2:
                        src = ps[:, 6 + part, :].rearrange("p (a b) -> p a b", b=P)
                        hi, lo = (x[:, 4 * part:4 * part + 4, :] for x in bt)
                    else:
                        src = ps[0:META, 6, 0:P]
                        hi, lo = (x[0:META, NT, :] for x in bt)
                    dve.tensor_tensor(lo, src, hi.bitcast(F32), ALU.subtract).then_inc(sem(name), 1)

            for f in range(NX):
                if 2 <= f <= NXT + 1:
                    out_x(f - 2, (2,))
                if 1 <= f <= NXT:
                    out_x(f - 1, (0, 1))
                dve.wait_ge(sem("pre_out"), 3 * f + 3)
                if f == 0:
                    dve.wait_ge(sem("pad_set"), 1)
                if f >= 2:
                    dve.wait_ge(sem("xc_done"), f - 1)
                a = acc[:, f % 2, :]
                for i in range(4):
                    w = col(k, "convw", 4 * f + i)
                    src = pre[:, f % 2, 1 + i:1 + i + POS]
                    if i == 0:
                        dve.tensor_scalar(a, src, w, None, ALU.mult).then_inc(sem("conv_step"), 1)
                    else:
                        dve.wait_ge(sem("conv_step"), 3 * f + i)
                        mm = dve.scalar_tensor_tensor(a, src, w, a, ALU.mult, ALU.add)
                        mm.then_inc(sem("conv_done" if i == 3 else "conv_step"), 1)
                if f >= KD:
                    dve.wait_ge(sem("bc_hi"), f - KD + 1)
                    if f > KD:
                        dve.wait_ge(sem("bc_sent"), 32 * (f - KD))
                    dve.tensor_tensor(fb[1][:, :], xc[:, f % 2, META:POS], fb[0][:, :].bitcast(F32), ALU.subtract).then_inc(sem("bc_lo"), 1)
            dve.wait_ge(sem("wdt_in"), 16)
            dve.wait_ge(sem("x_done"), NX)
            wd = [w[:, 0:KD, KVL + ROPE:KVL + ROPE + SH] for w in W]
            dve.tensor_copy(wd[0], wdt).then_inc(sem("wdt_cut"), 1)
            dve.wait_ge(sem("wdt_cut"), 1)
            dve.tensor_tensor(wd[1], wdt, wd[0].bitcast(F32), ALU.subtract).then_inc(sem("wdt_cut"), 1)
            dve.wait_ge(sem("xc_done"), NX)
            dve.wait_ge(sem("bc_lo"), NX - KD)
            for name in ("bt_sent", "btm_sent"):
                dve.wait_ge(sem(name), 32 * GROUPS)
            dve.wait_ge(sem("bc_sent"), 32 * 2 * GROUPS)
            for q in range(2):
                dve.wait_ge(sem(f"xt_sent{q}"), 32 * KD // 2)
            dve.memset(cks[:, NT, :], 0.0).then_inc(sem("rest_set"), 1)
            dve.memset(kro[:, :, ROPE:P], 0.0).then_inc(sem("rest_set"), 1)
            dve.memset(k.dt[:, NT, :], 0.0).then_inc(sem("rest_set"), 1)
            for t in range(NT):
                dve.wait_ge(sem("cq_done"), t + 1)
                dve.tensor_copy(cqs[:, t, :], ps[:, t % 4, 0:QL]).then_inc(sem("cq_out"), 1)
            dve.wait_ge(sem("rest_set"), 3)
            for t in range(NT + 1):
                rows = P if t < NT else META
                dve.wait_ge(sem("ck_done"), t + 1)
                dve.tensor_copy(cks[0:rows, t, :], ps[0:rows, t % 4, 0:KVL + ROPE]).then_inc(sem("ck_raw"), 1)
                dve.tensor_copy(k.dt[0:rows, t, :], ps[0:rows, t % 4, KVL + ROPE:KVL + ROPE + SH]).then_inc(sem("ck_out"), 1)
            def tables(dve):
                dt, acum, da = k.dt, k.acum, k.da
                flat9 = lambda a: a[:, :, :].rearrange("p a b -> p (a b)")
                N9 = (NT + 1) * SH
                d = sem("p_step")
                dve.wait_ge(sem("p_in"), 48)
                raw = dt[:, :, :]
                dve.tensor_tensor(raw, raw, dtb.unsqueeze(1).broadcast_to(T9), ALU.add).then_inc(sem("p_x"), 1)
                dve.wait_ge(sem("p_x"), 1)
                dve.scalar_tensor_tensor(flat9(pa), flat9(dt), -1.0, flat9(dt), ALU.mult, ALU.max).then_inc(sem("p_x"), 1)
                dve.wait_ge(sem("p_u"), 2)
                dve.tensor_scalar(flat9(pa), flat9(pb), 1.0, None, ALU.add).then_inc(sem("p_w"), 1)
                dve.wait_ge(sem("p_ln"), 1)
                dve.tensor_scalar(flat9(pa), flat9(pa), -1.0, None, ALU.add).then_inc(d, 1)
                dve.wait_ge(d, 1)
                dve.tensor_scalar(flat9(acum), flat9(pa), 0.0, None, ALU.is_equal).then_inc(d, 1)
                dve.wait_ge(d, 2)
                dve.tensor_tensor(flat9(pa), flat9(pa), flat9(acum), ALU.add).then_inc(d, 1)
                dve.tensor_tensor(flat9(pc), flat9(pc), flat9(acum), ALU.add).then_inc(d, 1)
                dve.wait_ge(d, 4)
                dve.tensor_tensor(flat9(pc), flat9(pc), flat9(pb), ALU.mult).then_inc(d, 1)
                dve.reciprocal(flat9(acum), flat9(pa)).then_inc(d, 1)
                dve.wait_ge(d, 6)
                dve.tensor_tensor(flat9(pc), flat9(pc), flat9(acum), ALU.mult).then_inc(d, 1)
                dve.wait_ge(d, 7)
                dve.scalar_tensor_tensor(flat9(dt), flat9(dt), 0.0, flat9(pc), ALU.max, ALU.add).then_inc(d, 1)
                dve.wait_ge(d, 8)
                dve.tensor_tensor(pc[:, :, :], raw, av.unsqueeze(1).broadcast_to(T9), ALU.mult).then_inc(d, 1)
                dve.wait_ge(d, 9)
                dve.tensor_scalar(flat9(pb), flat9(pc), -1.0, None, ALU.mult).then_inc(sem("p_dt"), 1)
                dve.wait_ge(sem("p_da"), 1)
                dve.tensor_tensor(flat9(da[1]), flat9(pb), flat9(da[0]).bitcast(F32), ALU.subtract).then_inc(sem("p_da"), 1)
                dve.wait_ge(sem("p_sums"), 1)
                dve.tensor_copy(flat9(acum), ps[:, 4, 0:N9]).then_inc(sem("p_diff"), 1)
                dve.tensor_copy(flat9(pc), ps[:, 5, 0:N9]).then_inc(sem("p_diff"), 1)
                dve.wait_ge(sem("p_diff"), 2)
                dve.tensor_tensor(flat9(pa), flat9(pc), flat9(acum), ALU.subtract).then_inc(sem("p_diff"), 1)

            dve.wait_ge(sem("lat_sq"), NW)
            rsqrt_before(dve, k, v[:, 0:NT], ss[:, 0:NT], 1.0 / QL, "lat_v", 1)
            rsqrt_before(dve, k, v[:, NT:NW], ss[:, NT:NW], 1.0 / KVL, "lat_v", 2)
            rsqrt_after(dve, k, r[:, 0:NW], v[:, 0:NW], s_[:, 0:NW], t1[:, 0:NW], "lat_sqrt", 1, "rs2")
            for t in range(NT):
                dve.tensor_scalar(cqs[:, t, :], cqs[:, t, :], r[:, t:t + 1], None, ALU.mult).then_inc(sem("cq_scaled"), 1)
            for t in range(NT + 1):
                rows = P if t < NT else META
                dve.tensor_scalar(cks[0:rows, t, 0:KVL], cks[0:rows, t, 0:KVL], r[0:rows, NT + t:NT + t + 1], None,
                                  ALU.mult).then_inc(sem("ck_scaled"), 1)
            dve.wait_ge(sem("rope_in"), 16)
            dve.wait_ge(sem("ck_out"), NT + 1)
            x1, x2 = cks[:, :, KVL:KVL + 32], cks[:, :, KVL + 32:KVL + 64]
            cos, sin = rope[:, :, 0:32], rope[:, :, 32:64]
            a3, b3 = ta[:, 0:288].rearrange("p (t c) -> p t c", c=32), tb[:, 0:288].rearrange("p (t c) -> p t c", c=32)
            rotate(dve, k, x1, x2, cos, sin, a3, b3, kro[:, :, 0:32], kro[:, :, 32:64], "kro", 0)
            tables(dve)
            for n in range(13):
                c0 = 512 * (n % 2)
                src = ps[:, 4 + n % 4, :]
                if n == 12:
                    dve.wait_ge(sem("lat_turned"), 13)
                    w = k.par[:, PARAM["kva"]:PARAM["kva"] + 2].unsqueeze(2).broadcast_to([P, 2, META])
                    dve.tensor_tensor(mt[:, 0:2, :], ps[:, 4, 0:2 * META].rearrange("p (a b) -> p a b", a=2), w, ALU.mult).then_inc(sem("lat_mt"), 1)
                    dve.tensor_copy(mt[:, 2, :], ps[:, 4, 2 * META:3 * META]).then_inc(sem("lat_mt"), 1)
                    dve.wait_ge(sem("lat_hi"), 14)
                    dve.wait_ge(sem("lat_mt"), 2)
                    dve.tensor_tensor(k.ckT[1][:, :, 0:META], mt[:, 0:2, :], k.ckT[0][:, :, 0:META].bitcast(F32), ALU.subtract).then_inc(sem("lat_m"), 1)
                    dve.tensor_tensor(k.krT[1][:, 0:META], mt[:, 2, :], k.krT[0][:, 0:META].bitcast(F32), ALU.subtract).then_inc(sem("lat_lo"), 1)
                    continue
                dve.wait_ge(sem("lat_hi"), n + 1)
                if n < 6:
                    hi, lo = (x[:, n // 2, c0:c0 + 512] for x in k.cqT)
                    w = col(k, "qa", n // 2)
                elif n < 10:
                    kk = (n - 6) // 2
                    hi, lo = (x[:, kk, META + c0:META + c0 + 512] for x in k.ckT)
                    w = col(k, "kva", kk)
                else:
                    hi, lo = (x[:, META + c0:META + c0 + 512] for x in k.krT)
                    w = 1.0
                dve.scalar_tensor_tensor(lo, src, w, hi.bitcast(F32), ALU.mult, ALU.subtract).then_inc(sem("lat_lo"), 1)

            def low_qr(t):
                dve.wait_ge(sem("qrT_hi"), t + 1)
                if t >= 2:
                    dve.wait_ge(sem(f"qr_sent{t % 2}"), 32 * (t // 2))
                dve.tensor_tensor(k.qrT[1][:, t % 2, :, :], ps[:, 4 + t % 2, :].rearrange("p (a b) -> p a b", b=P), k.qrT[0][:, t % 2, :, :].bitcast(F32),
                                  ALU.subtract).then_inc(sem("qrT_lo"), 1)

            for t in range(NT):
                rotate_half(dve, t, 0, ta, tb)
                if t:
                    low_qr(t - 1)
            low_qr(NT - 1)


def rotate(dve, k, x1, x2, cos, sin, a, b, out1, out2, name, turn):
    c = k.sem(name + "_step")
    n = 4 * turn
    if turn:
        dve.wait_ge(k.sem(name + "_done"), 2 * turn)
    dve.tensor_tensor(a, x1, cos, ALU.mult).then_inc(c, 1)
    dve.tensor_tensor(b, x2, sin, ALU.mult).then_inc(c, 1)
    dve.wait_ge(c, n + 2)
    dve.tensor_tensor(out1, a, b, ALU.subtract).then_inc(k.sem(name + "_done"), 1)
    dve.wait_ge(k.sem(name + "_done"), 2 * turn + 1)
    dve.tensor_tensor(a, x2, cos, ALU.mult).then_inc(c, 1)
    dve.tensor_tensor(b, x1, sin, ALU.mult).then_inc(c, 1)
    dve.wait_ge(c, n + 4)
    dve.tensor_tensor(out2, a, b, ALU.add).then_inc(k.sem(name + "_done"), 1)


def wo_blocks(k):
    wo = k.io["w_out"][0]
    return [wo[D * part + P * kk:D * part + P * kk + P, 512 * c:512 * c + 512] for part in range(2) for c in range(2) for kk in range(KD)]



def phase_attend(k):
    nc, sem, m, ps, io = k.nc, k.sem, k.map, k.ps, k.io
    o = O_RING

    def pair(name, shape, o):
        a, o = m.at(name + "hi", shape, F32R, o)
        b, o = m.at(name + "lo", shape, F32R, o)
        return (a, b), o

    kT, v, qT, qr = {}, {}, {}, {}
    for u in range(2):
        kT[u], o = pair(f"kT{u}", [P, POS], o)
        v[u], o = pair(f"v{u}", [P, NT + 1, VH], o)
        qT[u], o = pair(f"qT{u}", [P, SEQ], o)
        if u == 0:
            qr[u], o = pair(f"qr{u}", [ROPE, SEQ], o)
    assert o <= O_RING + 59648
    o = k.o_lat
    pT, o = pair("pT", [P, NT + 1, 512], o)
    oT, o = pair("oT", [P, 2, 512], o)
    prob, o = m.at("prob", [P, 4, POS], F32, o)
    qr[1], o = pair("qr1", [ROPE, SEQ], o)
    assert o <= k.o_wkv
    wq, wkv = k.wq, k.wkv
    k.wo_blocks = wo_blocks(k)
    mx, nb, sm, rs, bias = k.st[0], k.st[1], k.st[2], k.st[3], k.st[4]
    flat = ps[:, :, :].rearrange("p a b -> p (a b)")
    KQ, KK = QL // P, KVL // P
    PASSES = ((0, 0), (0, 1), (1, 0))
    width = lambda b: META + P * (b + 1)
    start = lambda b: 0 if b % 2 == 0 else 4 * 512 - width(b)
    TURN, OUT, PROJ = 4, 6, 7
    batches = [(b, p0, min(4, b + 2 - p0)) for b in range(NT) for p0 in range(0, b + 2, 4)]
    NB = len(batches)
    assert NB % 2 == 0
    first_batch = [next(i for i, x in enumerate(batches) if x[0] == b) for b in range(NT)]

    def of_block(b):
        return [(i, x) for i, x in enumerate(batches) if x[0] == b]

    FIRST_BANKS = (7, 6, 5, 4, 2, 1, 7)

    def evacs(n, u, bank=PROJ):
        pbank = ps[:, bank, :]
        if n < 2:
            return [(pbank, [x[:, 512 * n:512 * n + 512] for x in qT[u]])]
        if n < 5:
            c0, w = TC[n - 2]
            e = [(ps[:, bank, 0:w], [x[:, c0:c0 + w] for x in kT[u]])]
            if n == 4:
                e.append((ps[0:META, bank, w:w + VH], [x[0:META, NT, :] for x in v[u]]))
            return e
        q = n - 5
        return [(pbank.rearrange("p (a b) -> p a b", b=VH), [x[:, 4 * q:4 * q + 4, :] for x in v[u]])]

    PIECES = 7
    NE = 8
    before = [n + (n > 4) for n in range(PIECES + 1)]

    with nc.Block() as block:
        @block.sync
        def _(sp):
            def rotated(h, u):
                for i in range(2):
                    sp.dma_start(qr[u][i][:, :].bitcast(F32), k.d_qr[i].rearrange("(h c) t -> h c t", c=ROPE)[h]).then_inc(sem("a_qr_in"), 16)

            def outputs(h, g):
                sp.wait_ge(sem("a_o_lo"), 2 * h + g + 2)
                for i in range(2):
                    sp.dma_start(k.d_att[i].rearrange("(h c) t -> h c t", c=VH)[h][:, 512 * g:512 * g + 512],
                                 oT[i][:, g, :].bitcast(F32)).then_inc(sem(f"a_sent{g}"), 16)

            def head(h, u, left):
                if left >= 2:
                    sp.wait_ge(sem("a_cut"), 4 * h + 8)
                    head_weights(sp, k, h + 2)
                if left >= 1:
                    sp.wait_ge(sem("a_s"), NT * h + 1)
                    rotated(h + 1, 1 - u)
                for g in range(2):
                    outputs(h, g)

            for q in range(2):
                sp.wait_ge(sem(f"qr_sent{q}"), 32 * NT // 2)
            rotated(0, 0)
            head_weights(sp, k, 1)
            with sp.Fori(0, HEADS // 2 - 1) as i:
                for u in range(2):
                    head(2 * i + u, u, 2)
            head(HEADS - 2, 0, 1)
            for n in range(RING // 2):
                load_block(sp, k, "u", n, k.wo_blocks[n])
            head(HEADS - 1, 1, 0)

        @block.gpsimd
        def _(pool):
            with pool.Fori(1, HEADS) as h:
                cut_head(pool, k, h, lambda n: pool.wait_ge(sem("a_proj"), PIECES * (h - 1) + (PIECES if n else 2)))
            pool.wait_ge(sem("a_o"), 2 * HEADS - 2)
            for n in range(RING // 2):
                cut_block(pool, k, "u", n, 512)

        @block.tensor
        def _(pe):
            def piece(h, u, n, first=False):
                if n in (0, 2):
                    pe.wait_ge(sem("a_cut"), 4 * h + 2 + n)
                bank = FIRST_BANKS[n] if first else PROJ
                pbank = ps[:, bank, :]
                if not first:
                    pe.wait_ge(sem("a_e_lo"), NE * h + before[n])
                elif n == PIECES - 1:
                    pe.wait_ge(sem("a_e_lo"), before[1])
                if n < 2:
                    for kk in range(KQ):
                        for a, b in PASSES:
                            mm = pe.matmul(pbank, wq[a][:, kk, :], k.cqT[b][:, kk, 512 * n:512 * n + 512],
                                           start=(kk == 0 and (a, b) == (0, 0)), stop=(kk == KQ - 1 and a == 1))
                elif n < 5:
                    c0, w = TC[n - 2]
                    for kk in range(KK):
                        for a, b in PASSES:
                            mm = pe.matmul(ps[:, bank, 0:w], wkv[a][:, kk, 0:NOPE], k.ckT[b][:, kk, c0:c0 + w],
                                           start=(kk == 0 and (a, b) == (0, 0)), stop=(kk == KK - 1 and a == 1))
                tiles = [(TC[2][1], 0)] if n == 4 else [(VH * j, META + P * (4 * (n - 5) + j)) for j in range(4)] if n > 4 else []
                for at, c0 in tiles:
                    for kk in range(KK):
                        for a, b in PASSES:
                            mm = pe.matmul(ps[:, bank, at:at + VH], k.ckT[a][:, kk, c0:c0 + P], wkv[b][:, kk, NOPE:NOPE + VH],
                                           start=(kk == 0 and (a, b) == (0, 0)), stop=(kk == KK - 1 and a == 1))
                mm.then_inc(sem("a_proj"), 1)

            def scores(h, u, b, first=False):
                n, s0 = width(b), start(b)
                if b == 0:
                    pe.wait_ge(sem("a_qr_in"), 32 * h + 32)
                need = {0: 3, 2: 4, 5: 5}.get(b)
                if need:
                    pe.wait_ge(sem("a_e_lo"), NE * h + need)
                if b >= 2 or not first:
                    pe.wait_ge(sem("a_exp"), NT * h + b - 1)
                cuts = sorted({s0, s0 + n} | {c for c in range(0, 2048, 512) if s0 < c < s0 + n})
                tiles = [(c - s0, d - s0) for c, d in zip(cuts[:-1], cuts[1:])][::-1]
                d0, d1 = n - P, n
                for i, (c0, c1) in enumerate(tiles):
                    if b == NT - 1 and i == len(tiles) - 1:
                        pe.wait_ge(sem("a_exp"), NT * h + b)
                    out = flat[:, s0 + c0:s0 + c1]
                    q = slice(P * b, P * b + P)
                    pe.matmul(out, qT[u][0][:, q], kT[u][0][:, c0:c1], start=True, stop=False)
                    lo, hi = max(c0, d0), min(c1, d1)
                    if lo < hi:
                        pe.matmul(flat[:, s0 + lo:s0 + hi], k.mask_b[:, :], k.ident_b[:, lo - d0:hi - d0], start=False, stop=False)
                    pe.matmul(out, qT[u][0][:, q], kT[u][1][:, c0:c1], start=False, stop=False)
                    pe.matmul(out, qT[u][1][:, q], kT[u][0][:, c0:c1], start=False, stop=False)
                    for a, c in PASSES:
                        mm = pe.matmul(out, qr[u][a][:, q], k.krT[c][0:ROPE, c0:c1], start=False, stop=(a == 1))
                mm.then_inc(sem("a_s"), 1)

            def turn(h, b):
                pe.wait_ge(sem("a_p"), NT * h + b + 1)
                for i, (_, p0, np_) in of_block(b):
                    if i >= 2:
                        pe.wait_ge(sem("a_t_lo"), NB * h + i - 1)
                    for j in range(np_):
                        c0 = 0 if p0 + j == 0 else META + P * (p0 + j - 1)
                        mm = pe.transpose(ps[:, TURN + i % 2, P * j:P * j + P], prob[:, b % 4, c0:c0 + P], k.ident[:, :])
                    mm.then_inc(sem("a_t"), 1)

            def weigh(h, u, g):
                pe.wait_ge(sem("a_t_lo"), NB * h + (first_batch[4] if g == 0 else NB))
                pe.wait_ge(sem("a_o_lo"), 2 * h + g + 1)
                if g == 0:
                    pe.wait_ge(sem("a_e_lo"), NE * h + NE)
                last = 4 * g + 3
                for j in range(-1, last + 1):
                    rows = slice(0, META if j < 0 else P)
                    vt = NT if j < 0 else j
                    c0 = P * max(0, j - 4 * g)
                    for a, b in PASSES:
                        mm = pe.matmul(ps[:, OUT, c0:512], v[u][a][rows, vt, :], pT[b][rows, j + 1, c0:512],
                                       start=(j < 0 and (a, b) == (0, 0)), stop=(j == last and a == 1))
                mm.then_inc(sem("a_o"), 1)

            def late(h, u, more):
                for b in range(3, NT):
                    scores(h, u, b)
                    if more:
                        piece(h + 1, 1 - u, b - 3)
                    if b == 6:
                        weigh(h, u, 0)
                    turn(h, b - 2)

            def next_early(h, u):
                for b in range(3):
                    scores(h + 1, 1 - u, b)
                    if b < 2:
                        piece(h + 1, 1 - u, 5 + b)
                        turn(h, NT - 2 + b)
                weigh(h, u, 1)
                turn(h + 1, 0)

            for n in range(PIECES):
                piece(0, 0, n, True)
            for b in range(3):
                scores(0, 0, b, True)
            turn(0, 0)
            pe.wait_ge(sem("a_e_lo"), NE)
            with pe.Fori(0, HEADS // 2 - 1) as i:
                for u in range(2):
                    late(2 * i + u, u, True)
                    next_early(2 * i + u, u)
            late(HEADS - 2, 0, True)
            next_early(HEADS - 2, 0)
            late(HEADS - 1, 1, False)
            for b in (NT - 2, NT - 1):
                turn(HEADS - 1, b)
            weigh(HEADS - 1, 1, 1)

        @block.scalar
        def _(act):
            def high(h, b):
                for i, (_, p0, np_) in of_block(b):
                    act.wait_ge(sem("a_t"), NB * h + i + 1)
                    act.activation(pT[0][:, p0:p0 + np_, P * (b % 4):P * (b % 4) + P],
                                   ps[:, TURN + i % 2, 0:P * np_].rearrange("p (a b) -> p a b", b=P), ACT.Copy).then_inc(sem("a_t_hi"), 1)

            def exp(h, b):
                n, s0 = width(b), start(b)
                act.wait_ge(sem("a_nb"), NT * h + b + 1)
                act.activation(prob[:, b % 4, 0:n], flat[:, s0:s0 + n], ACT.Exp, bias=nb[:, b:b + 1], scale=SCALE,
                               accum_out=sm[:, b:b + 1]).then_inc(sem("a_exp"), 1)

            def out(h, g):
                act.wait_ge(sem("a_o"), 2 * h + g + 1)
                act.wait_ge(sem(f"a_sent{g}"), 32 * h + 1)
                act.activation(oT[0][:, g, :], ps[:, OUT, :], ACT.Copy).then_inc(sem("a_o_hi"), 1)

            def piece(h, u, n, bank=PROJ):
                act.wait_ge(sem("a_proj"), PIECES * h + n + 1)
                for src, dst in evacs(n, u, bank):
                    act.activation(dst[0], src, ACT.Copy).then_inc(sem("a_e_hi"), 1)

            def late(h, u, more):
                for b in range(3, NT):
                    if more:
                        piece(h + 1, 1 - u, b - 3)
                    high(h, b - 2)
                    exp(h, b)
                    if b == 6:
                        out(h, 0)

            def next_early(h, u):
                for b in range(3):
                    if b < 2:
                        piece(h + 1, 1 - u, 5 + b)
                        high(h, NT - 2 + b)
                    exp(h + 1, b)
                out(h, 1)
                high(h + 1, 0)

            for n in range(PIECES):
                piece(0, 0, n, FIRST_BANKS[n])
            for b in range(3):
                exp(0, b)
            high(0, 0)
            with act.Fori(0, HEADS // 2 - 1) as i:
                for u in range(2):
                    late(2 * i + u, u, True)
                    next_early(2 * i + u, u)
            late(HEADS - 2, 0, True)
            next_early(HEADS - 2, 0)
            late(HEADS - 1, 1, False)
            for b in (NT - 2, NT - 1):
                high(HEADS - 1, b)
            out(HEADS - 1, 1)

        @block.vector
        def _(dve):
            dve.memset(bias[:, 0:1], 0.0).then_inc(sem("a_o_lo"), 1)
            for g in range(2):
                dve.memset(bias[:, 1 + g:2 + g], 0.0).then_inc(sem(f"a_sent{g}"), 1)

            def most(h, b):
                n, s0 = width(b), start(b)
                dve.wait_ge(sem("a_s"), NT * h + b + 1)
                dve.tensor_reduce(mx[:, b:b + 1], flat[:, s0:s0 + n], AX.X, ALU.max).then_inc(sem("a_mx"), 1)
                dve.wait_ge(sem("a_mx"), NT * h + b + 1)
                dve.tensor_scalar(nb[:, b:b + 1], mx[:, b:b + 1], -SCALE, None, ALU.mult).then_inc(sem("a_nb"), 1)

            def normalise(h, b):
                n = width(b)
                dve.wait_ge(sem("a_exp"), NT * h + b + 1)
                dve.reciprocal(rs[:, b:b + 1], sm[:, b:b + 1]).then_inc(sem("a_rs"), 1)
                dve.wait_ge(sem("a_rs"), NT * h + b + 1)
                dve.tensor_scalar(prob[:, b % 4, 0:n], prob[:, b % 4, 0:n], rs[:, b:b + 1], None, ALU.mult).then_inc(sem("a_p"), 1)

            def low(h, b):
                for i, (_, p0, np_) in of_block(b):
                    dve.wait_ge(sem("a_t_hi"), NB * h + i + 1)
                    hi, lo = (x[:, p0:p0 + np_, P * (b % 4):P * (b % 4) + P] for x in pT)
                    dve.tensor_tensor(lo, ps[:, TURN + i % 2, 0:P * np_].rearrange("p (a b) -> p a b", b=P), hi.bitcast(F32),
                                      ALU.subtract).then_inc(sem("a_t_lo"), 1)

            def out(h, g):
                dve.wait_ge(sem("a_o_hi"), 2 * h + g + 1)
                dve.tensor_tensor(oT[1][:, g, :], ps[:, OUT, :], oT[0][:, g, :].bitcast(F32), ALU.subtract).then_inc(sem("a_o_lo"), 1)

            def piece(h, u, n, bank=PROJ):
                e = evacs(n, u, bank)
                dve.wait_ge(sem("a_e_hi"), NE * h + before[n] + len(e))
                for src, dst in e:
                    dve.tensor_tensor(dst[1], src, dst[0].bitcast(F32), ALU.subtract).then_inc(sem("a_e_lo"), 1)

            def late(h, u, more):
                for b in range(3, NT):
                    most(h, b)
                    normalise(h, b - 1)
                    if more:
                        piece(h + 1, 1 - u, b - 3)
                    low(h, b - 2)
                    if b == 6:
                        out(h, 0)

            def next_early(h, u):
                for b in range(3):
                    most(h + 1, b)
                    if b == 0:
                        normalise(h, NT - 1)
                    else:
                        normalise(h + 1, b - 1)
                    if b < 2:
                        piece(h + 1, 1 - u, 5 + b)
                        low(h, NT - 2 + b)
                out(h, 1)
                low(h + 1, 0)

            for n in range(PIECES):
                piece(0, 0, n, FIRST_BANKS[n])
            for b in range(3):
                most(0, b)
                if b:
                    normalise(0, b - 1)
            low(0, 0)
            with dve.Fori(0, HEADS // 2 - 1) as i:
                for u in range(2):
                    late(2 * i + u, u, True)
                    next_early(2 * i + u, u)
            late(HEADS - 2, 0, True)
            next_early(HEADS - 2, 0)
            late(HEADS - 1, 1, False)
            normalise(HEADS - 1, NT - 1)
            for b in (NT - 2, NT - 1):
                low(HEADS - 1, b)
            out(HEADS - 1, 1)



def phase_ssd(k):
    nc, sem, m, ps, io = k.nc, k.sem, k.map, k.ps, k.io
    o = O_R

    def pair(name, shape, o):
        a, o = m.at(name + "hi", shape, F32R, o)
        b, o = m.at(name + "lo", shape, F32R, o)
        return (a, b), o

    xs, o = m.at("s_x", [P, SSMW], F32, o)
    zs, o = m.at("s_z", [P, SSMW], F32, o)
    bT, o = pair("s_bT", [P, GROUPS, P], o)
    cT, o = pair("s_cT", [P, GROUPS, P], o)
    bt, o = pair("s_bt", [P, GROUPS * STATE], o)
    run, o = pair("run", [P, SH, P], o)
    aT, o = pair("s_aT", [P, 2, KD, P], o)
    xdt, o = m.at("xdt", [P, SSMW], F32, o)
    xh, o = pair("xdt_", [P, SSMW], o)
    xw, o = m.at("xw", [P, SSMW], F32, o)
    xwh, o = pair("xw_", [P, SSMW], o)
    xd, o = m.at("xd", [P, SSMW], F32, o)
    state, o = m.at("state", [P, SSMW], F32, o)
    sth, o = pair("state_", [P, SSMW], o)
    es, o = m.at("es", [P, 2, 512], F32, o)
    wl, o = pair("wl", [P, 2, 4, P], o)
    cbs, o = m.at("cbs", [P, GROUPS, P], F32, o)
    wrow, o = m.at("ssm_w", [P, SSMW], F32, o)
    mixs, o = m.at("mixs", [P, D], F32, o)
    pick, o = m.at("pick", [P, 8], F32R, o)
    op = o
    y, o = m.at("y", [P, 2, SSMW], F32, o)
    sT, o = pair("sT", [P, KD, P], o)
    assert o <= O_TABLES
    junk = k.spare[:, 0:512]
    dt = k.dt

    xm, op = m.at("p_xm", [META, SSMW], F32, op)
    bm, op = pair("p_bm", [META, GROUPS * STATE], op)
    acum, ecum, dend, cdec, dsk = k.acum, k.ecum, k.dend, k.cdec, k.dsk
    ss, v, s_, r, t1, bias = k.st
    PASSES = ((0, 0), (0, 1), (1, 0))
    W = (k.whi, k.wlo)
    heads = lambda a: a.rearrange("p (h c) -> p h c", c=SHD)
    by_head = lambda a, rows=P: a.unsqueeze(2).broadcast_to([rows, SH, SHD])

    LAST = NT - 1
    QUARTER = KD // 2

    with nc.Block() as block:
        @block.sync
        def _(sp):
            rows = lambda a, t: a.rearrange("(t p) n -> t p n", p=P)[t]
            cols = lambda a, t: a.rearrange("(k p) (t n) -> t p k n", p=P, n=P)[t]

            def load_x(t):
                sp.dma_start(xs[:, :], rows(k.d_x, t)).then_inc(sem("s_x_in"), 16)

            def load_z(t):
                sp.dma_start(zs[:, :], rows(k.d_z, t)).then_inc(sem("s_z_in"), 16)

            def load_bc(t):
                for i in range(2):
                    sp.dma_start(bT[i][:, :, :].bitcast(F32), cols(k.d_bt[i], t)).then_inc(sem("s_bc_in"), 16)
                    sp.dma_start(cT[i][:, :, :].bitcast(F32), cols(k.d_ct[i], t)).then_inc(sem("s_bc_in"), 16)
                    sp.dma_start(bt[i][:, :].bitcast(F32), rows(k.d_b[i], t)).then_inc(sem("s_bc_in"), 16)

            def load_at(t, u):
                for i in range(2):
                    sp.dma_start(aT[i][:, u, :, :].bitcast(F32), cols(k.d_att[i], t)).then_inc(sem(f"s_at_in{u}"), 16)

            def load_first(u):
                sp.wait_ge(sem("s_sent"), 32 * (u + 1) + 1)
                if u == 0:
                    sp.wait_ge(sem("s_mix"), 2 * NT - 2)
                for i in range(2):
                    sp.dma_start(aT[i][:, u, :, :].bitcast(F32), cols(k.d_ssm[i], u)).then_inc(sem(f"s_first_in{u}"), 16)

            def store_mix(t, c):
                sp.wait_ge(sem("s_mixc"), 2 * t + c + 1)
                sp.dma_start(rows(k.d_mix, t)[:, 512 * c:512 * c + 512], mixs[:, 512 * c:512 * c + 512]).then_inc(sem(f"s_mix_sent{c}"), 16)

            def store_ssm(t):
                sp.wait_ge(sem("s_end"), t + 2)
                for i in range(2):
                    sp.dma_start(cols(k.d_ssm[i], t), sT[i][:, :, :].bitcast(F32)).then_inc(sem("s_sent"), 16)

            def turn(t, u, first, left):
                if not first:
                    sp.wait_ge(sem("s_gz"), t)
                    load_z(t)
                store_mix(t, 0)
                if left >= 1:
                    sp.wait_ge(sem("s_stp"), t + 1)
                    load_bc(t + 1)
                    sp.wait_ge(sem("s_xd"), t + 1)
                    load_x(t + 1)
                if not first:
                    store_ssm(t - 1)
                if left >= 2:
                    sp.wait_ge(sem("s_mix"), 2 * t + 2)
                    load_at(t + 2, u)
                store_mix(t, 1)

            sp.dma_start(xm[:, :], k.d_xm).then_inc(sem("s_start_in"), 16)
            for i in range(2):
                sp.dma_start(bm[i][:, :].bitcast(F32), k.d_bm[i]).then_inc(sem("s_start_in"), 16)
            load_bc(0)
            load_x(0)
            for g in range(2):
                sp.wait_ge(sem(f"a_sent{g}"), 32 * HEADS + 1)
            load_at(0, 0)
            for n in range(RING // 2, RING // 2 + STAGES):
                load_block(sp, k, "u", n, k.wo_blocks[n])
            for n in range(RING // 2 + STAGES, RING):
                load_block(sp, k, "u", n, k.wo_blocks[n])
            load_z(0)
            load_at(1, 1)
            sp.dma_start(wrow[:, :], io["ssm_norm"][0].partition_broadcast(P)).then_inc(sem("s_w_in"), 16)
            turn(0, 0, True, LAST)
            with sp.Fori(0, NT // 2 - 2) as i:
                for u in (1, 0):
                    turn(2 * i + 2 - u, u, False, 2)
            turn(NT - 3, 1, False, 2)
            turn(NT - 2, 0, False, 1)
            for n in range(RING, RING + STAGES):
                load_block(sp, k, "u", n, k.wo_blocks[n])
            load_first(0)
            for n in range(RING + STAGES, RING + KD):
                load_block(sp, k, "u", n, k.wo_blocks[n])
            sp.wait_ge(sem("s_gz"), LAST)
            load_z(LAST)
            store_mix(LAST, 0)
            sp.wait_ge(sem("s_mix"), 2 * NT)
            load_first(1)
            store_ssm(LAST - 1)
            store_mix(LAST, 1)
            for n in range(RING + KD, 2 * RING):
                load_block(sp, k, "u", n, k.wo_blocks[n])
            store_ssm(LAST)
            sp.wait_ge(sem("s_sent"), 32 * NT + 1)
            for c in range(2):
                sp.wait_ge(sem(f"s_mix_sent{c}"), 16 * NT)

        @block.gpsimd
        def _(pool):
            def gate(t, u):
                pool.wait_ge(sem("s_yd"), t + 1)
                pool.tensor_tensor(y[:, u, :], y[:, u, :], xd[:, :], ALU.add).then_inc(sem("s_ya"), 1)
                pool.wait_ge(sem("s_ya"), t + 1)
                pool.wait_ge(sem("s_z_in"), 16 * t + 16)
                pool.tensor_tensor(y[:, u, :], y[:, u, :], zs[:, :], ALU.mult).then_inc(sem("s_gz"), 1)

            def chunk(t, u, first):
                if not first:
                    pool.wait_ge(sem("s_xwlo"), t)
                pool.wait_ge(sem("s_xdt"), t + 1)
                pool.tensor_tensor(heads(xw[:, :]), heads(xdt[:, :]), by_head(dend[:, t, :]), ALU.mult).then_inc(sem("s_xw"), 1)
                if not first:
                    gate(t - 1, 1 - u)
                pool.wait_ge(sem("s_xwh"), t + 1)
                pool.tensor_tensor(xwh[1][:, :], xw[:, :], xwh[0][:, :].bitcast(F32), ALU.subtract).then_inc(sem("s_xwlo"), 1)
                pool.wait_ge(sem("s_xh"), t + 1)
                pool.tensor_tensor(xh[1][:, :], xdt[:, :], xh[0][:, :].bitcast(F32), ALU.subtract).then_inc(sem("s_xlo"), 1)
                pool.tensor_tensor(heads(xd[:, :]), heads(xs[:, :]), by_head(dsk[:, :]), ALU.mult).then_inc(sem("s_xd"), 1)

            for n in range(RING // 2, RING // 2 + STAGES):
                cut_block(pool, k, "u", n, 512)
            chunk(0, 0, True)
            with pool.Fori(0, NT // 2 - 1) as i:
                for u in (1, 0):
                    chunk(2 * i + 2 - u, u, False)
            chunk(LAST, 1, False)
            for n in range(RING, RING + KD):
                cut_lo(pool, k, "u", n)
            gate(LAST, 1)
            for n in range(RING + KD, 2 * RING):
                cut_lo(pool, k, "u", n)

        @block.tensor
        def _(pe):
            def meta_state():
                pe.wait_ge(sem("p_xwlo"), 1)
                for g in range(GROUPS):
                    for a, b in PASSES:
                        mm = pe.matmul(ps[:, 2 + g, :], bm[a][:, P * g:P * g + P], xwh[b][0:META, 512 * g:512 * g + 512], start=(a == 0 and b == 0), stop=(a == 1))
                mm.then_inc(sem("p_state"), 1)

            def decays(q, first):
                bank = 7 - q % 2
                if first:
                    pe.wait_ge(sem("s_run"), 2 * q + 2)
                pe.matmul(ps[:, bank, :], k.ident_b[:, :], k.mask_b[:, :].unsqueeze(1).broadcast_to([P, 4, P]), start=True, stop=False)
                for a in range(2):
                    mm = pe.matmul(ps[:, bank, :], pick[:, 0:1].broadcast_to([P, P]), run[a][:, 4 * q:4 * q + 4, :].rearrange("p a b -> p (a b)"),
                                   start=False, stop=(a == 1))
                mm.then_inc(sem("s_eb"), 1)

            pe.transpose(ps[:, 0, 0:P], acum[:, 0:NT, :].rearrange("p a b -> p (a b)"), k.ident[:, :]).then_inc(sem("s_run_turned"), 1)

            def mix(t, u, c, k0, k1, first):
                if k0 == 0 and not first:
                    pe.wait_ge(sem("s_mixc"), 2 * t - 1 + c)
                for kk in range(k0, k1):
                    if first and c:
                        pe.wait_ge(sem("u_cut"), KD * c + kk + 1)
                    for a, b in PASSES:
                        mm = pe.matmul(ps[:, 4 + c, :], aT[a][:, u, kk, :], W[b][:, KD * c + kk, :],
                                       start=(kk == 0 and (a, b) == (0, 0)), stop=(kk == KD - 1 and a == 1))
                if k1 == KD:
                    mm.then_inc(sem("s_mix"), 1)

            def diag(t, q):
                pe.wait_ge(sem("s_wlo"), 4 * t + q + 1)
                for j in range(4):
                    h = 4 * q + j
                    out = ps[:, 2 + h // 8, SHD * (h % 8):SHD * (h % 8) + SHD]
                    for a, b in PASSES:
                        mm = pe.matmul(out, wl[a][:, q % 2, j, :], xh[b][:, SHD * h:SHD * h + SHD], start=(a == 0 and b == 0), stop=(a == 1))
                mm.then_inc(sem("s_dg"), 1)

            def turned(t, u):
                pe.wait_ge(sem("s_g"), 2 * t + 2)
                for c in range(2):
                    for j in range(4):
                        kk = 4 * c + j
                        mm = pe.transpose(ps[:, c, P * j:P * j + P], y[:, u, P * kk:P * kk + P], k.ident[:, :])
                    mm.then_inc(sem("s_tr"), 1)

            def chunk(t, u, first, last=False):
                pe.wait_ge(sem("s_bc_in"), 96 * t + 96)
                if not first:
                    pe.wait_ge(sem("s_sub"), 4 * t)
                for g in range(GROUPS):
                    for a, b in PASSES:
                        mm = pe.matmul(ps[:, 6, P * g:P * g + P], bT[a][:, g, :], cT[b][:, g, :], start=(a == 0 and b == 0), stop=(a == 1))
                mm.then_inc(sem("s_cb"), 1)
                pe.wait_ge(sem("s_pick"), t + 1)
                decays(0, first)
                if first:
                    meta_state()
                    pe.wait_ge(sem(f"s_at_in{u}"), 16 * (t - u) + 32)
                    mix(t, u, 0, 0, QUARTER, first)
                pe.wait_ge(sem("s_stlo"), t + 1)
                if not first:
                    pe.wait_ge(sem("s_end"), t)
                for g in range(GROUPS):
                    for a, b in PASSES:
                        mm = pe.matmul(ps[:, g, :], cT[a][:, g, :], sth[b][:, 512 * g:512 * g + 512], start=(a == 0 and b == 0), stop=(a == 1))
                mm.then_inc(sem("s_off"), 1)
                pe.wait_ge(sem("s_cbs"), t + 1)
                decays(1, first)
                if not first:
                    pe.wait_ge(sem(f"s_at_in{u}"), 16 * (t - u) + 32)
                    mix(t, u, 0, 0, QUARTER, first)
                for q in (2, 3):
                    pe.wait_ge(sem("s_sub"), 4 * t + q - 1)
                    decays(q, first)
                mix(t, u, 0, QUARTER, KD, first)
                mix(t, u, 1, 0, 6 if last else 5, first)
                pe.wait_ge(sem("s_xwlo"), t + 1)
                pe.wait_ge(sem("s_yo"), t + 1)
                for g in range(GROUPS):
                    for a, b in PASSES:
                        mm = pe.matmul(ps[:, g, :], bt[a][:, P * g:P * g + P], xwh[b][:, 512 * g:512 * g + 512],
                                       start=(a == 0 and b == 0), stop=(a == 1))
                mm.then_inc(sem("s_stp"), 1)
                pe.wait_ge(sem("s_xlo"), t + 1)
                if not first:
                    pe.wait_ge(sem("s_yd"), t)
                diag(t, 0)
                mix(t, u, 1, 6 if last else 5, 7 if last else 6, first)
                diag(t, 1)
                pe.wait_ge(sem("s_st"), t + 2)
                if not first:
                    turned(t - 1, 1 - u)
                mix(t, u, 1, 7 if last else 6, KD if last else 7, first)
                diag(t, 2)
                if not last:
                    mix(t, u, 1, 7, KD, first)
                diag(t, 3)

            chunk(0, 0, True)
            with pe.Fori(0, NT // 2 - 1) as i:
                for u in (1, 0):
                    chunk(2 * i + 2 - u, u, False)
            chunk(LAST, 1, False, True)
            def first_tiles(c, u, kk):
                for a, b in PASSES:
                    mm = pe.matmul(ps[:, 4 + 2 * u + c, :], aT[a][:, u, kk, :], W[b][:, KD * c + kk, :],
                                   start=(kk == 0 and (a, b) == (0, 0)), stop=(kk == KD - 1 and a == 1))
                return mm

            pe.wait_ge(sem("s_mixc"), 2 * NT - 1)
            pe.wait_ge(sem("s_sub"), 4 * NT)
            pe.wait_ge(sem("s_first_in0"), 32)
            for kk in range(KD):
                pe.wait_ge(sem("u_cut"), RING + kk + 1)
                first_tiles(0, 0, kk)
            pe.wait_ge(sem("s_first_in1"), 32)
            for kk in range(KD):
                first_tiles(0, 1, kk)
            turned(LAST, 1)
            pe.wait_ge(sem("s_mixc"), 2 * NT)
            for kk in range(KD):
                pe.wait_ge(sem("u_cut"), RING + KD + kk + 1)
                for u in range(2):
                    mm = first_tiles(1, u, kk)
            mm.then_inc(sem("s_first"), 1)

        @block.scalar
        def _(act):
            def cuts(n0, n1):
                for n in range(n0, n1):
                    cut_hi(act, k, "u", n)

            for g in range(2):
                act.wait_ge(sem(f"a_sent{g}"), 32 * HEADS + 1)
            act.wait_ge(sem("s_run_turned"), 1)
            act.activation(wl[0][:, 0, 0, :], ps[:, 0, 0:P], ACT.Copy).then_inc(sem("s_run_hi"), 1)
            act.wait_ge(sem("p_xw"), 2)
            act.activation(xwh[0][0:META, :], xw[0:META, :], ACT.Copy).then_inc(sem("p_xwhi"), 1)
            act.wait_ge(sem("p_st0"), 1)
            act.activation(sth[0][:, :], state[:, :], ACT.Copy).then_inc(sem("s_sthi"), 1)

            def squares(t, u):
                act.wait_ge(sem("s_gz"), t + 1)
                for g in range(GROUPS):
                    act.wait_ge(sem("s_sq"), 2 * t + g + 1)
                    act.activation(junk, y[:, u, 512 * g:512 * g + 512], ACT.Square, accum_out=ss[:, g:g + 1]).then_inc(sem("s_sq"), 1)

            def root(t):
                act.wait_ge(sem("s_v"), t + 1)
                act.activation(s_[:, 0:2], v[:, 0:2], ACT.Sqrt).then_inc(sem("s_sqrt"), 1)

            def turned(t):
                act.wait_ge(sem("s_sent"), 32 * t + 1)
                for c in range(2):
                    act.wait_ge(sem("s_tr"), 2 * t + c + 1)
                    act.activation(sT[0][:, 4 * c:4 * c + 4, :].rearrange("p a b -> p (a b)"), ps[:, c, :], ACT.Copy).then_inc(sem("s_gh"), 1)

            def chunk(t, u, first, last=False):
                def w_hi(q):
                    act.wait_ge(sem("s_wm"), 4 * t + q + 1)
                    if q >= 2:
                        act.wait_ge(sem("s_dg"), 4 * t + q - 1)
                    act.activation(wl[0][:, q % 2, :, :].rearrange("p a b -> p (a b)"), es[:, q % 2, :], ACT.Copy).then_inc(sem("s_whi"), 1)

                def expo(q):
                    act.wait_ge(sem("s_sub"), 4 * t + q + 1)
                    act.activation(es[:, q % 2, :], es[:, q % 2, :], ACT.Exp).then_inc(sem("s_exp"), 1)

                def mix_out(c):
                    act.wait_ge(sem("s_mix"), 2 * t + c + 1)
                    if not first:
                        act.wait_ge(sem(f"s_mix_sent{c}"), 16 * t)
                    act.activation(mixs[:, 512 * c:512 * c + 512], ps[:, 4 + c, :], ACT.Copy).then_inc(sem("s_mixc"), 1)

                act.wait_ge(sem("s_cb"), t + 1)
                act.activation(cbs[:, :, :].rearrange("p a b -> p (a b)"), ps[:, 6, 0:GROUPS * P], ACT.Copy).then_inc(sem("s_cbs"), 1)
                expo(0)
                act.wait_ge(sem("s_xdt"), t + 1)
                if not first:
                    act.wait_ge(sem("s_dg"), 4 * t)
                act.activation(xh[0][:, :], xdt[:, :], ACT.Copy).then_inc(sem("s_xh"), 1)
                expo(1)
                w_hi(0)
                act.wait_ge(sem("s_xw"), t + 1)
                if not first:
                    act.wait_ge(sem("s_stp"), t)
                act.activation(xwh[0][:, :], xw[:, :], ACT.Copy).then_inc(sem("s_xwh"), 1)
                w_hi(1)
                expo(2)
                if first:
                    cuts(RING - STAGES, RING)
                if not first:
                    squares(t - 1, 1 - u)
                expo(3)
                if not first:
                    root(t - 1)
                mix_out(0)
                if last:
                    act.wait_ge(sem("s_mix"), 2 * NT - 1)
                    cuts(RING, RING + STAGES)
                act.wait_ge(sem("s_st"), t + 2)
                act.activation(sth[0][:, :], state[:, :], ACT.Copy).then_inc(sem("s_sthi"), 1)
                w_hi(2)
                w_hi(3)
                if not first:
                    turned(t - 1)
                mix_out(1)

            chunk(0, 0, True)
            with act.Fori(0, NT // 2 - 1) as i:
                for u in (1, 0):
                    chunk(2 * i + 2 - u, u, False)
            chunk(LAST, 1, False, True)
            cuts(RING + STAGES, RING + KD)
            squares(LAST, 1)
            root(LAST)
            cuts(RING + KD, RING + KD + STAGES)
            turned(LAST)
            cuts(RING + KD + STAGES, 2 * RING)

        @block.vector
        def _(dve):
            def cuts(n0, n1):
                for n in range(n0, n1):
                    cut_lo(dve, k, "u", n)

            def choose(t):
                dve.tensor_copy(pick[:, 0:1], k.heads[:, bass.ds(SH + t, 1)]).then_inc(sem("s_pick"), 1)

            for g in range(2):
                dve.wait_ge(sem(f"a_sent{g}"), 32 * HEADS + 1)
            choose(0)
            dve.wait_ge(sem("s_run_hi"), 1)
            turned_run = (wl[0][:, 0, 0, :], wl[1][:, 0, 0, :])
            dve.tensor_tensor(turned_run[1], ps[:, 0, 0:P], turned_run[0].bitcast(F32), ALU.subtract).then_inc(sem("s_run_lo"), 1)
            dve.wait_ge(sem("s_run_lo"), 1)

            def spread(q):
                for i in range(2):
                    dve.tensor_tensor(run[i][:, 4 * q:4 * q + 4, :], turned_run[i].bitcast(F32).unsqueeze(1).broadcast_to([P, 4, P]),
                                      k.heads[:, 4 * q:4 * q + 4].unsqueeze(2).broadcast_to([P, 4, P]), ALU.mult).then_inc(sem("s_run"), 1)

            spread(0)
            dve.wait_ge(sem("s_start_in"), 16 * 3)
            dve.tensor_tensor(bias[0:META, 0:SH], dt[0:META, NT, :], dend[0:META, NT, :], ALU.mult).then_inc(sem("p_xw"), 1)
            dve.wait_ge(sem("p_xw"), 1)
            dve.tensor_tensor(heads(xw[0:META, :]), heads(xm[:, :]), by_head(bias[0:META, 0:SH], META), ALU.mult).then_inc(sem("p_xw"), 1)
            dve.wait_ge(sem("p_xwhi"), 1)
            dve.tensor_tensor(xwh[1][0:META, :], xw[0:META, :], xwh[0][0:META, :].bitcast(F32), ALU.subtract).then_inc(sem("p_xwlo"), 1)
            for q in range(1, SH // 4):
                spread(q)
            dve.wait_ge(sem("p_state"), 1)
            dve.tensor_copy(state[:, :], ps[:, 2:4, :].rearrange("p a b -> p (a b)")).then_inc(sem("p_st0"), 1)
            dve.memset(r[:, 11:12], 0.0).then_inc(sem("s_sent"), 1)
            dve.memset(r[:, 12:13], 0.0).then_inc(sem("s_end"), 1)
            dve.memset(r[:, 13:14], 0.0).then_inc(sem("s_sq"), 1)
            dve.memset(r[:, 14:15], 0.0).then_inc(sem("s_st"), 1)
            dve.wait_ge(sem("s_sthi"), 1)
            dve.tensor_tensor(sth[1][:, :], state[:, :], sth[0][:, :].bitcast(F32), ALU.subtract).then_inc(sem("s_stlo"), 1)

            def norm(t, u):
                dve.wait_ge(sem("s_sq"), 2 * t + 3)
                rsqrt_before(dve, k, v[:, 0:2], ss[:, 0:2], 1.0 / (SSMW // GROUPS), "s_v", 1)
                rsqrt_after(dve, k, r[:, 0:2], v[:, 0:2], s_[:, 0:2], t1[:, 0:2], "s_sqrt", t + 1, "s_rs", 5 * t)
                dve.wait_ge(sem("s_w_in"), 16)
                for g in range(GROUPS):
                    part = slice(512 * g, 512 * g + 512)
                    dve.scalar_tensor_tensor(y[:, u, part], y[:, u, part], r[:, g:g + 1], wrow[:, part], ALU.mult, ALU.mult).then_inc(sem("s_g"), 1)

            def turned(t):
                for c in range(2):
                    dve.wait_ge(sem("s_gh"), 2 * t + c + 1)
                    hi, lo = (x[:, 4 * c:4 * c + 4, :].rearrange("p a b -> p (a b)") for x in sT)
                    mm = dve.tensor_tensor(lo, ps[:, c, :], hi.bitcast(F32), ALU.subtract)
                mm.then_inc(sem("s_end"), 1)

            def chunk(t, u, first, last=False):
                def sub(q):
                    if q >= 2 or not first:
                        dve.wait_ge(sem("s_wlo"), 4 * t + q - 1)
                    dve.wait_ge(sem("s_eb"), 4 * t + q + 1)
                    dve.tensor_tensor(es[:, q % 2, :].rearrange("p (a b) -> p a b", b=P), ps[:, 7 - q % 2, :].rearrange("p (a b) -> p a b", b=P),
                                      acum[:, t, 4 * q:4 * q + 4].unsqueeze(2).broadcast_to([P, 4, P]), ALU.subtract).then_inc(sem("s_sub"), 1)

                def mul(q):
                    dve.wait_ge(sem("s_exp"), 4 * t + q + 1)
                    if q == 0:
                        dve.wait_ge(sem("s_cbs"), t + 1)
                    e = es[:, q % 2, :].rearrange("p (a b) -> p a b", b=P)
                    dve.tensor_tensor(e, e, cbs[:, q // 2, :].unsqueeze(1).broadcast_to([P, 4, P]), ALU.mult).then_inc(sem("s_wm"), 1)

                def low(q):
                    dve.wait_ge(sem("s_whi"), 4 * t + q + 1)
                    hi, lo = (x[:, q % 2, :, :].rearrange("p a b -> p (a b)") for x in wl)
                    dve.tensor_tensor(lo, es[:, q % 2, :], hi.bitcast(F32), ALU.subtract).then_inc(sem("s_wlo"), 1)

                dve.wait_ge(sem("s_x_in"), 16 * t + 16)
                if not first:
                    dve.wait_ge(sem("s_xlo"), t)
                dve.tensor_tensor(heads(xdt[:, :]), heads(xs[:, :]), by_head(dt[:, t, :]), ALU.mult).then_inc(sem("s_xdt"), 1)
                sub(0)
                sub(1)
                mul(0)
                dve.wait_ge(sem("s_off"), t + 1)
                dve.tensor_tensor(heads(y[:, u, :]), ps[:, 0:2, :].rearrange("p a (h c) -> p (a h) c", c=SHD), by_head(ecum[:, t, :]), ALU.mult).then_inc(sem("s_yo"), 1)
                mul(1)
                low(0)
                low(1)
                sub(2)
                sub(3)
                if not last:
                    choose(t + 1)
                if first:
                    cuts(RING - STAGES, RING)
                dve.tensor_tensor(heads(state[:, :]), heads(state[:, :]), by_head(cdec[:, t, :]), ALU.mult).then_inc(sem("s_dec"), 1)
                mul(2)
                if not first:
                    norm(t - 1, 1 - u)
                dve.wait_ge(sem("s_stp"), t + 1)
                dve.wait_ge(sem("s_dec"), t + 1)
                dve.tensor_tensor(state[:, :], ps[:, 0:2, :].rearrange("p a b -> p (a b)"), state[:, :], ALU.add).then_inc(sem("s_st"), 1)
                mul(3)
                dve.wait_ge(sem("s_sthi"), t + 2)
                dve.tensor_tensor(sth[1][:, :], state[:, :], sth[0][:, :].bitcast(F32), ALU.subtract).then_inc(sem("s_stlo"), 1)
                low(2)
                low(3)
                if not first:
                    turned(t - 1)
                dve.wait_ge(sem("s_xd"), t + 1)
                dve.wait_ge(sem("s_dg"), 4 * t + 4)
                dve.tensor_tensor(xd[:, :], ps[:, 2:4, :].rearrange("p a b -> p (a b)"), xd[:, :], ALU.add).then_inc(sem("s_yd"), 1)

            chunk(0, 0, True)
            with dve.Fori(0, NT // 2 - 1) as i:
                for u in (1, 0):
                    chunk(2 * i + 2 - u, u, False)
            chunk(LAST, 1, False, True)
            norm(LAST, 1)
            turned(LAST)



def phase_out(k):
    nc, sem, m, ps, io = k.nc, k.sem, k.map, k.ps, k.io
    o = O_R
    hmT = []
    for s in ("hi", "lo"):
        t, o = m.at("hmT" + s, [P, KD, SEQ], F32R, o)
        hmT.append(t)
    GRP = 512
    GRPS = DFF // GRP
    FT = GRP // P
    HALF = RING // 2
    f1, om = [], o
    for s in ("hi", "lo"):
        t, o = m.at("f1" + s, [P, FT, SEQ], F32R, o)
        f1.append(t)
    o_acc = o
    acc, o = m.at("acc", [P, NT, D], F32, o)
    sT = []
    for s in ("hi", "lo"):
        t, om = m.at("m_sT" + s, [P, 2, KD, P], F32R, om)
        sT.append(t)
    mix, om = m.at("m_mix", [P, 2, D], F32, om)
    junk, om = m.at("m_junk", [P, D], F32, om)
    wrow, om = m.at("m_wrow", [P, D], F32, om)
    assert om <= o_acc
    h, om = m.at("m_h", [P, 2, D], F32, o_acc)
    hn, om = m.at("m_hn", [P, 2, D], F32, om)
    relu, _ = m.at("relu", [P, 2, 512], F32, k.o_relu)
    e_h, oh = m.at("e_h", [P, NT, D], F32, O_R)
    e_wrow, oh = m.at("e_wrow", [P, D], F32, oh)
    e_junk, oh = m.at("e_junk", [P, D], F32, oh)
    ss, v, s_, r, t1, bias = k.st
    W = (k.whi, k.wlo)
    PASSES = ((0, 0), (0, 1), (1, 0))
    PAIRS = NT // 2
    DN = 2 * NT
    UP = 2 * FT
    rows = lambda a, t: a.rearrange("(t p) n -> t p n", p=P)[t]
    cols = lambda a, t: a.rearrange("(k p) (t n) -> t p k n", p=P, n=P)[t]
    up = io["w_mlp_up"][0].rearrange("(k p) (g n) -> g k p n", p=P, n=GRP)
    down = io["w_mlp_down"][0].rearrange("(g j p) (c n) -> g j c p n", p=P, j=FT, n=512)

    def block_of(g, n):
        return up[g, n] if n < HALF else down[g, (n - HALF) // 2, (n - HALF) % 2]

    def place(n):
        return n % FT, slice(512 * (n // FT), 512 * (n // FT) + 512)

    def bank_of(n, first):
        return n if first and n < FT else n % 2

    with nc.Block() as block:
        @block.sync
        def _(sp):
            def load_left(t, u):
                for i in range(2):
                    sp.dma_start(sT[i][:, u, :, :].bitcast(F32), cols(k.d_ssm[i], t)).then_inc(sem(f"m_s_in{u}"), 16)

            def load_mix(t, u):
                sp.dma_start(mix[:, u, :], rows(k.d_mix, t)).then_inc(sem(f"m_mix_in{u}"), 16)

            def load_h(t, u):
                sp.dma_start(h[:, u, :], rows(io["x"][0], t)).then_inc(sem(f"m_h_in{u}"), 16)

            def store(t, u):
                sp.wait_ge(sem("m_h"), t + 1)
                sp.dma_start(rows(k.d_h, t), h[:, u, :]).then_inc(sem(f"m_sent{u}"), 16)

            load_left(2, 0)
            load_mix(0, 0)
            load_left(3, 1)
            load_mix(1, 1)
            for u in range(2):
                load_h(u, u)
            sp.dma_start(wrow[:, :], io["norm_mix_post"][0].partition_broadcast(P)).then_inc(sem("m_w_in"), 16)
            for n in range(STAGES):
                load_block(sp, k, "v", n, block_of(0, n))
            def turn(i, more):
                for u in range(2):
                    store(2 * i + u, u)
                    load_mix(2 * i + u + 2, u)
                for u in range(2):
                    if more:
                        sp.wait_ge(sem("m_mm"), 4 * i + 2 * u + 2)
                        load_left(2 * i + u + 4, u)
                    sp.wait_ge(sem("m_hn"), 2 * i + u + 1)
                    sp.wait_ge(sem(f"m_sent{u}"), 16 * i + 16)
                    load_h(2 * i + u + 2, u)

            with sp.Fori(0, PAIRS - 2) as i:
                turn(i, True)
            turn(PAIRS - 2, False)
            for n in range(STAGES, HALF):
                load_block(sp, k, "v", n, block_of(0, n))
            for u in range(2):
                store(NT - 2 + u, u)
            for n in range(HALF, RING):
                load_block(sp, k, "v", n, block_of(0, n))
            with sp.Fori(1, GRPS) as g:
                for n in range(RING):
                    sp.wait_ge(sem("v_cut"), RING * g + n - STAGES + 1)
                    sp.dma_start(k.stage[:, n % STAGES, :], block_of(g, n)).then_inc(sem(f"v_landed{n % STAGES}"), 16)
            sp.wait_ge(sem("v_up"), UP * GRPS)
            for u in range(2):
                sp.wait_ge(sem(f"m_sent{u}"), 16 * PAIRS)
            sp.dma_start(e_wrow[:, :], io["norm_mlp_post"][0].partition_broadcast(P)).then_inc(sem("e_w_in"), 16)
            for t in range(NT):
                sp.dma_start(e_h[:, t, :], rows(k.d_h, t)).then_inc(sem("e_h_in"), 16)
            for t in range(NT):
                sp.wait_ge(sem("e_out"), t + 1)
                sp.dma_start(io["out"][0, P * t:P * t + P, :], e_h[:, t, :]).then_inc(sem("e_sent"), 16)
            sp.wait_ge(sem("e_sent"), 16 * NT)

        @block.gpsimd
        def _(pool):
            def residual(i):
                for u in range(2):
                    pool.wait_ge(sem("m_scaled"), 2 * i + u + 1)
                    pool.wait_ge(sem(f"m_h_in{u}"), 16 * i + 16)
                    pool.tensor_tensor(h[:, u, :], mix[:, u, :], h[:, u, :], ALU.add).then_inc(sem("m_h"), 1)

            with pool.Fori(0, PAIRS - 1) as i:
                residual(i)
            for n in range(HALF):
                cut_lo(pool, k, "v", n)
            residual(PAIRS - 1)
            pool.wait_ge(sem("m_mm"), 2 * NT - 4)
            for n in range(HALF, RING):
                cut_block(pool, k, "v", n, 512)
            with pool.Fori(1, GRPS) as g:
                for n in range(RING):
                    if n == 0:
                        pool.wait_ge(sem("v_up"), UP * g)
                    if n == HALF:
                        pool.wait_ge(sem("v_down"), DN * g)
                    cut_block(pool, k, "v", n, 512, RING * g, 16 * (RING // STAGES) * g)
            pool.wait_ge(sem("e_h_in"), 16 * NT)
            for t in range(NT):
                pool.wait_ge(sem("e_scaled"), t + 1)
                pool.tensor_tensor(e_h[:, t, :], acc[:, t, :], e_h[:, t, :], ALU.add).then_inc(sem("e_out"), 1)

        @block.tensor
        def _(pe):
            def mm_tile(t, u, first):
                pe.wait_ge(sem(f"m_s_in{u}"), 16 * (t - u))
                for c in range(2):
                    if not first:
                        pe.wait_ge(sem("m_add"), 2 * t + c - 3)
                    for kk in range(KD):
                        for a, b in PASSES:
                            mm = pe.matmul(ps[:, 2 * u + c, :], sT[a][:, u, kk, :], W[b][:, KD * c + kk, :],
                                           start=(kk == 0 and a == 0 and b == 0), stop=(kk == KD - 1 and a == 1))
                    mm.then_inc(sem("m_mm"), 1)

            def turn_pair(i):
                for u in range(2):
                    pe.wait_ge(sem("m_hn"), 2 * i + u + 1)
                    for c in range(2):
                        pe.wait_ge(sem("m_lo"), 4 * i + 2 * u + c + 1)
                        for j in range(4):
                            kk = 4 * c + j
                            mm = pe.transpose(ps[:, 4 + 2 * u + c, P * j:P * j + P], hn[:, u, P * kk:P * kk + P], k.ident[:, :])
                        mm.then_inc(sem("m_turned"), 1)

            def up_bank(g, n, first):
                j, at = place(n)
                if first and n < FT:
                    pe.wait_ge(sem("m_add"), 2 * NT)
                else:
                    pe.wait_ge(sem("v_sq_out"), UP * g + n + 1)
                for kk in range(KD):
                    if n == 0:
                        pe.wait_ge(sem("v_cut"), RING * g + kk + 1)
                    for a, b in PASSES:
                        mm = pe.matmul(ps[:, bank_of(n, first), :], W[a][:, kk, P * j:P * j + P], hmT[b][:, kk, at],
                                       start=(kk == 0 and a == 0 and b == 0), stop=(kk == KD - 1 and a == 1))
                mm.then_inc(sem("v_up"), 1)

            def down_group(g):
                pe.wait_ge(sem("v_cut"), RING * g + RING)
                for n in range(DN):
                    t, c = n // 2, n % 2
                    if n in (0, DN // 2):
                        pe.wait_ge(sem("v_sq_out"), UP * g + 2 + (FT if n == 0 else UP))
                    pe.wait_ge(sem("v_added"), DN * g + n + 1)
                    for j in range(FT):
                        for a, b in PASSES:
                            mm = pe.matmul(ps[:, 2 + n % 4, :], f1[a][:, j, P * t:P * t + P], W[b][:, HALF + 2 * j + c, :],
                                           start=(j == 0 and a == 0 and b == 0), stop=(j == FT - 1 and a == 1))
                    mm.then_inc(sem("v_down"), 1)

            for u in range(2):
                mm_tile(u + 2, u, True)
            turn_pair(0)
            with pe.Fori(1, PAIRS - 1) as i:
                for u in range(2):
                    mm_tile(2 * i + u + 2, u, False)
                turn_pair(i)
            pe.wait_ge(sem("m_lo"), 4 + 2 * PAIRS)
            for n in range(FT - 1):
                up_bank(0, n, True)
            turn_pair(PAIRS - 1)
            up_bank(0, FT - 1, True)
            for n in range(FT, UP):
                if n == FT:
                    pe.wait_ge(sem("m_lo"), 4 + 4 * PAIRS)
                up_bank(0, n, True)
            down_group(0)
            with pe.Fori(1, GRPS) as g:
                for n in range(UP):
                    up_bank(g, n, False)
                down_group(g)

        @block.scalar
        def _(act):
            def norms(i, cuts=lambda n0, n1: None):
                for u in range(2):
                    act.wait_ge(sem("m_add"), 4 * i + 2 * u + 2)
                    act.wait_ge(sem("m_sq"), 4 * i + u + 1)
                    act.activation(junk[:, :], mix[:, u, :], ACT.Square, accum_out=ss[:, u:u + 1]).then_inc(sem("m_sq"), 1)
                cuts(STAGES, STAGES + 1)
                act.wait_ge(sem("m_v"), 2 * i + 1)
                act.activation(s_[:, 0:2], v[:, 0:2], ACT.Sqrt).then_inc(sem("m_sqrt"), 1)
                cuts(STAGES + 1, HALF)
                for u in range(2):
                    act.wait_ge(sem("m_h"), 2 * i + u + 1)
                    act.wait_ge(sem("m_sq"), 4 * i + u + 3)
                    act.activation(junk[:, :], h[:, u, :], ACT.Square, accum_out=ss[:, 2 + u:3 + u]).then_inc(sem("m_sq"), 1)
                act.wait_ge(sem("m_v"), 2 * i + 2)
                act.activation(s_[:, 2:4], v[:, 2:4], ACT.Sqrt).then_inc(sem("m_sqrt"), 1)
                act.wait_ge(sem("m_r"), i + 1)
                for u in range(2):
                    act.wait_ge(sem("m_turned"), 4 * i + 2 * u + 2)
                    act.activation(hn[:, u, :], h[:, u, :], ACT.Copy, scale=r[:, 2 + u:3 + u]).then_inc(sem("m_hn"), 1)

            def high_pair(i):
                for n in range(4):
                    act.wait_ge(sem("m_turned"), 4 * i + n + 5)
                    for j in range(4):
                        kk = 4 * (n % 2) + j
                        act.activation(hmT[0][:, kk, bass.ds(P * (2 * i + n // 2), P)], ps[:, 4 + n, P * j:P * j + P], ACT.Copy,
                                       scale=col(k, "mlp", kk)).then_inc(sem("m_hi"), 1)

            def high(g, n, first=False):
                j, at = place(n)
                act.wait_ge(sem("v_up"), UP * g + n + 1)
                bank = ps[:, bank_of(n, first), :]
                act.activation(relu[:, n % 2, :], bank, ACT.Relu).then_inc(sem("v_relu"), 1)
                act.wait_ge(sem("v_sq"), UP * g + n + 1)
                act.activation(f1[0][:, j, at], bank, ACT.Copy).then_inc(sem("v_f1hi"), 1)

            def cuts(n0, n1):
                for n in range(n0, n1):
                    cut_hi(act, k, "v", n)

            with act.Fori(0, PAIRS - 2) as i:
                norms(i)
                high_pair(i)
            norms(PAIRS - 2)
            act.wait_ge(sem("m_mm"), 2 * NT - 5)
            cuts(0, STAGES)
            high_pair(PAIRS - 2)
            norms(PAIRS - 1, cuts)
            for n in range(2):
                high(0, n, True)
            high_pair(PAIRS - 1)
            for n in range(2, FT):
                high(0, n, True)
            for n in range(FT, UP):
                high(0, n)
            with act.Fori(1, GRPS) as g:
                for n in range(UP):
                    high(g, n)
            for t in range(NT):
                act.wait_ge(sem("v_added"), 4 + DN * (GRPS - 1) + 2 * t + 2)
                if t:
                    act.wait_ge(sem("e_sq"), t)
                act.activation(e_junk[:, :], acc[:, t, :], ACT.Square, accum_out=ss[:, t:t + 1]).then_inc(sem("e_sq"), 1)
                act.wait_ge(sem("e_v"), t + 1)
                act.activation(s_[:, t:t + 1], v[:, t:t + 1], ACT.Sqrt).then_inc(sem("e_sqrt"), 1)

        @block.vector
        def _(dve):
            dve.memset(bias[:, 0:1], 0.0).then_inc(sem("m_sq"), 1)
            dve.memset(bias[:, 1:2], 0.0).then_inc(sem("m_lo"), 4)
            dve.memset(bias[:, 2:3], 0.0).then_inc(sem("m_turned"), 4)

            def add_pair(t, by_pairs, first=False):
                for u in range(2):
                    dve.wait_ge(sem(f"m_mix_in{u}"), by_pairs + 16)
                    for c in range(2):
                        if not first:
                            dve.wait_ge(sem("m_mm"), 2 * t + 2 * u + c - 3)
                        part = mix[:, u, 512 * c:512 * c + 512]
                        dve.tensor_tensor(part, ps[:, 2 * u + c + 4 * first, :], part, ALU.add).then_inc(sem("m_add"), 1)

            def norms(i):
                dve.wait_ge(sem("m_sq"), 4 * i + 3)
                rsqrt_before(dve, k, v[:, 0:2], ss[:, 0:2], 1.0 / D, "m_v", 1)
                rsqrt_after(dve, k, r[:, 0:2], v[:, 0:2], s_[:, 0:2], t1[:, 0:2], "m_sqrt", 2 * i + 1, "m_rs", 10 * i)
                for u in range(2):
                    dve.scalar_tensor_tensor(mix[:, u, :], mix[:, u, :], r[:, u:u + 1], wrow[:, :], ALU.mult, ALU.mult).then_inc(sem("m_scaled"), 1)
                dve.wait_ge(sem("m_sq"), 4 * i + 5)
                rsqrt_before(dve, k, v[:, 2:4], ss[:, 2:4], 1.0 / D, "m_v", 1)
                rsqrt_after(dve, k, r[:, 2:4], v[:, 2:4], s_[:, 2:4], t1[:, 2:4], "m_sqrt", 2 * i + 2, "m_rs", 10 * i + 5)
                dve.tensor_copy(t1[:, 4:6], r[:, 2:4]).then_inc(sem("m_r"), 1)

            def low_pair(i):
                for n in range(4):
                    dve.wait_ge(sem("m_hi"), 16 * i + 4 * n + 4)
                    at = bass.ds(P * (2 * i + n // 2), P)
                    for j in range(4):
                        kk = 4 * (n % 2) + j
                        mm = dve.scalar_tensor_tensor(hmT[1][:, kk, at], ps[:, 4 + n, P * j:P * j + P], col(k, "mlp", kk), hmT[0][:, kk, at].bitcast(F32),
                                                      ALU.mult, ALU.subtract)
                    mm.then_inc(sem("m_lo"), 1)

            def square(g, n, first=False):
                j, at = place(n)
                bank = ps[:, bank_of(n, first), :]
                dve.wait_ge(sem("v_relu"), UP * g + n + 1)
                dve.tensor_tensor(bank, bank, relu[:, n % 2, :], ALU.mult).then_inc(sem("v_sq"), 1)
                dve.wait_ge(sem("v_f1hi"), UP * g + n + 1)
                dve.tensor_tensor(f1[1][:, j, at], bank, f1[0][:, j, at].bitcast(F32), ALU.subtract).then_inc(sem("v_sq_out"), 1)

            def add(g, n):
                dve.wait_ge(sem("v_down"), DN * g + n + 1)
                t, c = n // 2, n % 2
                part = acc[:, t, 512 * c:512 * c + 512]
                dve.tensor_tensor(part, ps[:, 2 + n % 4, :], part, ALU.add).then_inc(sem("v_added"), 1)

            add_pair(0, 0, True)
            dve.wait_ge(sem("m_w_in"), 16)
            with dve.Fori(0, PAIRS - 1) as i:
                norms(i)
                add_pair(2 * i + 2, 16 * i + 16)
                low_pair(i)
            dve.memset(bias[:, 3:4], 0.0).then_inc(sem("v_sq_out"), 2)
            norms(PAIRS - 1)
            for n in range(2):
                square(0, n, True)
            low_pair(PAIRS - 1)
            for n in range(2, FT):
                square(0, n, True)
            dve.memset(bias[:, 4:5], 0.0).then_inc(sem("v_added"), 4)
            for u in range(2):
                dve.wait_ge(sem(f"m_sent{u}"), 16 * PAIRS)
            for n in range(FT, UP):
                square(0, n)
                for t in range(2 * (n - FT), 2 * (n - FT) + 2):
                    dve.memset(acc[:, t, :], 0.0).then_inc(sem("acc_set"), 1)
            dve.wait_ge(sem("acc_set"), NT)
            for n in range(DN):
                add(0, n)
            with dve.Fori(1, GRPS - 1) as g:
                for n in range(UP):
                    square(g, n)
                for n in range(DN):
                    add(g, n)
            g = GRPS - 1
            for n in range(UP):
                square(g, n)
            dve.wait_ge(sem("e_w_in"), 16)
            for t in range(NT):
                add(g, 2 * t)
                add(g, 2 * t + 1)
                dve.wait_ge(sem("e_sq"), t + 1)
                rsqrt_before(dve, k, v[:, t:t + 1], ss[:, t:t + 1], 1.0 / D, "e_v", 1)
                rsqrt_after(dve, k, r[:, t:t + 1], v[:, t:t + 1], s_[:, t:t + 1], t1[:, t:t + 1], "e_sqrt", t + 1, "e_rs", 5 * t)
                dve.scalar_tensor_tensor(acc[:, t, :], acc[:, t, :], r[:, t:t + 1], e_wrow[:, :], ALU.mult, ALU.mult).then_inc(sem("e_scaled"), 1)


def build(nc, io):
    k = setup(nc, io)
    phase_norm(k)
    phase_project(k)
    k.sem.renew(("a_q_in", "a_kv_in", "a_cut", "qr_sent0", "qr_sent1"))
    phase_attend(k)
    phase_ssd(k)
    phase_out(k)


_INS = ["x", "meta_tokens", "w_in", "w_q_up", "w_kv_up", "dt_bias", "a_log", "d_skip", "ssm_norm", "w_out",
        "norm_mix_post", "w_mlp_up", "w_mlp_down", "norm_mlp_post"]


def _constants():
    inv = np.float32(10000.0) ** (-np.arange(0, ROPE, 2, dtype=np.float32) / np.float32(ROPE))
    ang = np.arange(POS, dtype=np.float32)[:, None] * inv.astype(np.float32)[None, :]
    table = np.concatenate([np.cos(ang), np.sin(ang)], axis=1).astype(np.float32)
    rope = np.zeros((P, NT + 1, ROPE), np.float32)
    rope[:, :NT] = table[META:].reshape(NT, P, ROPE).transpose(1, 0, 2)
    rope[:META, NT] = table[:META]
    i = np.arange(P)
    ahead = i[:, None] <= i[None, :]
    return {
        "c_ident": np.eye(P, dtype=np.float32),
        "c_tri": ahead.astype(np.float32),
        "c_mask": np.where(ahead, 0.0, NEG).astype(np.float32),
        "c_rope": rope,
        "c_heads": np.concatenate([i[:, None] % SH == np.arange(SH), i[:, None] // SH == np.arange(NT)], axis=1).astype(np.float32),
    }


def _arrays(inputs):
    arrays = {n: np.ascontiguousarray(inputs[n]) for n in _INS}
    columns = lambda a: np.asarray(a).reshape(-1, P).T
    arrays["c_par"] = np.ascontiguousarray(np.concatenate([
        columns(inputs["norm_mix_pre"]), columns(inputs["norm_mlp_pre"]), columns(inputs["q_a_norm"]), columns(inputs["kv_a_norm"]),
        np.asarray(inputs["conv_w"])[0].reshape(4, CONVW // P, P).transpose(2, 1, 0).reshape(P, -1), columns(inputs["conv_b"])], axis=1))
    return {**arrays, **_constants()}


def _declare(nc, arrays):
    io = {n: nc.dram_tensor(n, a.shape, mybir.dt.from_np(a.dtype), kind="ExternalInput").ap() for n, a in arrays.items()}
    io["out"] = nc.dram_tensor("out", (1, SEQ, D), F32, kind="ExternalOutput").ap()
    return io


def kernel(**inputs):
    import concourse.bacc as bacc
    from concourse.bass_utils import run_bass_kernel_spmd

    arrays = _arrays(inputs)
    nc = bacc.Bacc("TRN2", target_bir_lowering=False, num_devices=1)
    build(nc, _declare(nc, arrays))
    r = run_bass_kernel_spmd(nc, [arrays], core_ids=[0])
    return r.results[0]["out"]
```
